# Optimizing a Trainium2 kernel written in Bass

```python
import jax, jax.numpy as jnp
from jax import lax
import numpy as np

D_MODEL = 2048
BATCH = 1
SEQ = 256
DEPTH = 1

MIX_WIDTH = D_MODEL
SB_HEADS = 8
SB_HEAD_DIM = 128
SB_WIDTH = SB_HEADS * SB_HEAD_DIM
SB_BLOCK = 128
SSD_HEADS = 16
SSD_HEAD_DIM = 64
SSD_WIDTH = SSD_HEADS * SSD_HEAD_DIM
SSD_GROUPS = 2
SSD_STATE = 128
SSD_CONV = 4
SSD_CHUNK = 128
SSD_CONV_DIM = SSD_WIDTH + 2 * SSD_GROUPS * SSD_STATE
IN_PROJ_DIM = 3 * SB_WIDTH + SSD_WIDTH + SSD_CONV_DIM + SSD_HEADS
PEER_HEADS = 8
PEER_N_KEYS = 128
PEER_N_EXPERTS = PEER_N_KEYS * PEER_N_KEYS
PEER_KEY_DIM = 256
PEER_HALF = PEER_KEY_DIM // 2
PEER_TOPK = 16
PEER_TOKEN_BLOCK = 128
RMS_EPS = 1e-6


def rms_norm(x, gain):
    xf = x.astype(jnp.float32)
    inv = lax.rsqrt(jnp.mean(xf * xf, axis=-1, keepdims=True) + RMS_EPS)
    return (xf * inv).astype(x.dtype) * gain

def stick_breaking_attention(q, k, v):
    b, s, h, dh = q.shape
    nb = s // SB_BLOCK
    scale = dh ** -0.5
    kf = k.astype(jnp.float32)
    vf = v.astype(jnp.float32)
    key_pos = jnp.arange(s)
    q_blocks = q.reshape(b, nb, SB_BLOCK, h, dh).transpose(1, 0, 2, 3, 4)

    def block(args):
        qb, bi = args
        q_pos = bi * SB_BLOCK + jnp.arange(SB_BLOCK)
        logits = jnp.einsum('bqhd,bkhd->bhqk', qb.astype(jnp.float32), kf) * scale
        causal = key_pos[None, :] < q_pos[:, None]
        log_beta = jax.nn.log_sigmoid(logits)
        log_keep = jnp.where(causal, jax.nn.log_sigmoid(-logits), 0.0)
        later = lax.cumsum(log_keep, axis=3, reverse=True) - log_keep
        weights = jnp.where(causal, jnp.exp(jnp.where(causal, log_beta + later, 0.0)), 0.0)
        return jnp.einsum('bhqk,bkhd->bqhd', weights, vf)

    out = lax.map(block, (q_blocks, jnp.arange(nb)))
    return out.transpose(1, 0, 2, 3, 4).reshape(b, s, h, dh).astype(q.dtype)

def ssd_scan(x, dt, a, bmat, cmat):
    f32 = jnp.float32
    b, s, h, p = x.shape
    g, n = bmat.shape[-2], bmat.shape[-1]
    hg = h // g
    nc, l = s // SSD_CHUNK, SSD_CHUNK
    xf = (x.astype(f32) * dt[..., None]).reshape(b, nc, l, g, hg, p)
    a_dt = (dt * a).reshape(b, nc, l, g, hg).transpose(0, 3, 4, 1, 2)
    bf = bmat.astype(f32).reshape(b, nc, l, g, n)
    cf = cmat.astype(f32).reshape(b, nc, l, g, n)
    a_cs = jnp.cumsum(a_dt, axis=-1)
    seg = a_cs[..., :, None] - a_cs[..., None, :]
    tri = jnp.tril(jnp.ones((l, l), dtype=bool))
    decay = jnp.where(tri, jnp.exp(jnp.where(tri, seg, 0.0)), 0.0).transpose(0, 3, 1, 2, 4, 5)
    cb = jnp.einsum('bclgn,bcsgn->bcgls', cf, bf)
    scores = cb[:, :, :, None] * decay
    y_diag = jnp.einsum('bcghls,bcsghp->bclghp', scores, xf)
    decay_states = jnp.exp(a_cs[..., -1:] - a_cs).transpose(0, 3, 4, 1, 2)
    states = jnp.einsum('bclgn,bclghp->bcghpn', bf, xf * decay_states[..., None])
    chunk_decay = jnp.exp(a_cs[..., -1]).transpose(3, 0, 1, 2)

    def step(carry, inp):
        st, dec = inp
        return carry * dec[..., None, None] + st, carry

    init = jnp.zeros((b, g, hg, p, n), f32)
    _, prev = lax.scan(step, init, (states.transpose(1, 0, 2, 3, 4, 5), chunk_decay))
    prev = prev.transpose(1, 0, 2, 3, 4, 5)
    state_decay_out = jnp.exp(a_cs).transpose(0, 3, 4, 1, 2)
    y_off = jnp.einsum('bclgn,bcghpn->bclghp', cf, prev) * state_decay_out[..., None]
    return (y_diag + y_off).reshape(b, s, h, p)

def hybrid_mixer(xn, w_in, sb_q_norm, sb_k_norm, conv_w, conv_b, dt_bias, a_log, d_skip,
                 sb_out_norm, ssd_out_norm, w_out):
    b, s, _ = xn.shape
    proj = xn @ w_in
    o1 = SB_WIDTH
    o2 = 2 * SB_WIDTH
    o3 = 3 * SB_WIDTH
    o4 = o3 + SSD_WIDTH
    o5 = o4 + SSD_CONV_DIM
    q, k, v, z, xbc, dt_raw = jnp.split(proj, [o1, o2, o3, o4, o5], axis=-1)
    q = rms_norm(q.reshape(b, s, SB_HEADS, SB_HEAD_DIM), sb_q_norm)
    k = rms_norm(k.reshape(b, s, SB_HEADS, SB_HEAD_DIM), sb_k_norm)
    v = v.reshape(b, s, SB_HEADS, SB_HEAD_DIM)
    attn = stick_breaking_attention(q, k, v).reshape(b, s, SB_WIDTH)
    attn = rms_norm(attn, sb_out_norm)
    xbc = lax.conv_general_dilated(xbc, conv_w, window_strides=(1,), padding=[(SSD_CONV - 1, 0)],
                                   dimension_numbers=('NWC', 'WIO', 'NWC'),
                                   feature_group_count=SSD_CONV_DIM) + conv_b
    xbc = jax.nn.silu(xbc)
    xs, bm, cm = jnp.split(xbc, [SSD_WIDTH, SSD_WIDTH + SSD_GROUPS * SSD_STATE], axis=-1)
    xs = xs.reshape(b, s, SSD_HEADS, SSD_HEAD_DIM)
    bm = bm.reshape(b, s, SSD_GROUPS, SSD_STATE)
    cm = cm.reshape(b, s, SSD_GROUPS, SSD_STATE)
    dt = jax.nn.softplus(dt_raw.astype(jnp.float32) + dt_bias.astype(jnp.float32))
    a = -jnp.exp(a_log.astype(jnp.float32))
    y = ssd_scan(xs, dt, a, bm, cm) + d_skip[:, None] * xs
    y = y.reshape(b, s, SSD_WIDTH).astype(xn.dtype) * jax.nn.silu(z)
    y = rms_norm(y.reshape(b, s, SSD_GROUPS, SSD_WIDTH // SSD_GROUPS),
                 ssd_out_norm.reshape(SSD_GROUPS, SSD_WIDTH // SSD_GROUPS)).reshape(b, s, SSD_WIDTH)
    return jnp.concatenate([attn, y], axis=-1) @ w_out

def peer_ffn(hn, w_query, sub_keys, expert_down, expert_up):
    b, s, d = hn.shape
    t = b * s
    xt = hn.reshape(t, d)
    q = (xt @ w_query).reshape(t, PEER_HEADS, 2, PEER_HALF)
    scores = jnp.einsum('thcd,hckd->thck', q.astype(jnp.float32), sub_keys.astype(jnp.float32))
    top_s, top_i = lax.top_k(scores, PEER_TOPK)
    cand_s = (top_s[:, :, 0, :, None] + top_s[:, :, 1, None, :]).reshape(t, PEER_HEADS, PEER_TOPK * PEER_TOPK)
    cand_i = (top_i[:, :, 0, :, None] * PEER_N_KEYS + top_i[:, :, 1, None, :]).reshape(t, PEER_HEADS, PEER_TOPK * PEER_TOPK)
    best_s, best_pos = lax.top_k(cand_s, PEER_TOPK)
    expert_idx = jnp.take_along_axis(cand_i, best_pos, axis=-1)
    gates = jax.nn.softmax(best_s, axis=-1)
    nblk = t // PEER_TOKEN_BLOCK

    def block(args):
        xb, idx, gb = args
        u = expert_down[idx]
        act = jax.nn.gelu(jnp.einsum('thkd,td->thk', u, xb), approximate=False)
        vv = expert_up[idx]
        return jnp.einsum('thk,thkd->td', (gb * act).astype(vv.dtype), vv)

    out = lax.map(block, (xt.reshape(nblk, PEER_TOKEN_BLOCK, d),
                          expert_idx.reshape(nblk, PEER_TOKEN_BLOCK, PEER_HEADS, PEER_TOPK),
                          gates.reshape(nblk, PEER_TOKEN_BLOCK, PEER_HEADS, PEER_TOPK)))
    return out.reshape(b, s, d).astype(hn.dtype)

def first_inputs(seed: int = 0) -> dict:
    key = jax.random.key(seed)
    ks = jax.random.split(key, 20)
    f32 = jnp.float32
    nrm = lambda k, shape, sc: jax.random.normal(k, shape, f32) * sc
    gain = lambda k, shape: 1.0 + 0.02 * jax.random.normal(k, shape, f32)
    dt0 = jnp.exp(jax.random.uniform(ks[8], (DEPTH, SSD_HEADS), f32, float(np.log(1e-3)), float(np.log(1e-1))))
    return {
        "x": jax.random.normal(ks[0], (BATCH, SEQ, D_MODEL), f32),
        "attn_norm": gain(ks[1], (DEPTH, D_MODEL)),
        "w_in": nrm(ks[2], (DEPTH, D_MODEL, IN_PROJ_DIM), D_MODEL ** -0.5),
        "sb_q_norm": gain(ks[3], (DEPTH, SB_HEAD_DIM)),
        "sb_k_norm": gain(ks[4], (DEPTH, SB_HEAD_DIM)),
        "conv_w": nrm(ks[5], (DEPTH, SSD_CONV, 1, SSD_CONV_DIM), SSD_CONV ** -0.5),
        "conv_b": nrm(ks[6], (DEPTH, SSD_CONV_DIM), 0.02),
        "dt_bias": jnp.log(jnp.expm1(dt0)),
        "a_log": jnp.log(jax.random.uniform(ks[9], (DEPTH, SSD_HEADS), f32, 1.0, 16.0)),
        "d_skip": gain(ks[10], (DEPTH, SSD_HEADS)),
        "sb_out_norm": gain(ks[11], (DEPTH, SB_WIDTH)),
        "ssd_out_norm": gain(ks[12], (DEPTH, SSD_WIDTH)),
        "w_out": nrm(ks[13], (DEPTH, MIX_WIDTH, D_MODEL), MIX_WIDTH ** -0.5),
        "ffn_norm": gain(ks[14], (DEPTH, D_MODEL)),
        "peer_query": nrm(ks[15], (DEPTH, D_MODEL, PEER_HEADS * PEER_KEY_DIM), D_MODEL ** -0.5),
        "peer_sub_keys": nrm(ks[16], (DEPTH, PEER_HEADS, 2, PEER_N_KEYS, PEER_HALF), PEER_HALF ** -0.5),
        "peer_down": nrm(ks[17], (DEPTH, PEER_N_EXPERTS, D_MODEL), D_MODEL ** -0.5),
        "peer_up": nrm(ks[18], (DEPTH, PEER_N_EXPERTS, D_MODEL), (PEER_HEADS * PEER_TOPK) ** -0.5),
    }

def first_block(x, attn_norm, w_in, sb_q_norm, sb_k_norm, conv_w, conv_b, dt_bias, a_log, d_skip,
              sb_out_norm, ssd_out_norm, w_out, ffn_norm, peer_query, peer_sub_keys, peer_down, peer_up):
    h = x
    for layer in range(DEPTH):
        xn = rms_norm(h, attn_norm[layer])
        h = h + hybrid_mixer(xn, w_in[layer], sb_q_norm[layer], sb_k_norm[layer], conv_w[layer],
                             conv_b[layer], dt_bias[layer], a_log[layer], d_skip[layer],
                             sb_out_norm[layer], ssd_out_norm[layer], w_out[layer])
        hn = rms_norm(h, ffn_norm[layer])
        h = h + peer_ffn(hn, peer_query[layer], peer_sub_keys[layer], peer_down[layer], peer_up[layer])
    return h


DEPTH_2 = 2

N_MIXERS = 2
N_POOL_LAYERS = (DEPTH_2 + 1) // 2
N_ATTN_LAYERS = DEPTH_2 // 2
EPS = 1e-6

POOL_WINDOWS = (2, 4, 8, 16)
N_POOL_GROUPS = 4
POOL_GROUP_DIM = D_MODEL // N_POOL_GROUPS
POOL_IN = 2 * D_MODEL

N_HEADS = 16
HEAD_DIM = D_MODEL // N_HEADS
ATTN_WIDTH = N_HEADS * HEAD_DIM
ROT_DIM = HEAD_DIM // 4
IDX_HEADS = 16
IDX_DIM = 64
IDX_ROT = IDX_DIM // 4
ROPE_THETA = 500000.0
TOP_K_MAX = 256
Q_BLOCK = 128
ATTN_SPLITS = (ATTN_WIDTH, 2 * ATTN_WIDTH, 3 * ATTN_WIDTH, 4 * ATTN_WIDTH,
               4 * ATTN_WIDTH + IDX_HEADS * IDX_DIM,
               4 * ATTN_WIDTH + IDX_HEADS * IDX_DIM + IDX_DIM)
ATTN_IN = 4 * ATTN_WIDTH + IDX_HEADS * IDX_DIM + IDX_DIM + IDX_HEADS


def rms_norm_2(x, g):
    xf = x.astype(jnp.float32)
    y = xf * lax.rsqrt(jnp.mean(xf * xf, axis=-1, keepdims=True) + EPS)
    return (y * g.astype(jnp.float32)).astype(x.dtype)

def rope_partial(x, positions, rot_dim):
    half = rot_dim // 2
    inv_freq = ROPE_THETA ** (-jnp.arange(half, dtype=jnp.float32) * 2.0 / rot_dim)
    ang = positions.astype(jnp.float32)[..., None] * inv_freq
    cos = jnp.cos(ang)[:, :, None, :]
    sin = jnp.sin(ang)[:, :, None, :]
    xf = x.astype(jnp.float32)
    x1, x2, rest = xf[..., :half], xf[..., half:rot_dim], xf[..., rot_dim:]
    out = jnp.concatenate([x1 * cos - x2 * sin, x2 * cos + x1 * sin, rest], axis=-1)
    return out.astype(x.dtype)

def pool_branch(h, w_in, w_grp, layer_scale, w_out):
    B, L, D = h.shape
    v, gate = jnp.split(h @ w_in, 2, axis=-1)
    vf = v.astype(jnp.float32)
    cs = jnp.concatenate([jnp.zeros((B, 1, D), jnp.float32),
                          jnp.cumsum(vf, axis=1)], axis=1)
    t = jnp.arange(L, dtype=jnp.int32)
    outs = []
    for gi, w in enumerate(POOL_WINDOWS):
        sl = slice(gi * POOL_GROUP_DIM, (gi + 1) * POOL_GROUP_DIM)
        lo = jnp.maximum(t + 1 - w, 0)
        window_sum = cs[:, t + 1, sl] - cs[:, lo, sl]
        count = jnp.minimum(t + 1, w).astype(jnp.float32)[None, :, None]
        pooled = (window_sum / count - vf[:, :, sl]).astype(h.dtype)
        outs.append(jnp.einsum('bsc,cd->bsd', pooled, w_grp[gi]))
    mixed = jnp.concatenate(outs, axis=-1) * layer_scale
    return (mixed * jax.nn.silu(gate)) @ w_out

def dsa_branch(h, positions, w_in, w_out):
    B, L, _ = h.shape
    proj = h @ w_in
    q, k, v, gate, qi, ki, wi = jnp.split(proj, ATTN_SPLITS, axis=-1)
    q = rope_partial(q.reshape(B, L, N_HEADS, HEAD_DIM), positions, ROT_DIM)
    k = rope_partial(k.reshape(B, L, N_HEADS, HEAD_DIM), positions, ROT_DIM)
    v = v.reshape(B, L, N_HEADS, HEAD_DIM)
    qi = rope_partial(qi.reshape(B, L, IDX_HEADS, IDX_DIM), positions, IDX_ROT)
    ki = rope_partial(ki.reshape(B, L, 1, IDX_DIM), positions, IDX_ROT)[:, :, 0]
    ki_f = ki.astype(jnp.float32)
    top_k = min(TOP_K_MAX, L // 4)
    nb = L // Q_BLOCK
    key_idx = jnp.arange(L, dtype=jnp.int32)
    idx_scale = (IDX_HEADS ** -0.5) * (IDX_DIM ** -0.5)
    attn_scale = HEAD_DIM ** -0.5

    def to_blocks(a):
        return jnp.moveaxis(a.reshape(B, nb, Q_BLOCK, *a.shape[2:]), 1, 0)

    def block_fn(args):
        qb, qib, wb, tb = args
        s = jnp.einsum('bqhd,bsd->bqhs', qib.astype(jnp.float32), ki_f)
        score = jnp.einsum('bqhs,bqh->bqs', jax.nn.relu(s),
                           wb.astype(jnp.float32)) * idx_scale
        admissible = key_idx[None, None, :] <= tb[None, :, None]
        score = jnp.where(admissible, score, -jnp.inf)
        _, sel = lax.top_k(score, top_k)
        valid = sel <= tb[None, :, None]
        k_sel = jax.vmap(lambda kk, ii: kk[ii])(k, sel)
        v_sel = jax.vmap(lambda vv, ii: vv[ii])(v, sel)
        logits = jnp.einsum('bqhd,bqkhd->bhqk', qb, k_sel).astype(jnp.float32) * attn_scale
        logits = jnp.where(valid[:, None], logits, -jnp.inf)
        p = jax.nn.softmax(logits, axis=-1).astype(v.dtype)
        return jnp.einsum('bhqk,bqkhd->bqhd', p, v_sel)

    t_blocks = key_idx.reshape(nb, Q_BLOCK)
    outs = lax.map(block_fn, (to_blocks(q), to_blocks(qi), to_blocks(wi), t_blocks))
    o = jnp.moveaxis(outs, 0, 1).reshape(B, L, ATTN_WIDTH)
    return (o * jax.nn.silu(gate)) @ w_out

def second_inputs(seed: int = 0) -> dict:
    key = jax.random.key(seed)
    ks = jax.random.split(key, 13)
    D = D_MODEL
    x = jax.random.normal(ks[0], (BATCH, SEQ, D), jnp.float32)
    c = jax.random.normal(ks[1], (BATCH, D), jnp.float32)
    positions = jnp.broadcast_to(jnp.arange(SEQ, dtype=jnp.int32)[None, :], (BATCH, SEQ))
    norm_g = 1.0 + 0.02 * jax.random.normal(ks[2], (DEPTH_2, D), jnp.float32)
    mod_w = 0.5 * D ** -0.5 * jax.random.normal(ks[3], (DEPTH_2, D, 3 * D), jnp.float32)
    mod_b = 0.02 * jax.random.normal(ks[4], (DEPTH_2, 3 * D), jnp.float32)
    pool_w_in = D ** -0.5 * jax.random.normal(ks[5], (N_POOL_LAYERS, D, POOL_IN), jnp.float32)
    pool_w_grp = POOL_GROUP_DIM ** -0.5 * jax.random.normal(
        ks[6], (N_POOL_LAYERS, N_POOL_GROUPS, POOL_GROUP_DIM, POOL_GROUP_DIM), jnp.float32)
    pool_scale = 1.0 + 0.1 * jax.random.normal(ks[7], (N_POOL_LAYERS, D), jnp.float32)
    pool_w_out = D ** -0.5 * jax.random.normal(ks[8], (N_POOL_LAYERS, D, D), jnp.float32)
    attn_w_in = D ** -0.5 * jax.random.normal(ks[9], (N_ATTN_LAYERS, D, ATTN_IN), jnp.float32)
    attn_w_out = ATTN_WIDTH ** -0.5 * jax.random.normal(
        ks[10], (N_ATTN_LAYERS, ATTN_WIDTH, D), jnp.float32)
    final_g = 1.0 + 0.02 * jax.random.normal(ks[11], (D,), jnp.float32)
    return {"x": x, "c": c, "positions": positions, "norm_g": norm_g,
            "mod_w": mod_w, "mod_b": mod_b, "pool_w_in": pool_w_in,
            "pool_w_grp": pool_w_grp, "pool_scale": pool_scale,
            "pool_w_out": pool_w_out, "attn_w_in": attn_w_in,
            "attn_w_out": attn_w_out, "final_g": final_g}

def second_block(x, c, positions, norm_g, mod_w, mod_b, pool_w_in, pool_w_grp,
              pool_scale, pool_w_out, attn_w_in, attn_w_out, final_g):
    cond = jax.nn.silu(c)
    for i in range(DEPTH_2):
        mod = cond @ mod_w[i] + mod_b[i]
        shift, scale, gate = jnp.split(mod, 3, axis=-1)
        h = rms_norm_2(x, norm_g[i]) * (1.0 + scale[:, None, :]) + shift[:, None, :]
        j = i // N_MIXERS
        if i % N_MIXERS == 0:
            out = pool_branch(h, pool_w_in[j], pool_w_grp[j], pool_scale[j], pool_w_out[j])
        else:
            out = dsa_branch(h, positions, attn_w_in[j], attn_w_out[j])
        x = x + gate[:, None, :] * out
    return rms_norm_2(x, final_g)


def setup_inputs(seed=0):
    out = dict(first_inputs(seed))
    for name, value in second_inputs(seed + 1).items():
        if name != "x":
            out[name + "_2"] = value
    return out


def reference(
    x, attn_norm, w_in, sb_q_norm, sb_k_norm, conv_w, conv_b, dt_bias, a_log, d_skip,
    sb_out_norm, ssd_out_norm, w_out, ffn_norm, peer_query, peer_sub_keys, peer_down, peer_up,
    c_2, positions_2, norm_g_2, mod_w_2, mod_b_2, pool_w_in_2, pool_w_grp_2, pool_scale_2,
    pool_w_out_2, attn_w_in_2, attn_w_out_2, final_g_2,
):
    x = first_block(
        x, attn_norm, w_in, sb_q_norm, sb_k_norm, conv_w, conv_b, dt_bias, a_log, d_skip,
        sb_out_norm, ssd_out_norm, w_out, ffn_norm, peer_query, peer_sub_keys, peer_down,
        peer_up,
    )
    return second_block(
        x, c_2, positions_2, norm_g_2, mod_w_2, mod_b_2, pool_w_in_2, pool_w_grp_2,
        pool_scale_2, pool_w_out_2, attn_w_in_2, attn_w_out_2, final_g_2,
    )


_drawn_inputs = setup_inputs


def setup_inputs(seed=0):
    import zlib

    import numpy as np

    out = dict(_drawn_inputs(seed))
    spreads = {}
    factors = {'attn_norm': 2.682,
     'sb_q_norm': 8.0,
     'sb_k_norm': 8.0,
     'conv_b': 3.947,
     'd_skip': 6.636,
     'sb_out_norm': 5.125,
     'ssd_out_norm': 4.946,
     'ffn_norm': 8.0,
     'norm_g_2': 8.0,
     'mod_b_2': 4.795,
     'pool_scale_2': 4.338,
     'final_g_2': 2.865}
    for name, (base, spread) in spreads.items():
        noise = np.random.default_rng([zlib.crc32(name.encode()), seed]).standard_normal(out[name].shape)
        drawn = base * np.exp(spread * noise) if base else spread * noise
        out[name] = __import__('jax').numpy.asarray(drawn.astype(out[name].dtype))
    for name, factor in factors.items():
        out[name] = (out[name] * factor).astype(out[name].dtype)
    return out
```

```python
from contextlib import ExitStack

import concourse.bass as bass
from concourse import mybir
import numpy as np

F32 = mybir.dt.float32
I32 = mybir.dt.int32
U32 = mybir.dt.uint32
ALU = mybir.AluOpType
ACT = mybir.ActivationFunctionType
AX = mybir.AxisListType.X

P = 128
D = 2048
NB = 2
T = NB * P
KC = D // P
EPS = 1e-6
UPS = 8 + 16 * 8
SLOTS = 5
UNIT = 4096
SBH, SSH = 8, 16
XC = 12
PH, NK, TOPK = 8, 128, 16
NH, IH = 16, 16
SELECT = 64
WINDOWS = (2, 4, 8, 16)
NEG = -3.0e38
TAKEN = -3.3e38
MASKED = -1.0e30
TWO_PI_HI = 6.28125
TWO_PI_LO = float(np.float32(2 * np.pi - 6.28125))
PI = 3.1415925
INV_FREQ = [float(v) for v in (np.float32(500000.0) ** (-np.arange(16, dtype=np.float32) * np.float32(2.0) / np.float32(32)))]

A_NORM, A_MIX, A_Q, A_K, A_CB, A_CW, A_ROWS = 0, 16, 32, 33, 34, 46, 94
B_NORM, B_SCALE, B_COND, B_ROWS = 0, 32, 48, 64

STAGES = [
    ("q", "w_in", 0, 2, "N"), ("k", "w_in", 1024, 2, "N"), ("v", "w_in", 2048, 2, "N"),
    ("z", "w_in", 3072, 2, "N"), ("xbc", "w_in", 4096, 3, "T"), ("mix", "w_out", 0, 4, "N"),
    ("query", "peer_query", 0, 4, "T"),
    ("pv", "pool_w_in", 0, 4, "T"), ("pg", "pool_w_in", 2048, 4, "T"), ("grp", "pool_w_grp", 0, 4, "G"),
    ("po", "pool_w_out", 0, 4, "N"),
    ("aq", "attn_w_in", 0, 4, "N"), ("ak", "attn_w_in", 2048, 4, "N"), ("av", "attn_w_in", 4096, 4, "N"),
    ("ag", "attn_w_in", 6144, 4, "T"), ("ai", "attn_w_in", 8192, 2, "N"), ("ao", "attn_w_out", 0, 4, "N"),
]


def plan():
    first, units, halves, g = {}, [], 0, 0
    for name, weight, col, n, kind in STAGES:
        first[name] = g
        for c in range(n):
            if kind == "N":
                halves += 1
                units.append((g, kind, weight, col + 512 * c, 0, ("half", halves)))
                units.append((g, kind, weight, col + 512 * c, 1, ("bank", 2 * g + 2)))
            elif kind == "T":
                for u in range(2):
                    units.append((g, kind, weight, col + 512 * c + 256 * u, u, ("bank", 2 * g + u + 1)))
            elif c % 2 == 0:
                units.append((g, kind, weight, 0, c, ("bank", 2 * (g + 1) + 2)))
            g += 1
    return first, units


FIRST, UNITS = plan()
UNITS_OF = {}
for _n, _u in enumerate(UNITS):
    UNITS_OF.setdefault(_u[0], []).append(_n)
N_BEFORE = sum(1 for u in UNITS if u[0] < FIRST["pv"])


ROOTS = {0: 1, 1: 3, 2: 4, 3: 5, 4: 6, 5: 7}
ROW_NORMS = (0, 2, 3, 4, 5)


def done(g, i):
    return 2 * g + i + 1


def program(nc, a, out, mod_raw, mod_full):
    with ExitStack() as ctx:
        def sb(name, shape, dt=F32):
            return ctx.enter_context(nc.sbuf_tensor(name, shape, dt))

        def sem(name):
            return ctx.enter_context(nc.semaphore(name))

        ring = sb("ring", [P, SLOTS, UNIT])
        xres = sb("xres", [P, NB, D])
        nat = sb("nat", [P, NB, D])
        actT = sb("actT", [P, KC, T])
        big = sb("big", [P, 12288])
        wide = sb("wide", [P, D])
        stage = sb("stage", [P, 2, 512])
        work = sb("work", [P, 1792])
        ident = sb("ident", [P, P])
        later_ones = sb("later_ones", [P, P])
        prefix_ones = sb("prefix_ones", [P, P])
        ones = sb("ones", [P, P])
        sb_mask = sb("sb_mask", [P, 384])
        rows_a = sb("rows_a", [A_ROWS, P])
        rows_b = sb("rows_b", [B_ROWS, P])
        cols_a = sb("cols_a", [P, A_ROWS])
        cols_b = sb("cols_b", [P, B_ROWS])
        cond = sb("cond", [P, KC])
        const = sb("const", [P, 4])
        iota_i = sb("iota_i", [P, 16], I32)
        iota_f = sb("iota_f", [P, 16])
        inv_freq = sb("inv_freq", [P, 16])
        pos_i = sb("pos_i", [P, NB], I32)
        pos_f = sb("pos_f", [P, NB])
        cosine = sb("cosine", [P, NB, 16])
        sine = sb("sine", [P, NB, 16])
        ang = sb("ang", [P, 4, NB, 16])
        ang_i = sb("ang_i", [P, NB, 16], I32)
        bc16 = sb("bc16", [P, 3, 16])
        ssq = sb("ssq", [P, 16])
        root = sb("root", [P, 16])
        rinv = sb("rinv", [P, 16])
        hstat = sb("hstat", [P, 3, 4])
        dts = sb("dts", [P, 6, NB, 16])
        ds_out = sb("ds_out", [P, 4, 16])
        expert = sb("expert", [P, NB, PH * 16], I32)
        gates = sb("gates", [P, NB, PH * 16])
        gsum = sb("gsum", [P, 2, PH])
        expert_now = sb("expert_now", [P, 2, 16], I32)
        dots = sb("dots", [P, 2, 16])
        gelu = sb("gelu", [P, 2, 16])
        weight = sb("weight", [P, 2, 16])
        mod_cols = sb("mod_cols", [P, 96])
        mod_gain = sb("mod_gain", [P, 2, KC])
        ki_wi = sb("ki_wi", [P, NB, 144])
        best8 = sb("best8", [P, 8])
        smax = sb("smax", [P, 2, 3])
        ssum = sb("ssum", [P, 2, 4])
        junk = sb("junk", [P, 4])
        PS = ctx.enter_context(nc.psum_tensor("PS", [P, 8, 512], F32))

        act_flat = actT[:, :, :].rearrange("p k t -> p (k t)")
        gather_buf = ring[:, :, :].rearrange("p s (h d) -> p (s h) d", h=2)
        mod_buf = gather_buf[:, 8:10, :].rearrange("p s (k n) -> p s k n", k=4)
        qT_a = big[:, 0:2048].rearrange("p (h t) -> p h t", h=SBH)
        kT_a = big[:, 2048:4096].rearrange("p (h t) -> p h t", h=SBH)
        xbcT = big[:, 4096:7168].rearrange("p (c t) -> p c t", c=XC)
        scr = big[:, 7168:12288]
        xpad = scr[:, 0:XC * 259].rearrange("p (c t) -> p c t", c=XC)
        square = scr[:, 3200:3712]
        sb_l, sb_e, sb_sp = [scr[:, 1536 * i:1536 * (i + 1)].rearrange("p (h t) -> p h t", h=4) for i in range(3)]
        xs_nat = scr[:, 0:2048].rearrange("p (b n) -> p b n", b=NB)
        x_dt = scr[:, 2048:4096].rearrange("p (b n) -> p b n", b=NB)
        x_end = scr[:, 4096:5120]
        decay = big[:, 0:4096].rearrange("p (b h l) -> p b h l", b=NB, h=SSH)
        b_nat = act_flat[:, 0:256]
        cb_mask = act_flat[:, 256:768].rearrange("p (b g l) -> p b g l", b=NB, g=2)
        states = act_flat[:, 768:1792]
        y_tmp = act_flat[:, 1792:2816]
        y_skip = act_flat[:, 2816:3840]
        queryT = big[:, 0:4096].rearrange("p (s t) -> p s t", s=16)
        keys_nat = big[:, 4096:6144].rearrange("p (s k) -> p s k", s=16)
        keysT = big[:, 6144:8192].rearrange("p (s k) -> p s k", s=16)
        scores = [big[:, 8192:10240].rearrange("p (s k) -> p s k", s=16), keys_nat]
        cand = big[:, 10240:12288].rearrange("p (h c) -> p h c", h=PH)
        poolT = big[:, 0:4096].rearrange("p (c t) -> p c t", c=KC)
        pgateT = big[:, 4096:8192].rearrange("p (c t) -> p c t", c=KC)
        sums = [big[:, 8192 + 1024 * i:9216 + 1024 * i].rearrange("p (c t) -> p c t", c=4) for i in range(2)]
        counts = big[:, 10240:11264].rearrange("p (w t) -> p w t", w=4)
        qT_b = poolT
        kT_b = pgateT
        agateT = big[:, 8192:12288].rearrange("p (c t) -> p c t", c=NH)
        qiT = wide[:, :].rearrange("p (h t) -> p h t", h=8)
        w_dt = work[:, 0:256].rearrange("p (k n) -> p k n", k=KC)
        top_s = work[:, 0:256].rearrange("p (s k) -> p s k", s=16)
        top_u = work[:, 256:512].bitcast(U32).rearrange("p (s k) -> p s k", s=16)
        top_f = work[:, 512:768].rearrange("p (s k) -> p s k", s=16)
        best = work[:, 768:896].rearrange("p (h k) -> p h k", h=PH)
        pos_u = work[:, 896:1024].bitcast(U32).rearrange("p (h k) -> p h k", h=PH)
        pos_12 = work[:, 1024:1280].bitcast(U32).rearrange("p (c h k) -> p c h k", c=2, h=PH)
        pos_12f = work[:, 1280:1536].rearrange("p (c h k) -> p c h k", c=2, h=PH)
        half_id = work[:, 1536:1792].rearrange("p (c h k) -> p c h k", c=2, h=PH)
        w_small = work[:, 0:1280].rearrange("p (k n) -> p k n", k=KC)
        rope_t = work[:, 1280:1792].rearrange("p (i n) -> p i n", i=4)
        diag = stage[:, 0, :].rearrange("p (i n) -> p i n", i=4)
        mod_rows = stage[0:96, 1, 0:256].rearrange("p (i n) -> p i n", i=2)
        mod_row = big[0:1, 0:1536]
        kiT = sb_mask[:, 0:T]
        final_gain = big[:, 0:D]
        lm = act_flat[:, 0:768].rearrange("p (e s) -> p e s", e=2)
        pr = act_flat[:, 768:1536].rearrange("p (e s) -> p e s", e=2)
        prT = act_flat[:, 1536:2304].rearrange("p (e s) -> p e s", e=2)
        relu = act_flat[:, 2304:2816].rearrange("p (e s) -> p e s", e=2)
        iscore = act_flat[:, 2816:3328].rearrange("p (b s) -> p b s", b=NB)
        iwork = act_flat[:, 3328:3584]
        sel_bias = act_flat[:, 3584:3968]

        s_in = sem("x_loaded")
        s_rows = sem("rows_loaded")
        s_bc = sem("spread_rows_loaded")
        s_wdt = sem("w_dt_loaded")
        s_wsmall = sem("w_small_loaded")
        s_keys = sem("keys_loaded")
        s_wide = sem("wide_loaded")
        s_modr = sem("mod_rows_loaded")
        s_modst = sem("mod_stored")
        s_out = sem("out_stored")
        s_fin = sem("final_gain_loaded")
        s_issue = sem("gathers_issued")
        s_now = sem("experts_of_head")
        s_cnt = sem("window_counts")
        s_causal = sem("selection_causal")
        s_xpad = sem("conv_padded")
        s_resu = sem("residual_with_experts")
        s_iuse = sem("index_relu_used")
        unit_in = [sem(f"unit_in_slot{i}") for i in range(SLOTS)]
        half_used = sem("half_used")
        bank_done = sem("gemm_bank_done")
        bank_free = [sem(f"gemm_bank_free{i}") for i in range(4)]
        s_const = sem("constants_ready")
        s_pool = sem("pool_step")
        s_dve = sem("dve_step")
        s_act = sem("act_step")
        s_colps = sem("columns_in_psum")
        s_cols = sem("columns_ready")
        s_ssq = sem("square_sums")
        s_root = sem("roots")
        s_nat = sem("normed_rows")
        s_tp = sem("transposes_done")
        s_xt = sem("activations_T")
        s_shift = sem("shifted_T")
        s_qkst = sem("qk_staged")
        s_qkrt = sem("qk_roots")
        s_qkss = sem("qk_square_sums")
        s_qkn = sem("qk_normed")
        s_qktp = sem("qk_transposed")
        s_qkT = sem("qk_T_ready")
        s_xraw = sem("conv_input")
        s_conv = sem("conv_done")
        s_silu = sem("conv_silu")
        s_dtps = sem("dt_in_psum")
        s_dtst = sem("dt_rows")
        s_dtl = sem("dt_log")
        s_dt = sem("dt_ready")
        s_L = sem("sb_logits")
        s_neg = sem("sb_neg_abs")
        s_ln = sem("sb_log1p")
        s_sp = sem("sb_softplus")
        s_S = sem("sb_later")
        s_w0 = sem("sb_exponent")
        s_w1 = sem("sb_exp")
        s_w = sem("sb_weights")
        s_O = sem("sb_out_psum")
        s_att = sem("sb_out")
        s_xsps = sem("xs_transposed")
        s_xs = sem("xs_natural")
        s_acsps = sem("cumulated_psum")
        s_acs = sem("cumulated")
        s_R = sem("cumulated_rows")
        s_seg = sem("segments")
        s_dec = sem("decay")
        s_edge = sem("edge_decays")
        s_edgein = sem("edge_decay_inputs")
        s_cbps = sem("cb_psum")
        s_cb = sem("cb_masked")
        s_sc = sem("ssd_scores")
        s_xf = sem("ssd_x")
        s_yd = sem("y_diag")
        s_stps = sem("states_psum")
        s_st = sem("states")
        s_yo = sem("y_off")
        s_y = sem("y_rows")
        s_res = sem("residual_ready")
        s_ktps = sem("keys_transposed")
        s_kt = sem("keys_T")
        s_scps = sem("peer_scores_psum")
        s_psc = sem("peer_scores")
        s_gin = sem("gate_exponents")
        s_gex = sem("gate_exps")
        s_route = sem("routing_ready")
        landed = [sem(f"gathered_buf{i}") for i in range(8)]
        s_down = sem("down_used")
        s_up = sem("up_used")
        s_gelu = sem("gelu_ready")
        s_wt = sem("expert_weights")
        s_diag = sem("diagonals")
        mod_in = [sem(f"mod_in{i}") for i in range(2)]
        s_modu = sem("mod_used")
        s_mode = sem("mod_chunk_copied")
        s_modf = sem("mod_full_ready")
        s_modps = sem("mod_cols_psum")
        s_modc = sem("mod_cols_ready")
        s_pool_T = sem("pooled_T")
        s_angle = sem("angles")
        s_trig = sem("sines")
        s_rst = sem("rope_staged")
        s_rope = sem("roped")
        s_rtp = sem("rope_transposed")
        s_rT = sem("qkT_ready")
        s_kips = sem("ki_psum")
        s_kist = sem("ki_staged")
        s_kirope = sem("ki_roped")
        s_kitp = sem("ki_transposed")
        s_kiT = sem("kiT_ready")
        s_ips = sem("index_psum")
        s_relu = sem("index_relu")
        s_iacc = sem("index_sum")
        s_iadm = sem("index_admissible")
        s_sel = sem("selection")
        s_lps = sem("logits_psum")
        s_lm = sem("logits_masked")
        s_pe = sem("probs_exp")
        s_pn = sem("probs_normed")
        s_ptps = sem("probs_transposed")
        s_pT = sem("probs_T")
        s_ops = sem("attn_out_psum")
        s_oT = sem("attn_out_T")

        def spread(src, n):
            return bass.AP(tensor=src.tensor, offset=src.offset, ap=[[0, P], [1, n]])

        def counted(eng, default):
            counts = {}

            def step(ins, s=default, by=1):
                counts[s.name] = counts.get(s.name, 0) + by
                ins.then_inc(s, by)
                eng.wait_ge(s, counts[s.name])

            def mark(ins, s, by=1):
                counts[s.name] = counts.get(s.name, 0) + by
                ins.then_inc(s, by)
            return step, mark

        def copied(eng, name, chunks=2):
            n = next(x[3] for x in STAGES if x[0] == name)
            for g in range(FIRST[name] + n - chunks, FIRST[name] + n):
                for i in range(2):
                    eng.wait_ge(bank_free[2 * (g % 2) + i], g // 2 + 1)

        block = ctx.enter_context(nc.Block())

        @block.sync
        def _(sp):
            weights = {k: a[k] for k in ("w_in", "w_out", "peer_query")}
            weights["pool_w_in"], weights["pool_w_out"] = a["pool_w_in_2"], a["pool_w_out_2"]
            weights["attn_w_in"], weights["attn_w_out"] = a["attn_w_in_2"], a["attn_w_out_2"]
            for b in range(NB):
                sp.dma_start(xres[:, b, :], a["x"][0, b * P:(b + 1) * P, :]).then_inc(s_in, 16)

            def load(n):
                _, kind, w, col, part, _ = UNITS[n]
                slot = ring[:, n % SLOTS, :]
                if kind == "N":
                    src = weights[w][0, part * 1024:(part + 1) * 1024, col:col + 512]
                    dst = slot.rearrange("p (k n) -> p k n", k=8)
                    src = src.rearrange("(k p) n -> p k n", p=P)
                elif kind == "T":
                    src = weights[w][0, :, col:col + 256].rearrange("(k p) n -> p k n", p=P)
                    dst = slot.rearrange("p (k n) -> p k n", k=KC)
                else:
                    src = a["pool_w_grp_2"][0, part:part + 2].rearrange("g (k p) n -> p (g k) n", p=P)
                    dst = slot.rearrange("p (k n) -> p k n", k=8)
                sp.dma_start(dst, src).then_inc(unit_in[n % SLOTS], 16)

            for n in range(N_BEFORE):
                if n >= SLOTS:
                    what, value = UNITS[n - SLOTS][5]
                    sp.wait_ge(half_used if what == "half" else bank_done, value)
                load(n)
            sp.wait_ge(bank_done, done(FIRST["pv"] - 1, 1))
            for layer in range(NB):
                mw = a["mod_w_2"][layer].rearrange("(k p) n -> p k n", p=P)
                with sp.Fori(0, 4) as j:
                    for m in range(12):
                        sp.wait_ge(s_modu, j * 12 + (48 * layer + m + 1))
                        quarter = m % 4
                        sp.dma_start(mod_buf[:, m % 2], mw[:, 4 * quarter:4 * quarter + 4,
                                                          bass.ds(j * 1536 + (m // 4) * 512, 512)]).then_inc(mod_in[m % 2], 16)
            sp.wait_ge(s_up, UPS * NB)
            sp.wait_ge(s_modu, 2 + 48 * NB)
            for n in range(N_BEFORE, len(UNITS)):
                if n >= N_BEFORE + SLOTS:
                    what, value = UNITS[n - SLOTS][5]
                    sp.wait_ge(half_used if what == "half" else bank_done, value)
                load(n)
            for b in range(NB):
                sp.wait_ge(s_y, 4 + b)
                sp.dma_start(out[0, b * P:(b + 1) * P, :], nat[:, b, :]).then_inc(s_out, 16)
            sp.wait_ge(s_out, 16 * NB)

        @block.gpsimd
        def _(pool):
            step, mark = counted(pool, s_pool)
            g = nc.gpsimd
            step(g.memset(ident[:], 0.0))
            step(g.affine_select(out=ident[:], in_=ident[:], compare_op=ALU.not_equal, fill=1.0, base=0,
                                 pattern=[[-1, P]], channel_multiplier=1))
            step(g.memset(ones[:], 1.0))
            step(g.affine_select(out=later_ones[:], in_=ones[:], compare_op=ALU.is_gt, fill=0.0, base=0,
                                 pattern=[[-1, P]], channel_multiplier=1))
            step(g.affine_select(out=prefix_ones[:], in_=ones[:], compare_op=ALU.is_ge, fill=0.0, base=0,
                                 pattern=[[1, P]], channel_multiplier=-1))
            for i in (0, 2):
                step(g.affine_select(out=sb_mask[:, i * P:(i + 1) * P], in_=ones[:], compare_op=ALU.is_gt,
                                     fill=0.0, base=0, pattern=[[1, P]], channel_multiplier=-1))
            step(g.memset(sb_mask[:, P:2 * P], 1.0))
            for i, v in enumerate((EPS, 1.0, float(np.pi / 2), 0.0)):
                step(g.memset(const[:, i:i + 1], v))
            for i, v in enumerate(INV_FREQ):
                step(g.memset(inv_freq[:, i:i + 1], v))
            step(g.iota(iota_i[:], pattern=[[1, 16]], base=0, channel_multiplier=0))
            mark(g.tensor_copy(iota_f[:], iota_i[:]), s_const)

            tables = [a[k].rearrange("a e d -> (a e) d") for k in ("peer_down", "peer_up")]
            pool.wait_ge(bank_done, done(FIRST["pv"] - 1, 1))
            for b in range(NB):
                pool.wait_ge(s_route, b + 1)
                with pool.Fori(0, PH // 2) as j:
                    for e in range(2):
                        H = j * 2 + (PH * b + e)
                        per = bass.ds((j * 2 + e) * 16, 16)
                        g.tensor_copy(expert_now[:, e, :], expert[:, b, per]).then_inc(s_now, 1)
                        pool.wait_ge(s_now, H + 1)
                        for s in range(32):
                            buf = s % 8
                            if s < 8:
                                pool.wait_ge(s_up, H * 16 + (8 * b + buf + 1))
                            elif s < 24:
                                pool.wait_ge(s_down, H * 16 + (s - 8 + 1))
                            else:
                                pool.wait_ge(s_up, H * 16 + (8 * (b + 1) + buf + 1))
                            pool.sem_inc(s_issue, 1)
                            k = s % 16
                            g.indirect_dma_start(out=gather_buf[:, buf, :], out_offset=None, in_=tables[s // 16],
                                                 in_offset=bass.IndirectOffsetOnAxis(ap=expert_now[:, e, k:k + 1], axis=0)
                                                 ).then_inc(landed[buf], 16)

            for w, width in enumerate(WINDOWS):
                g.iota(counts[:, w, :].bitcast(I32), pattern=[[1, T]], base=1, channel_multiplier=0).then_inc(s_cnt, 1)
            for b in range(NB):
                S = P * (b + 1)
                pool.wait_ge(s_iacc, 1 + b)
                g.affine_select(out=iscore[:, b, 0:S], in_=iscore[:, b, 0:S], compare_op=ALU.is_ge, fill=NEG,
                                base=P * b, pattern=[[-1, S]], channel_multiplier=1).then_inc(s_iadm, 1)
                pool.wait_ge(s_sel, 1 + b)
                o = sel_bias[:, 0:P] if b == 0 else sel_bias[:, P:]
                g.affine_select(out=o, in_=o, compare_op=ALU.is_ge, fill=MASKED,
                                base=P * b, pattern=[[-1, S]], channel_multiplier=1).then_inc(s_causal, 1)

        @block.tensor
        def _(pe):
            mm, tr = nc.tensor.matmul, nc.tensor.transpose

            def banks_free(g):
                if g >= 2:
                    for i in range(2):
                        pe.wait_ge(bank_free[2 * (g % 2) + i], g // 2)

            def arrived(n):
                pe.wait_ge(unit_in[n % SLOTS], 16 * (n // SLOTS + 1))

            def gemm(name, lhs, before=None):
                n_chunks, kind = next((n, k) for m, _, _, n, k in STAGES if m == name)
                for g in range(FIRST[name], FIRST[name] + n_chunks):
                    if before is not None:
                        before(g - FIRST[name])
                    banks_free(g)
                    bank = 2 * (g % 2)
                    for part, n in enumerate(UNITS_OF[g]):
                        arrived(n)
                        slot = ring[:, n % SLOTS, :]
                        if kind == "N":
                            w = slot.rearrange("p (k n) -> p k n", k=8)
                            for b in range(NB):
                                for k in range(8):
                                    last = mm(PS[:, bank + b, :], lhs[:, 8 * part + k, b * P:(b + 1) * P], w[:, k, :],
                                              start=(part == 0 and k == 0), stop=(part == 1 and k == 7))
                                if part == 1:
                                    last.then_inc(bank_done, 1)
                            if part == 0:
                                last.then_inc(half_used, 1)
                        else:
                            w = slot.rearrange("p (k n) -> p k n", k=KC)
                            for h in range(2):
                                for k in range(KC):
                                    last = mm(PS[:, bank + part, h * T:(h + 1) * T], w[:, k, h * P:(h + 1) * P],
                                              lhs[:, k, :], start=(k == 0), stop=(k == KC - 1))
                            last.then_inc(bank_done, 1)

            def turn(r):
                for t in range(8):
                    b, c = t // 4, t % 4
                    pe.wait_ge(s_nat, 2 * r + b + 1)
                    if t >= 4:
                        pe.wait_ge(s_xt, 8 * r + t - 3)
                    for i in range(4):
                        ch = 4 * c + i
                        last = tr(PS[:, 4 + t % 4, i * P:(i + 1) * P], nat[:, b, ch * P:(ch + 1) * P], ident[:])
                    last.then_inc(s_tp, 1)

            pe.wait_ge(s_const, 1)
            pe.wait_ge(s_rows, 16 * 10)
            tr(PS[:, 4, 0:A_ROWS], rows_a[:], ident[0:A_ROWS, 0:A_ROWS]).then_inc(s_colps, 1)
            tr(PS[:, 5, 0:B_ROWS], rows_b[:], ident[0:B_ROWS, 0:B_ROWS]).then_inc(s_modu, 2)
            pe.wait_ge(s_cols, 2)
            turn(0)
            pe.wait_ge(s_xt, 8)

            def turn_qk(i):
                pe.wait_ge(s_qkn, i + 1)
                if i >= 2:
                    pe.wait_ge(s_qkT, i - 1)
                for h in range(4):
                    last = tr(PS[:, 4 + i % 2, h * P:(h + 1) * P], stage[:, i % 2, h * P:(h + 1) * P], ident[:])
                last.then_inc(s_qktp, 1)

            def turns(one, c):
                if c >= 2:
                    one(2 * c - 4)
                    one(2 * c - 3)

            gemm("q", actT)
            gemm("k", actT, lambda c: turns(turn_qk, c + 2))
            gemm("v", actT, lambda c: turns(turn_qk, c + 4))
            gemm("z", actT)
            gemm("xbc", actT)
            pe.wait_ge(s_wdt, 16)
            for b in range(NB):
                for k in range(KC):
                    last = mm(PS[:, 6, 16 * b:16 * b + 16], actT[:, k, b * P:(b + 1) * P], w_dt[:, k, :],
                              start=(k == 0), stop=(k == KC - 1))
            last.then_inc(s_dtps, 1)

            vnat = nat[:, :, 0:1024]
            for t in range(2):
                if t == 0:
                    pe.wait_ge(s_qkT, 8)
                    pe.wait_ge(s_dtst, 1)
                    copied(pe, "v")
                else:
                    pe.wait_ge(s_att, 1)
                for i in range(4):
                    h = 4 * t + i
                    mm(PS[:, 4 + i, 0:T], kT_a[:, h, 0:P], qT_a[:, h, :], start=True, stop=True)
                    last = mm(PS[:, 4 + i, T:384], kT_a[:, h, P:T], qT_a[:, h, P:T], start=True, stop=True)
                last.then_inc(s_L, 1)
                pe.wait_ge(s_sp, t + 1)
                for i in range(4):
                    mm(PS[:, 4 + i, 0:384], later_ones[:], sb_sp[:, i, :], start=True, stop=True)
                    last = mm(PS[:, 4 + i, P:T], ones[:], sb_sp[:, i, T:384], start=False, stop=True,
                              skip_group_check=True)
                last.then_inc(s_S, 1)
                pe.wait_ge(s_w, t + 1)
                for i in range(4):
                    h = 4 * t + i
                    hp = slice(i * P, (i + 1) * P)
                    v = slice(h * P, (h + 1) * P)
                    mm(PS[:, 4, hp], sb_l[:, i, 0:P], vnat[:, 0, v], start=True, stop=True)
                    mm(PS[:, 5, hp], sb_l[:, i, P:T], vnat[:, 0, v], start=True, stop=False)
                    last = mm(PS[:, 5, hp], sb_l[:, i, T:384], vnat[:, 1, v], start=False, stop=True)
                last.then_inc(s_O, 1)

            pe.wait_ge(s_att, 2)
            pe.wait_ge(s_silu, 1)
            for b in range(NB):
                for c in range(8):
                    last = tr(PS[:, 4 + 2 * b + c // 4, (c % 4) * P:(c % 4 + 1) * P],
                              xbcT[:, c, b * P:(b + 1) * P], ident[:])
            last.then_inc(s_xsps, 1)
            pe.wait_ge(s_xs, 1)
            for g in range(2):
                last = tr(PS[:, 4, g * P:(g + 1) * P], xbcT[:, 8 + g, 0:P], ident[:])
            last.then_inc(s_xsps, 1)
            pe.wait_ge(s_dt, 1)
            for b in range(NB):
                last = mm(PS[:, 5, 16 * b:16 * b + 16], prefix_ones[:], dts[:, 3, b, :], start=True, stop=True)
            last.then_inc(s_acsps, 1)
            for b in range(NB):
                for g in range(2):
                    last = mm(PS[:, 6, (2 * b + g) * P:(2 * b + g + 1) * P], xbcT[:, 8 + g, b * P:(b + 1) * P],
                              xbcT[:, 10 + g, b * P:(b + 1) * P], start=True, stop=True)
            last.then_inc(s_cbps, 1)
            pe.wait_ge(s_acs, 1)
            pe.wait_ge(s_cb, 1)
            pe.wait_ge(s_xs, 2)
            for b in range(NB):
                if b:
                    pe.wait_ge(s_edgein, 1)
                for h in range(SSH):
                    last = mm(PS[:, 4 + h // 4, (h % 4) * P:(h % 4 + 1) * P],
                              dts[:, 3, b, h:h + 1].to_broadcast([P, P]), prefix_ones[:], start=True, stop=True)
                last.then_inc(s_R, 1)
            pe.wait_ge(s_xf, 2)
            pe.wait_ge(s_edgein, 2)
            for g in range(2):
                last = mm(PS[:, 4 + g, :], b_nat[:, g * P:(g + 1) * P], x_end[:, g * 512:(g + 1) * 512],
                          start=True, stop=True)
            last.then_inc(s_stps, 1)
            for b in range(NB):
                pe.wait_ge(s_sc, b + 1)
                if b == 1:
                    banks_free(FIRST["mix"])
                    banks_free(FIRST["mix"] + 1)
                for h in range(SSH):
                    bank = (6 if b == 0 else 0) + h // 8
                    last = mm(PS[:, bank, (h % 8) * 64:(h % 8 + 1) * 64], decay[:, b, h, :],
                              x_dt[:, b, h * 64:(h + 1) * 64], start=True, stop=True)
                last.then_inc(s_yd, 1)
            pe.wait_ge(s_st, 1)
            for g in range(2):
                last = mm(PS[:, 2 + g, :], xbcT[:, 10 + g, P:T], states[:, g * 512:(g + 1) * 512],
                          start=True, stop=True)
            last.then_inc(s_yo, 1)

            turn(1)
            pe.wait_ge(s_xt, 16)
            gemm("mix", actT)

            pe.wait_ge(s_keys, 16)
            turn(2)
            pe.wait_ge(s_xt, 24)
            for t in range(4):
                for i in range(4):
                    last = tr(PS[:, 4 + t, i * P:(i + 1) * P], keys_nat[:, 4 * t + i, :], ident[:])
            last.then_inc(s_ktps, 1)
            gemm("query", actT)
            pe.wait_ge(s_kt, 1)
            copied(pe, "query")
            for b in range(NB):
                if b:
                    pe.wait_ge(s_psc, 1)
                for s in range(16):
                    last = mm(PS[:, 4 + s // 4, (s % 4) * P:(s % 4 + 1) * P], queryT[:, s, b * P:(b + 1) * P],
                              keysT[:, s, :], start=True, stop=True)
                last.then_inc(s_scps, 1)
            pe.wait_ge(s_psc, 2)

            banks_free(FIRST["pv"])
            banks_free(FIRST["pv"] + 1)
            pe.wait_ge(s_mode, 3)
            for b in range(NB):
                if b:
                    pe.wait_ge(s_resu, 1)
                for n in range(4):
                    mm(PS[:, 4 + n, :], ident[:], xres[:, b, n * 512:(n + 1) * 512], start=True,
                       stop=True).then_inc(s_up, 2)
                with pe.Fori(0, PH // 2) as j:
                    def modulate(m):
                        pe.wait_ge(s_mode, j * 3 + (12 * b + m + 1))
                        for quarter in range(4):
                            i = 4 * m + quarter
                            pe.wait_ge(mod_in[i % 2], j * 96 + 16 * (24 * b + i // 2 + 1))
                            for k in range(4):
                                kk = 4 * quarter + k
                                last = mm(PS[0:1, m, :], cond[:, kk:kk + 1], mod_buf[:, i % 2, k, :],
                                          start=(kk == 0), stop=(kk == KC - 1))
                            last.then_inc(s_modu, 1)

                    for e in range(2):
                        H = j * 2 + (PH * b + e)
                        modulate(e)
                        for k in range(16):
                            pe.wait_ge(s_diag, H * 16 + (k + 1))
                            pe.wait_ge(landed[k % 8], H * 64 + 16 * (3 + k // 8))
                            for n in range(4):
                                last = mm(PS[:, 4 + n, :], diag[:, k % 4, :], gather_buf[:, k % 8, n * 512:(n + 1) * 512],
                                          start=False, stop=True, skip_group_check=True)
                            last.then_inc(s_up, 1)
                    modulate(2)

            pe.wait_ge(s_modf, 1)
            tr(PS[:, 3, 0:96], mod_rows[:, 0, :], ident[0:96, 0:96]).then_inc(s_modps, 1)
            pe.wait_ge(s_modc, 1)
            turn(3)
            pe.wait_ge(s_shift, 1)
            gemm("pv", actT)
            gemm("pg", actT)
            for i in range(4):
                g = FIRST["grp"] + i
                pe.wait_ge(s_pool_T, i + 1)
                banks_free(g)
                n = UNITS_OF[FIRST["grp"] + (i // 2) * 2][0]
                arrived(n)
                w = ring[:, n % SLOTS, :].rearrange("p (g k n) -> p g k n", g=2, k=4)[:, i % 2]
                for o in range(4):
                    for k in range(4):
                        last = mm(PS[:, 2 * (g % 2) + o // 2, (o % 2) * T:(o % 2 + 1) * T], w[:, k, o * P:(o + 1) * P],
                                  poolT[:, 4 * i + k, :], start=(k == 0), stop=(k == 3))
                    if o % 2:
                        last.then_inc(bank_done, 1)
            copied(pe, "grp")
            gemm("po", pgateT)
            turn(4)
            pe.wait_ge(s_shift, 2)

            def turn_rope(i):
                pe.wait_ge(s_rope, i + 1)
                if i >= 2:
                    pe.wait_ge(s_rT, i - 1)
                for h in range(4):
                    last = tr(PS[:, 4 + i % 2, h * P:(h + 1) * P], stage[:, i % 2, h * P:(h + 1) * P], ident[:])
                last.then_inc(s_rtp, 1)

            gemm("aq", actT, lambda c: turns(turn_rope, c))
            gemm("ak", actT, lambda c: turns(turn_rope, c + 4))
            gemm("av", actT, lambda c: turns(turn_rope, c + 8) if c < 2 else None)
            gemm("ag", actT)
            gemm("ai", actT)
            pe.wait_ge(s_wsmall, 16)
            for b in range(NB):
                for k in range(KC):
                    last = mm(PS[:, 6, 80 * b:80 * b + 80], actT[:, k, b * P:(b + 1) * P], w_small[:, k, :],
                              start=(k == 0), stop=(k == KC - 1))
            last.then_inc(s_kips, 1)
            for i in range(16, 20):
                turn_rope(i)
            pe.wait_ge(s_kirope, 1)
            for b in range(NB):
                last = tr(PS[:, 7, b * P:(b + 1) * P], ki_wi[:, b, 0:P], ident[:])
            last.then_inc(s_kitp, 1)
            pe.wait_ge(s_kiT, 1)
            pe.wait_ge(s_rT, 20)
            for b in range(NB):
                for h in range(IH):
                    i = IH * b + h
                    if i >= 4:
                        pe.wait_ge(s_relu, i - 3)
                    part = slice(64 * (h % 2), 64 * (h % 2) + 64)
                    mm(PS[:, 4 + i % 4, 0:P * (b + 1)], qiT[part, h // 2, b * P:(b + 1) * P],
                       kiT[part, 0:P * (b + 1)], start=True, stop=True).then_inc(s_ips, 1)
            pe.wait_ge(s_relu, 2 * IH)
            copied(pe, "av")

            def logits(h):
                if h >= 2:
                    pe.wait_ge(s_lm, 2 * (h - 1))
                mm(PS[:, 4 + h % 2, 0:P], qT_b[:, h, 0:P], kT_b[:, h, 0:P], start=True, stop=True)
                mm(PS[:, 4 + h % 2, P:384], qT_b[:, h, P:T], kT_b[:, h, :], start=True, stop=True).then_inc(s_lps, 1)

            def values(h):
                pe.wait_ge(s_pn, h + 1)
                if h >= 1:
                    pe.wait_ge(s_pT, h)
                for i in range(3):
                    last = tr(PS[:, 6, i * P:(i + 1) * P], pr[:, h % 2, i * P:(i + 1) * P], ident[:])
                last.then_inc(s_ptps, 1)

            def outputs(h):
                pe.wait_ge(s_pT, h + 1)
                if h >= 1:
                    pe.wait_ge(s_oT, h)
                mm(PS[:, 7, 0:T], nat[:, 0, h * P:(h + 1) * P], prT[:, h % 2, 0:T], start=True, stop=True)
                mm(PS[:, 7, P:T], nat[:, 1, h * P:(h + 1) * P], prT[:, h % 2, T:384], start=False, stop=True,
                   skip_group_check=True).then_inc(s_ops, 1)

            for h in range(NH + 2):
                if h < NH:
                    logits(h)
                if 1 <= h <= NH:
                    values(h - 1)
                if h >= 2:
                    outputs(h - 2)
            pe.wait_ge(s_oT, NH)
            gemm("ao", agateT)

        @block.scalar
        def _(act):
            step, mark = counted(act, s_act)
            A = nc.scalar.activation
            for dst, src, n in (
                (rows_a[A_NORM:A_NORM + 16], a["attn_norm"], 16),
                (rows_a[A_MIX:A_MIX + 8], a["sb_out_norm"], 8),
                (rows_a[A_MIX + 8:A_MIX + 16], a["ssd_out_norm"], 8),
                (rows_a[A_Q:A_Q + 1], a["sb_q_norm"], 1),
                (rows_a[A_K:A_K + 1], a["sb_k_norm"], 1),
                (rows_a[A_CB:A_CB + 12], a["conv_b"], 12),
            ):
                act.dma_start(dst, src.rearrange("a (c p) -> (a c) p", p=P)).then_inc(s_rows, 16)
            act.dma_start(rows_a[A_CW:A_CW + 48], a["conv_w"].rearrange("a w i (c p) -> (a w i c) p", p=P)).then_inc(s_rows, 16)
            act.dma_start(rows_b[B_NORM:B_NORM + 32], a["norm_g_2"].rearrange("l (c p) -> (l c) p", p=P)).then_inc(s_rows, 16)
            act.dma_start(rows_b[B_SCALE:B_SCALE + 16], a["pool_scale_2"].rearrange("l (c p) -> (l c) p", p=P)).then_inc(s_rows, 16)
            act.dma_start(rows_b[B_COND:B_COND + 16], a["c_2"].rearrange("l (c p) -> (l c) p", p=P)).then_inc(s_rows, 16)
            for i, k in enumerate(("dt_bias", "a_log", "d_skip")):
                act.dma_start(bc16[:, i, :], spread(a[k], 16)).then_inc(s_bc, 16)
            act.dma_start(pos_i[:], a["positions_2"].rearrange("a (b p) -> p (a b)", p=P),
                          allow_slow_non_contiguous=True).then_inc(s_bc, 16)
            act.dma_start(w_dt, a["w_in"][0, :, 5632:5648].rearrange("(k p) n -> p k n", p=P)).then_inc(s_wdt, 16)
            act.dma_start(wide[:], spread(a["ffn_norm"], D)).then_inc(s_wide, 16)

            def norm_stats(r):
                for b in range(NB):
                    if r == 0:
                        act.wait_ge(s_in, 16 * NB)
                    mark(A(act_flat[:, b * D:(b + 1) * D], xres[:, b, :], ACT.Square, accum_out=ssq[:, b:b + 1]), s_ssq)
                act.wait_ge(s_ssq, 2 * ROW_NORMS.index(r) + 2)
                mark(A(root[:, 0:2], ssq[:, 0:2], ACT.Sqrt, bias=const[:, 0:1], scale=1.0 / D), s_root)

            def copy_banks(name, dst):
                n = next(x[3] for x in STAGES if x[0] == name)
                for c in range(n):
                    g = FIRST[name] + c
                    for b in range(NB):
                        act.wait_ge(bank_done, done(g, b))
                        A(dst(c, b), PS[:, 2 * (g % 2) + b, :], ACT.Copy).then_inc(bank_free[2 * (g % 2) + b], 1)

            act.wait_ge(s_const, 1)
            norm_stats(0)
            act.wait_ge(s_cols, 2)
            mark(A(cond[:], cols_b[:, B_COND:B_COND + 16], ACT.Silu), s_mode, 3)

            def qk_stage(i):
                g = FIRST["q"] + i // 2
                act.wait_ge(bank_done, done(g, i % 2))
                if i >= 2:
                    act.wait_ge(s_qktp, i - 1)
                A(stage[:, i % 2, :], PS[:, 2 * (g % 2) + i % 2, :], ACT.Copy).then_inc(bank_free[2 * (g % 2) + i % 2], 1)
                act.wait_ge(bank_free[2 * (g % 2) + i % 2], g // 2 + 1)
                mark(A(square, stage[:, i % 2, :], ACT.Square), s_qkst)

            for i in range(8):
                if i >= 1:
                    act.wait_ge(s_qkss, i)
                qk_stage(i)
                act.wait_ge(s_qkss, i + 1)
                mark(A(hstat[:, 1, :], hstat[:, 0, :], ACT.Sqrt, bias=const[:, 0:1], scale=1.0 / P), s_qkrt)
            copy_banks("v", lambda c, b: nat[:, b, c * 512:(c + 1) * 512])
            for c in range(2):
                g = FIRST["z"] + c
                for b in range(NB):
                    act.wait_ge(bank_done, done(g, b))
                    A(nat[:, b, 1024 + c * 512:1536 + c * 512], PS[:, 2 * (g % 2) + b, :], ACT.Silu
                      ).then_inc(bank_free[2 * (g % 2) + b], 1)
            act.wait_ge(s_xpad, 1)
            for c in range(3):
                g = FIRST["xbc"] + c
                for u in range(2):
                    act.wait_ge(bank_done, done(g, u))
                    ch = 4 * c + 2 * u
                    A(xpad[:, ch:ch + 2, 3:], PS[:, 2 * (g % 2) + u, :].rearrange("p (h t) -> p h t", h=2), ACT.Copy
                      ).then_inc(bank_free[2 * (g % 2) + u], 1)
            act.wait_ge(s_conv, 1)
            mark(A(xbcT, xbcT, ACT.Silu), s_silu)
            act.wait_ge(s_dtst, 2)
            step(A(dts[:, 1], dts[:, 1], ACT.Exp))
            step(A(bc16[:, 1, :], bc16[:, 1, :], ACT.Exp))
            mark(A(dts[:, 2], dts[:, 1], ACT.Ln, bias=const[:, 1:2]), s_dtl)
            for t in range(2):
                act.wait_ge(s_neg, t + 1)
                step(A(sb_e, sb_e, ACT.Exp))
                mark(A(sb_e, sb_e, ACT.Ln, bias=const[:, 1:2]), s_ln)
                act.wait_ge(s_w0, t + 1)
                mark(A(sb_l, sb_l, ACT.Exp), s_w1)
                act.wait_ge(s_O, t + 1)
                mark(A(nat[:, :, 512 * t:512 * t + 512], PS[:, 4:6, :], ACT.Copy), s_att)
            act.wait_ge(s_xsps, 1)
            mark(A(xs_nat, PS[:, 4:8, :].rearrange("p (b c) n -> p b (c n)", b=2), ACT.Copy), s_xs)
            act.wait_ge(s_xsps, 2)
            mark(A(b_nat, PS[:, 4, 0:256], ACT.Copy), s_xs)
            for b in range(NB):
                act.wait_ge(s_seg, b + 1)
                mark(A(decay[:, b], decay[:, b], ACT.Exp), s_dec)
                act.wait_ge(s_edgein, b + 1)
                mark(A(ds_out[:, 2 + b, :], ds_out[:, b, :], ACT.Exp), s_edge)
            act.wait_ge(s_stps, 1)
            mark(A(states, PS[:, 4:6, :].rearrange("p c n -> p (c n)"), ACT.Copy), s_st)
            act.wait_ge(s_y, 3)
            mark(A(root[:, 4:6], ssq[:, 10:12], ACT.Sqrt, bias=const[:, 0:1], scale=1.0 / 1024), s_root)
            mark(A(root[:, 6:10], ssq[:, 6:10], ACT.Sqrt, bias=const[:, 0:1], scale=1.0 / 512), s_root)
            act.wait_ge(s_y, 2)
            act.dma_start(keys_nat, a["peer_sub_keys"][0].rearrange("h c k d -> k (h c) d")).then_inc(s_keys, 16)
            act.wait_ge(s_res, 1)
            norm_stats(2)
            act.wait_ge(s_ktps, 1)
            mark(A(keysT, PS[:, 4:8, :].rearrange("p c (s k) -> p (c s) k", k=P), ACT.Copy), s_kt)
            for c in range(4):
                g = FIRST["query"] + c
                for u in range(2):
                    act.wait_ge(bank_done, done(g, u))
                    s = 4 * c + 2 * u
                    A(queryT[:, s:s + 2, :], PS[:, 2 * (g % 2) + u, :].rearrange("p (h t) -> p h t", h=2), ACT.Copy
                      ).then_inc(bank_free[2 * (g % 2) + u], 1)
            for b in range(NB):
                act.wait_ge(s_scps, b + 1)
                mark(A(scores[b], PS[:, 4:8, :].rearrange("p c (s k) -> p (c s) k", k=P), ACT.Copy), s_psc)
            for b in range(NB):
                act.wait_ge(s_gin, b + 1)
                mark(A(best, best, ACT.Exp), s_gex)
            act.wait_ge(s_angle, 1)
            mark(A(sine[:], ang[:, 2], ACT.Sin), s_trig)
            mark(A(cosine[:], ang[:, 3], ACT.Sin, scale=-1.0, bias=const[:, 2:3]), s_trig)
            for b in range(NB):
                with act.Fori(0, PH // 2) as j:
                    def copy_mod(m):
                        act.wait_ge(s_modu, j * 12 + (48 * b + 4 * m + 6))
                        A(mod_row[:, m * 512:(m + 1) * 512], PS[0:1, m, :], ACT.Copy).then_inc(s_mode, 1)

                    act.wait_ge(s_modst, j * 16 + 64 * b)
                    for e in range(2):
                        H = j * 2 + (PH * b + e)
                        act.wait_ge(s_down, H * 16 + 16)
                        A(gelu[:, e, :], dots[:, e, :], ACT.Gelu).then_inc(s_gelu, 1)
                        act.wait_ge(s_wt, H + 1)
                        for k in range(16):
                            act.wait_ge(s_up, H * 16 + (8 * (b + 1) + k - 3))
                            A(diag[:, k % 4, :], ident[:], ACT.Copy, scale=weight[:, e, k:k + 1]).then_inc(s_diag, 1)
                        copy_mod(e)
                    copy_mod(2)
                    act.wait_ge(s_mode, j * 3 + (12 * b + 6))
                    act.dma_start(mod_raw[b:b + 1, bass.ds(j * 1536, 1536)], mod_row).then_inc(s_modst, 16)
                act.wait_ge(s_up, UPS * (b + 1))
                mark(A(xres[:, b, :], PS[:, 4:8, :].rearrange("p c n -> p (c n)"), ACT.Copy), s_resu)
            act.wait_ge(s_modst, 128)
            act.dma_start(mod_rows[:, 0, :], mod_raw.rearrange("l (c p) -> (l c) p", p=P)).then_inc(s_modr, 16)
            act.dma_start(mod_rows[:, 1, :], a["mod_b_2"].rearrange("l (c p) -> (l c) p", p=P)).then_inc(s_modr, 16)
            act.dma_start(w_small, a["attn_w_in_2"][0, :, 9216:9296].rearrange("(k p) n -> p k n", p=P)).then_inc(s_wsmall, 16)
            act.wait_ge(s_modf, 1)
            act.dma_start(mod_full.rearrange("l (c p) -> (l c) p", p=P), mod_rows[:, 0, :]).then_inc(s_modr, 16)
            act.wait_ge(s_modr, 48)
            act.dma_start(wide[:], spread(mod_full[0:1, 4096:], D)).then_inc(s_wide, 16)
            act.wait_ge(s_resu, 2)
            norm_stats(3)
            for c in range(4):
                g = FIRST["pv"] + c
                for u in range(2):
                    act.wait_ge(bank_done, done(g, u))
                    s = 4 * c + 2 * u
                    A(poolT[:, s:s + 2, :], PS[:, 2 * (g % 2) + u, :].rearrange("p (h t) -> p h t", h=2), ACT.Copy
                      ).then_inc(bank_free[2 * (g % 2) + u], 1)
            for c in range(4):
                g = FIRST["pg"] + c
                for u in range(2):
                    act.wait_ge(bank_done, done(g, u))
                    s = 4 * c + 2 * u
                    A(pgateT[:, s:s + 2, :], PS[:, 2 * (g % 2) + u, :].rearrange("p (h t) -> p h t", h=2), ACT.Silu
                      ).then_inc(bank_free[2 * (g % 2) + u], 1)
            act.wait_ge(s_res, 9)
            norm_stats(4)
            def rope_stage(i, g):
                act.wait_ge(bank_done, done(g, i % 2))
                if i >= 2:
                    act.wait_ge(s_rtp, i - 1)
                A(stage[:, i % 2, :], PS[:, 2 * (g % 2) + i % 2, :], ACT.Copy).then_inc(bank_free[2 * (g % 2) + i % 2], 1)

            def rope_T(i):
                act.wait_ge(s_rtp, i + 1)
                b, c = i % 2, i // 2
                dst = (qT_b if c < 4 else kT_b)[:, 4 * (c % 4):4 * (c % 4) + 4, b * P:(b + 1) * P] if i < 16 else \
                    qiT[:, 4 * (c - 8):4 * (c - 8) + 4, b * P:(b + 1) * P]
                mark(A(dst, PS[:, 4 + i % 2, :].rearrange("p (h t) -> p h t", h=4), ACT.Copy), s_rT)

            for i in range(16):
                rope_stage(i, FIRST["aq"] + i // 2)
                if i >= 1:
                    rope_T(i - 1)
            copy_banks("av", lambda c, b: nat[:, b, c * 512:(c + 1) * 512])
            rope_T(15)
            for c in range(4):
                g = FIRST["ag"] + c
                for u in range(2):
                    act.wait_ge(bank_done, done(g, u))
                    s = 4 * c + 2 * u
                    A(agateT[:, s:s + 2, :], PS[:, 2 * (g % 2) + u, :].rearrange("p (h t) -> p h t", h=2), ACT.Silu
                      ).then_inc(bank_free[2 * (g % 2) + u], 1)
            for i in range(16, 20):
                rope_stage(i, FIRST["ai"] + (i - 16) // 2)
                if i > 16:
                    rope_T(i - 1)
            act.wait_ge(s_kips, 1)
            mark(A(ki_wi[:, :, 0:64], PS[:, 6, 0:160].rearrange("p (b n) -> p b n", b=2)[:, :, 0:64], ACT.Copy), s_kist)
            mark(A(ki_wi[:, :, 128:144], PS[:, 6, 0:160].rearrange("p (b n) -> p b n", b=2)[:, :, 64:80], ACT.Copy,
                   scale=float(IH ** -0.5 * 64 ** -0.5)), s_kist)
            rope_T(19)
            act.wait_ge(s_kitp, 1)
            mark(A(kiT, PS[:, 7, 0:T], ACT.Copy), s_kiT)
            for i in range(2 * IH):
                S = P * (i // IH + 1)
                act.wait_ge(s_ips, i + 1)
                if i >= 2:
                    act.wait_ge(s_iuse, i - 1)
                mark(A(relu[:, i % 2, 0:S], PS[:, 4 + i % 4, 0:S], ACT.Relu), s_relu)
            act.wait_ge(s_relu, 2 * IH)
            act.dma_start(wide[:], spread(mod_full[1:2, 4096:], D)).then_inc(s_wide, 16)

            def exps(h):
                e = h % 2
                for b in range(NB):
                    act.wait_ge(s_lm, 2 * h + b + 1)
                    if h >= 2 and b == 0:
                        act.wait_ge(s_ptps, h - 1)
                    s = slice(0, P) if b == 0 else slice(P, 384)
                    mark(A(pr[:, e, s], lm[:, e, s], ACT.Exp, bias=smax[:, e, b:b + 1], accum_out=ssum[:, e, b:b + 1]), s_pe)

            def probs_T(h):
                act.wait_ge(s_ptps, h + 1)
                if h >= 2:
                    act.wait_ge(s_ops, h - 1)
                mark(A(prT[:, h % 2, :], PS[:, 6, 0:384], ACT.Copy), s_pT)

            for h in range(NH + 1):
                if h < NH:
                    exps(h)
                if h >= 1:
                    probs_T(h - 1)
            act.wait_ge(s_lps, NH)
            act.dma_start(final_gain, spread(a["final_g_2"], D)).then_inc(s_fin, 16)
            act.wait_ge(s_res, 17)
            norm_stats(5)

        @block.vector
        def _(dve):
            step, mark = counted(dve, s_dve)
            v = nc.vector
            TT, TS, STT = v.tensor_tensor, v.tensor_scalar, v.scalar_tensor_tensor

            dve.wait_ge(s_colps, 1)
            mark(v.tensor_copy(cols_a[:], PS[:, 4, 0:A_ROWS]), s_cols)
            dve.wait_ge(s_modu, 2)
            mark(v.tensor_copy(cols_b[:], PS[:, 5, 0:B_ROWS]), s_cols)
            dve.wait_ge(s_cols, 2)

            def norm_rows(r):
                dve.wait_ge(s_root, ROOTS[r])
                step(v.reciprocal(rinv[:, 0:2], root[:, 0:2]))
                for b in range(NB):
                    if r == 2:
                        dve.wait_ge(s_wide, 16)
                        mark(STT(out=nat[:, b, :], in0=xres[:, b, :], scalar=rinv[:, b:b + 1], in1=wide[:],
                                 op0=ALU.mult, op1=ALU.mult), s_nat)
                    else:
                        mark(TS(nat[:, b, :], xres[:, b, :], rinv[:, b:b + 1], None, ALU.mult), s_nat)

            def take_T(r, gain):
                for t in range(8):
                    b, c = t // 4, t % 4
                    dve.wait_ge(s_tp, 8 * r + t + 1)
                    dst = actT[:, 4 * c:4 * c + 4, b * P:(b + 1) * P]
                    src = PS[:, 4 + t % 4, :].rearrange("p (c t) -> p c t", c=4)
                    if gain is None:
                        mark(v.tensor_copy(dst, src), s_xt)
                    else:
                        mark(TT(dst, src, gain[:, 4 * c:4 * c + 4].unsqueeze(2).to_broadcast([P, 4, P]), ALU.mult), s_xt)

            norm_rows(0)
            take_T(0, cols_a[:, A_NORM:A_NORM + 16])

            def qk_T(i):
                g, b = i // 2, i % 2
                dve.wait_ge(s_qktp, i + 1)
                dst = (qT_a if g < 2 else kT_a)[:, 4 * (g % 2):4 * (g % 2) + 4, b * P:(b + 1) * P]
                col = A_Q if g < 2 else A_K
                mark(TS(dst, PS[:, 4 + i % 2, :].rearrange("p (h t) -> p h t", h=4), cols_a[:, col:col + 1], None,
                        ALU.mult), s_qkT)

            for i in range(8):
                dve.wait_ge(s_qkst, i + 1)
                mark(v.tensor_reduce(hstat[:, 0, :], square.rearrange("p (h n) -> p h n", h=4), AX, ALU.add), s_qkss)
                dve.wait_ge(s_qkrt, i + 1)
                step(v.reciprocal(hstat[:, 2, :], hstat[:, 1, :]))
                st = stage[:, i % 2, :].rearrange("p (h n) -> p h n", h=4)
                mark(TT(st, st, hstat[:, 2, :].unsqueeze(2).to_broadcast([P, 4, P]), ALU.mult), s_qkn)
                if i >= 1:
                    qk_T(i - 1)
            qk_T(7)
            mark(v.memset(xpad[:, :, 0:3], 0.0), s_xpad)
            dve.wait_ge(s_xpad, 1)
            for c in range(XC):
                g = FIRST["xbc"] + c // 4
                if c % 2 == 0:
                    dve.wait_ge(bank_free[2 * (g % 2) + (c // 2) % 2], g // 2 + 1)

                def w(i):
                    return cols_a[:, A_CW + XC * i + c:A_CW + XC * i + c + 1]
                step(TS(xbcT[:, c, :], xpad[:, c, 3:], w(3), cols_a[:, A_CB + c:A_CB + c + 1], ALU.mult, ALU.add))
                for i in (2, 1, 0):
                    ins = STT(out=xbcT[:, c, :], in0=xpad[:, c, i:i + T], scalar=w(i), in1=xbcT[:, c, :],
                              op0=ALU.mult, op1=ALU.add)
                    if i == 0 and c == XC - 1:
                        mark(ins, s_conv)
                    else:
                        step(ins)
            dve.wait_ge(s_dtps, 1)
            dve.wait_ge(s_bc, 64)
            mark(TT(dts[:, 0], PS[:, 6, 0:32].rearrange("p (b h) -> p b h", b=2),
                    bc16[:, 0, :].unsqueeze(1).to_broadcast([P, 2, 16]), ALU.add), s_dtst)
            dve.wait_ge(s_dtst, 1)
            mark(STT(out=dts[:, 1], in0=dts[:, 0], scalar=-1.0, in1=dts[:, 0], op0=ALU.mult, op1=ALU.min), s_dtst)
            dve.wait_ge(s_dtl, 1)
            step(STT(out=dts[:, 2], in0=dts[:, 0], scalar=0.0, in1=dts[:, 2], op0=ALU.max, op1=ALU.add))
            mark(STT(out=dts[:, 3], in0=dts[:, 2], scalar=-1.0, in1=bc16[:, 1, :].unsqueeze(1).to_broadcast([P, 2, 16]),
                     op0=ALU.mult, op1=ALU.mult), s_dt)
            mask4 = sb_mask[:].unsqueeze(1).to_broadcast([P, 4, 384])
            for t in range(2):
                dve.wait_ge(s_L, t + 1)
                L = PS[:, 4:8, 0:384]
                step(TS(sb_l, L, float(P ** -0.5), None, ALU.mult))
                mark(STT(out=sb_e, in0=sb_l, scalar=-1.0, in1=sb_l, op0=ALU.mult, op1=ALU.min), s_neg)
                dve.wait_ge(s_ln, t + 1)
                step(STT(out=sb_sp, in0=sb_l, scalar=0.0, in1=sb_e, op0=ALU.max, op1=ALU.add))
                mark(TT(sb_sp, sb_sp, mask4, ALU.mult), s_sp)
                step(STT(out=sb_l, in0=sb_l, scalar=0.0, in1=sb_e, op0=ALU.min, op1=ALU.subtract))
                dve.wait_ge(s_S, t + 1)
                mark(TT(sb_l, sb_l, L, ALU.subtract), s_w0)
                dve.wait_ge(s_w1, t + 1)
                mark(TT(sb_l, sb_l, mask4, ALU.mult), s_w)
            dve.wait_ge(s_acsps, 1)
            mark(v.tensor_copy(dts[:, 4], PS[:, 5, 0:32].rearrange("p (b h) -> p b h", b=2)), s_acs)
            dve.wait_ge(s_cbps, 1)
            mark(TT(cb_mask.rearrange("p b g l -> p (b g) l"), PS[:, 6, :].rearrange("p (c l) -> p c l", c=4),
                    prefix_ones[:].unsqueeze(1).to_broadcast([P, 4, P]), ALU.mult), s_cb)
            dve.wait_ge(s_acs, 1)
            dve.wait_ge(s_xs, 1)
            mark(TT(x_dt.rearrange("p b (h n) -> p (b h) n", n=64), xs_nat.rearrange("p b (h n) -> p (b h) n", n=64),
                    dts[:, 2].rearrange("p b h -> p (b h)").unsqueeze(2).to_broadcast([P, 32, 64]), ALU.mult), s_xf)
            for b in range(NB):
                dve.wait_ge(s_R, b + 1)
                R = PS[:, 4:8, :].rearrange("p c (h l) -> p (c h) l", l=P)
                step(TT(decay[:, b], R, dts[:, 4, b, :].unsqueeze(2).to_broadcast([P, 16, P]), ALU.subtract))
                mark(TS(decay[:, b], decay[:, b], 0.0, None, ALU.min), s_seg)
                if b == 0:
                    mark(TT(ds_out[:, 0, :], R[:, :, P - 1:P].rearrange("p h o -> p (h o)"), dts[:, 4, 0, :], ALU.subtract), s_edgein)
                else:
                    mark(v.tensor_copy(ds_out[:, 1, :], dts[:, 4, 1, :]), s_edgein)
                if b == 0:
                    dve.wait_ge(s_edge, 1)
                    dve.wait_ge(s_xf, 1)
                    mark(TT(x_end.rearrange("p (h n) -> p h n", n=64), x_dt[:, 0, :].rearrange("p (h n) -> p h n", n=64),
                            ds_out[:, 2, :].unsqueeze(2).to_broadcast([P, 16, 64]), ALU.mult), s_xf)
                dve.wait_ge(s_dec, b + 1)
                dve.wait_ge(s_cb, 1)
                d4 = decay[:, b].rearrange("p (g h) l -> p g h l", g=2)
                mark(TT(d4, d4, cb_mask[:, b].unsqueeze(2).to_broadcast([P, 2, 8, P]), ALU.mult), s_sc)
            copied(dve, "z")
            skip = bc16[:, 2, :].unsqueeze(2).to_broadcast([P, 16, 64])
            for b in range(NB):
                z = nat[:, b, 1024:2048]
                step(TT(y_skip.rearrange("p (h n) -> p h n", n=64), xs_nat[:, b, :].rearrange("p (h n) -> p h n", n=64),
                        skip, ALU.mult))
                dve.wait_ge(s_yd, b + 1)
                bank = 6 if b == 0 else 0
                step(TT(y_skip, y_skip, PS[:, bank:bank + 2, :].rearrange("p c n -> p (c n)"), ALU.add))
                if b == 1:
                    dve.wait_ge(s_yo, 1)
                    dve.wait_ge(s_edge, 2)
                    step(TT(y_tmp.rearrange("p (h n) -> p h n", n=64), PS[:, 2:4, :].rearrange("p c (h n) -> p (c h) n", n=64),
                            ds_out[:, 3, :].unsqueeze(2).to_broadcast([P, 16, 64]), ALU.mult))
                    step(TT(y_skip, y_skip, y_tmp, ALU.add))
                step(TT(z, z, y_skip, ALU.mult), s_y)
            dve.wait_ge(s_att, 2)
            rows4 = nat[:, :, :].rearrange("p b (g n) -> p (b g) n", g=4)
            sq = big[:, 0:4096].rearrange("p (b n) -> p b n", b=8)
            step(TT(sq, rows4, rows4, ALU.mult))
            step(v.tensor_reduce(ds_out[:, 0, 0:8], sq, AX, ALU.add))
            ss = ds_out[:, 0, 0:8].rearrange("p (b g) -> p b g", b=2)
            step(v.tensor_copy(ssq[:, 6:10].rearrange("p (b g) -> p b g", b=2), ss[:, :, 2:4]))
            step(TT(ssq[:, 10:12], ss[:, :, 0], ss[:, :, 1], ALU.add), s_y)
            dve.wait_ge(s_root, ROOTS[1])
            step(v.reciprocal(rinv[:, 4:10], root[:, 4:10]))
            for b in range(NB):
                step(TS(nat[:, b, 0:1024], nat[:, b, 0:1024], rinv[:, 4 + b:5 + b], None, ALU.mult))
                mark(TT(nat[:, b, 1024:2048].rearrange("p (g n) -> p g n", g=2), nat[:, b, 1024:2048].rearrange("p (g n) -> p g n", g=2),
                        rinv[:, 6 + 2 * b:8 + 2 * b].unsqueeze(2).to_broadcast([P, 2, 512]), ALU.mult), s_nat)
            take_T(1, cols_a[:, A_MIX:A_MIX + 16])

            def add_plain(name, s):
                for c in range(4):
                    g = FIRST[name] + c
                    for b in range(NB):
                        dve.wait_ge(bank_done, done(g, b))
                        x = xres[:, b, c * 512:(c + 1) * 512]
                        TT(x, x, PS[:, 2 * (g % 2) + b, :], ALU.add).then_inc(bank_free[2 * (g % 2) + b], 1)
                copied(dve, name)
                mark(v.memset(junk[:, 1:2], 0.0), s)

            add_plain("mix", s_res)
            norm_rows(2)
            take_T(2, None)

            i16 = iota_f[:].unsqueeze(1).unsqueeze(1).to_broadcast([P, PH, 16, 16])
            for b in range(NB):
                sc = scores[b]
                dve.wait_ge(s_psc, b + 1)
                for s in range(16):
                    step(v.max(top_s[:, s, 0:8], sc[:, s, :]))
                    step(v.max_index(top_u[:, s, 0:8], top_s[:, s, 0:8], sc[:, s, :]))
                    step(v.match_replace(sc[:, s, :], top_s[:, s, 0:8], sc[:, s, :], TAKEN))
                    step(v.max(top_s[:, s, 8:16], sc[:, s, :]))
                    step(v.max_index(top_u[:, s, 8:16], top_s[:, s, 8:16], sc[:, s, :]))
                step(v.tensor_copy(top_f, top_u))
                ts = top_s.rearrange("p (h c) k -> p h c k", c=2)
                tf = top_f.rearrange("p (h c) k -> p h c k", c=2)
                c4 = cand.rearrange("p h (i j) -> p h i j", i=16)
                step(TT(c4, ts[:, :, 0, :].unsqueeze(3).to_broadcast([P, PH, 16, 16]),
                        ts[:, :, 1, :].unsqueeze(2).to_broadcast([P, PH, 16, 16]), ALU.add))
                for h in range(PH):
                    step(v.max(best[:, h, 0:8], cand[:, h, :]))
                    step(v.max_index(pos_u[:, h, 0:8], best[:, h, 0:8], cand[:, h, :]))
                    step(v.match_replace(cand[:, h, :], best[:, h, 0:8], cand[:, h, :], TAKEN))
                    step(v.max(best[:, h, 8:16], cand[:, h, :]))
                    step(v.max_index(pos_u[:, h, 8:16], best[:, h, 8:16], cand[:, h, :]))
                step(TS(pos_12[:, 0], pos_u, 4, None, ALU.logical_shift_right))
                step(TS(pos_12[:, 1], pos_u, 15, None, ALU.bitwise_and))
                step(v.tensor_copy(pos_12f, pos_12[:]))
                hot = cand.rearrange("p h (i j) -> p h i j", i=16)
                for c in range(2):
                    step(TT(hot, pos_12f[:, c].unsqueeze(3).to_broadcast([P, PH, 16, 16]), i16, ALU.is_equal))
                    step(TT(hot, hot, tf[:, :, c, :].unsqueeze(2).to_broadcast([P, PH, 16, 16]), ALU.mult))
                    step(v.tensor_reduce(half_id[:, c], hot, AX, ALU.add))
                step(STT(out=expert[:, b, :].rearrange("p (h k) -> p h k", h=PH), in0=half_id[:, 0], scalar=float(NK),
                         in1=half_id[:, 1], op0=ALU.mult, op1=ALU.add))
                step(v.tensor_copy(gsum[:, 0, :], best[:, :, 0]))
                mark(TT(best, best, gsum[:, 0, :].unsqueeze(2).to_broadcast([P, PH, 16]), ALU.subtract), s_gin)
                dve.wait_ge(s_gex, b + 1)
                step(v.tensor_reduce(gsum[:, 0, :], best, AX, ALU.add))
                step(v.reciprocal(gsum[:, 1, :], gsum[:, 0, :]))
                mark(TT(gates[:, b, :].rearrange("p (h k) -> p h k", h=PH), best,
                        gsum[:, 1, :].unsqueeze(2).to_broadcast([P, PH, 16]), ALU.mult), s_route)
                dve.wait_ge(s_route, b + 1)
            step(v.tensor_copy(pos_f[:], pos_i[:]))
            step(TT(ang[:, 0], pos_f[:].unsqueeze(2).to_broadcast([P, 2, 16]),
                    inv_freq[:].unsqueeze(1).to_broadcast([P, 2, 16]), ALU.mult))
            step(TS(ang[:, 1], ang[:, 0], float(1 / (2 * np.pi)), None, ALU.mult))
            step(v.tensor_copy(ang_i[:], ang[:, 1]))
            step(v.tensor_copy(ang[:, 1], ang_i[:]))
            step(STT(out=ang[:, 0], in0=ang[:, 1], scalar=-TWO_PI_HI, in1=ang[:, 0], op0=ALU.mult, op1=ALU.add))
            step(STT(out=ang[:, 0], in0=ang[:, 1], scalar=-TWO_PI_LO, in1=ang[:, 0], op0=ALU.mult, op1=ALU.add))
            for bound, op, turn_by in ((PI, ALU.is_gt, -2 * np.pi), (-PI, ALU.is_lt, 2 * np.pi)):
                step(TS(ang[:, 1], ang[:, 0], bound, float(turn_by), op, ALU.mult))
                step(TT(ang[:, 0], ang[:, 0], ang[:, 1], ALU.add))
            step(TS(ang[:, 2], ang[:, 0], PI, -PI, ALU.min, ALU.max))
            step(STT(out=ang[:, 3], in0=ang[:, 2], scalar=-1.0, in1=ang[:, 2], op0=ALU.mult, op1=ALU.max), s_angle)

            for b in range(NB):
                with dve.Fori(0, PH // 2) as j:
                    for e in range(2):
                        H = j * 2 + (PH * b + e)
                        for k in range(16):
                            dve.wait_ge(landed[k % 8], H * 64 + 16 * (1 + k // 8))
                            row = gather_buf[:, k % 8, :]
                            v.tensor_tensor_reduce(out=row, in0=row, in1=nat[:, b, :], scale=1.0, scalar=0.0,
                                                   op0=ALU.mult, op1=ALU.add, accum_out=dots[:, e, k:k + 1]
                                                   ).then_inc(s_down, 1)
                        dve.wait_ge(s_gelu, H + 1)
                        TT(weight[:, e, :], gelu[:, e, :], gates[:, b, bass.ds((j * 2 + e) * 16, 16)],
                           ALU.mult).then_inc(s_wt, 1)

            dve.wait_ge(s_modr, 32)
            step(TT(mod_rows[:, 0, :], mod_rows[:, 0, :], mod_rows[:, 1, :], ALU.add), s_modf)
            dve.wait_ge(s_modps, 1)
            step(v.tensor_copy(mod_cols[:], PS[:, 3, 0:96]))
            mc = mod_cols[:].rearrange("p (l c) -> p l c", l=2)
            mark(STT(out=mod_gain[:], in0=mc[:, :, 16:32], scalar=1.0,
                     in1=cols_b[:, B_NORM:B_NORM + 32].rearrange("p (l c) -> p l c", l=2), op0=ALU.add, op1=ALU.mult), s_modc)
            dve.wait_ge(s_modc, 1)

            def shift(layer):
                dve.wait_ge(s_xt, 8 * (4 + layer))
                mark(TT(actT[:], actT[:], mc[:, layer, 0:16].unsqueeze(2).to_broadcast([P, KC, T]), ALU.add), s_shift)

            norm_rows(3)
            take_T(3, mod_gain[:, 0, :])
            shift(0)
            dve.wait_ge(s_cnt, 4)
            step(v.tensor_copy(counts, counts.bitcast(I32)))
            for w, width in enumerate(WINDOWS):
                step(TS(counts[:, w, :], counts[:, w, :], float(width), None, ALU.min))
            step(v.reciprocal(counts, counts))
            for gi, width in enumerate(WINDOWS):
                g = FIRST["pv"] + gi
                for u in range(2):
                    dve.wait_ge(bank_free[2 * (g % 2) + u], g // 2 + 1)
                cur = poolT[:, 4 * gi:4 * gi + 4, :]
                own, by, i = cur, 1, 0
                while by < width:
                    nxt = sums[i % 2]
                    step(v.tensor_copy(nxt[:, :, 0:by], cur[:, :, 0:by]))
                    step(TT(nxt[:, :, by:], cur[:, :, by:], cur[:, :, 0:T - by], ALU.add))
                    cur, by, i = nxt, 2 * by, i + 1
                step(TT(cur, cur, counts[:, gi, :].unsqueeze(1).to_broadcast([P, 4, T]), ALU.mult))
                step(TT(own, cur, own, ALU.subtract), s_pool_T)
            for i in range(4):
                g = FIRST["grp"] + i
                for u in range(2):
                    dve.wait_ge(bank_done, done(g, u))
                    if i == 0 and u == 0:
                        copied(dve, "pg")
                    for o in range(2):
                        c = 4 * i + 2 * u + o
                        ins = STT(out=pgateT[:, c, :], in0=PS[:, 2 * (g % 2) + u, o * T:(o + 1) * T],
                                  scalar=cols_b[:, B_SCALE + c:B_SCALE + c + 1], in1=pgateT[:, c, :],
                                  op0=ALU.mult, op1=ALU.mult)
                        if o:
                            ins.then_inc(bank_free[2 * (g % 2) + u], 1)
                        else:
                            mark(ins, s_dve)

            def add_gated(name, layer):
                dve.wait_ge(s_wide, 32 + 16 * layer)
                for c in range(4):
                    g = FIRST[name] + c
                    for b in range(NB):
                        dve.wait_ge(bank_done, done(g, b))
                        bank = PS[:, 2 * (g % 2) + b, :]
                        cs = slice(c * 512, (c + 1) * 512)
                        TT(stage[:, b, :], bank, wide[:, cs], ALU.mult).then_inc(bank_free[2 * (g % 2) + b], 1)
                        dve.wait_ge(bank_free[2 * (g % 2) + b], g // 2 + 1)
                        step(TT(xres[:, b, cs], xres[:, b, cs], stage[:, b, :], ALU.add), s_res)

            add_gated("po", 0)
            norm_rows(4)
            take_T(4, mod_gain[:, 1, :])
            shift(1)

            def rotate(x, heads, half, cs, sn, last_sem):
                x1, x2 = x[:, :, 0:half], x[:, :, half:2 * half]
                cs, sn = [t.unsqueeze(1).to_broadcast([P, heads, half]) for t in (cs, sn)]
                t = [rope_t[:, i, 0:heads * half].rearrange("p (h n) -> p h n", h=heads) for i in range(4)]
                mark(TT(t[0], x1, cs, ALU.mult), s_dve)
                mark(TT(t[1], x2, sn, ALU.mult), s_dve)
                mark(TT(t[2], x2, cs, ALU.mult), s_dve)
                step(TT(t[3], x1, sn, ALU.mult))
                step(TT(x1, t[0], t[1], ALU.subtract))
                step(TT(x2, t[2], t[3], ALU.add), last_sem)

            dve.wait_ge(s_trig, 2)
            for i in range(20):
                g = FIRST["aq"] + i // 2 if i < 16 else FIRST["ai"] + (i - 16) // 2
                b = i % 2
                dve.wait_ge(bank_free[2 * (g % 2) + b], g // 2 + 1)
                if i < 16:
                    rotate(stage[:, b, :].rearrange("p (h n) -> p h n", h=4), 4, 16, cosine[:, b, :], sine[:, b, :], s_rope)
                else:
                    rotate(stage[:, b, :].rearrange("p (h n) -> p h n", h=8), 8, 8,
                           cosine[:, b, 0:16:2], sine[:, b, 0:16:2], s_rope)
            dve.wait_ge(s_kist, 2)
            for b in range(NB):
                rotate(ki_wi[:, b:b + 1, 0:64], 1, 8, cosine[:, b, 0:16:2], sine[:, b, 0:16:2], s_dve)
            step(v.tensor_copy(ki_wi[:, :, 64:128], ki_wi[:, :, 0:64]), s_kirope)
            for i in range(2 * IH):
                b, h = i // IH, i % IH
                S = P * (b + 1)
                dve.wait_ge(s_relu, i + 1)
                w = ki_wi[:, b, 128 + h:129 + h]
                if h == 0:
                    ins = TS(iscore[:, b, 0:S], relu[:, i % 2, 0:S], w, None, ALU.mult)
                else:
                    ins = STT(out=iscore[:, b, 0:S], in0=relu[:, i % 2, 0:S], scalar=w, in1=iscore[:, b, 0:S],
                              op0=ALU.mult, op1=ALU.add)
                step(ins, s_iuse)
                if h == IH - 1:
                    mark(v.memset(junk[:, 3:4], 0.0), s_iacc)
            for b in range(NB):
                S = P * (b + 1)
                dve.wait_ge(s_iadm, b + 1)
                src = iscore[:, b, 0:S]
                for r in range(SELECT // 8):
                    step(v.max(best8[:], src))
                    step(v.match_replace(iwork[:, 0:S], best8[:], src, TAKEN))
                    src = iwork[:, 0:S]
                o = sel_bias[:, 0:P] if b == 0 else sel_bias[:, P:]
                step(TT(o, iwork[:, 0:S], iscore[:, b, 0:S], ALU.is_equal))
                mark(TS(o, o, MASKED, None, ALU.mult), s_sel)
            dve.wait_ge(s_causal, 2)

            def masked(h):
                e = h % 2
                dve.wait_ge(s_lps, h + 1)
                if h >= 2:
                    dve.wait_ge(s_pe, 2 * (h - 1))
                for b in range(NB):
                    s = slice(0, P) if b == 0 else slice(P, 384)
                    step(v.tensor_tensor_reduce(out=lm[:, e, s], in0=PS[:, 4 + e, s], in1=sel_bias[:, s],
                                                scale=float(P ** -0.5), scalar=-3.0e38, op0=ALU.add, op1=ALU.max,
                                                accum_out=smax[:, e, b:b + 1]))
                    mark(TS(smax[:, e, b:b + 1], smax[:, e, b:b + 1], -1.0, None, ALU.mult), s_lm)

            def normed(h):
                e = h % 2
                dve.wait_ge(s_pe, 2 * h + 2)
                step(v.reciprocal(ssum[:, e, 2:4], ssum[:, e, 0:2]))
                step(TS(pr[:, e, 0:P], pr[:, e, 0:P], ssum[:, e, 2:3], None, ALU.mult))
                mark(TS(pr[:, e, P:384], pr[:, e, P:384], ssum[:, e, 3:4], None, ALU.mult), s_pn)

            def gated(h):
                dve.wait_ge(s_ops, h + 1)
                mark(TT(agateT[:, h, :], PS[:, 7, 0:T], agateT[:, h, :], ALU.mult), s_oT)

            copied(dve, "ag")
            for h in range(NH + 2):
                if h < NH:
                    masked(h)
                if 1 <= h <= NH:
                    normed(h - 1)
                if h >= 2:
                    gated(h - 2)
            add_gated("ao", 1)
            dve.wait_ge(s_fin, 16)
            dve.wait_ge(s_root, ROOTS[5])
            step(v.reciprocal(rinv[:, 0:2], root[:, 0:2]))
            for b in range(NB):
                step(STT(out=nat[:, b, :], in0=xres[:, b, :], scalar=rinv[:, b:b + 1], in1=final_gain,
                         op0=ALU.mult, op1=ALU.mult), s_y)


_OUT = ("out_0_dram", (1, T, D))


def kernel(**inputs):
    import numpy as _np
    import concourse.bacc as _bacc
    from concourse import mybir as _mybir
    from concourse.bass_utils import run_bass_kernel_spmd as _run

    nc = _bacc.Bacc("TRN2", target_bir_lowering=False, num_devices=1)
    arrays, args = {}, {}
    for name, value in inputs.items():
        value = _np.ascontiguousarray(value)
        if value.ndim == 1:
            value = value.reshape(1, -1)
        arrays[f"in_{name}_dram"] = value
        args[name] = nc.dram_tensor(f"in_{name}_dram", value.shape, _mybir.dt.from_np(value.dtype),
                                    kind="ExternalInput").ap()
    out = nc.dram_tensor(_OUT[0], _OUT[1], _mybir.dt.float32, kind="ExternalOutput").ap()
    mod_raw = nc.dram_tensor("mod_raw", (2, 3 * D), _mybir.dt.float32, kind="Internal").ap()
    mod_full = nc.dram_tensor("mod_full", (2, 3 * D), _mybir.dt.float32, kind="Internal").ap()
    program(nc, args, out, mod_raw, mod_full)
    r = _run(nc, [arrays], core_ids=[0])
    return r.results[0][_OUT[0]]
```

```python
from contextlib import ExitStack

import concourse.bass as bass
from concourse import mybir
import numpy as np

F32 = mybir.dt.float32
I32 = mybir.dt.int32
U32 = mybir.dt.uint32
ALU = mybir.AluOpType
ACT = mybir.ActivationFunctionType
AX = mybir.AxisListType.X

P = 128
D = 2048
NB = 2
T = NB * P
KC = D // P
EPS = 1e-6
UPS = 8 + 16 * 8
SLOTS = 5
UNIT = 4096
SBH, SSH = 8, 16
XC = 12
PH, NK, TOPK = 8, 128, 16
NH, IH = 16, 16
ROUTE_STEPS = 27
BEFORE_MAX = (1, 2, 3, 4, 5, 6, 7, 8, 9, 10, 13, 14, 15, 16, 17)
SELECT = 64
WINDOWS = (2, 4, 8, 16)
NEG = -3.0e38
TAKEN = -3.3e38
MASKED = -1.0e30
TWO_PI_HI = 6.28125
TWO_PI_LO = float(np.float32(2 * np.pi - 6.28125))
PI = 3.1415925
INV_FREQ = [float(v) for v in (np.float32(500000.0) ** (-np.arange(16, dtype=np.float32) * np.float32(2.0) / np.float32(32)))]

A_NORM, A_MIX, A_Q, A_K, A_CB, A_CW, A_ROWS = 0, 16, 32, 33, 34, 46, 94
B_NORM, B_SCALE, B_COND, B_ROWS = 0, 32, 48, 64

STAGES = [
    ("q", "w_in", 0, 2, "N"), ("k", "w_in", 1024, 2, "N"), ("v", "w_in", 2048, 2, "N"),
    ("z", "w_in", 3072, 2, "N"), ("xbc", "w_in", 4096, 3, "T"), ("mix", "w_out", 0, 4, "N"),
    ("query", "peer_query", 0, 4, "T"),
    ("pv", "pool_w_in", 0, 4, "T"), ("pg", "pool_w_in", 2048, 4, "T"), ("grp", "pool_w_grp", 0, 4, "G"),
    ("po", "pool_w_out", 0, 4, "N"),
    ("aq", "attn_w_in", 0, 4, "N"), ("ak", "attn_w_in", 2048, 4, "N"), ("av", "attn_w_in", 4096, 4, "N"),
    ("ag", "attn_w_in", 6144, 4, "T"), ("ai", "attn_w_in", 8192, 2, "N"), ("ao", "attn_w_out", 0, 4, "N"),
]


MOD_AFTER = {"q": (1, 1), "k": (1, 1), "v": (2, 2), "z": (2, 1), "xbc": (2, 1, 0), "mix": (1, 2, 2, 1),
             "query": (1, 2, 1, 0), "pv": (2, 2, 2, 2), "pg": (2, 2, 2, 2), "po": (2, 2, 2, 2)}
MOD_BUFS = 4


def plan():
    first, units, halves, g, mods = {}, [], 0, 0, 0
    for name, weight, col, n, kind in STAGES:
        first[name] = g
        for c in range(n):
            if kind == "N":
                halves += 1
                units.append((g, kind, weight, col + 512 * c, 0, ("half", halves)))
                units.append((g, kind, weight, col + 512 * c, 1, ("bank", 2 * g + 2)))
            elif kind == "T":
                for u in range(2):
                    units.append((g, kind, weight, col + 512 * c + 256 * u, u, ("bank", 2 * g + u + 1)))
            elif c % 2 == 0:
                units.append((g, kind, weight, 0, c, ("bank", 2 * (g + 1) + 2)))
            for _ in range(MOD_AFTER[name][c] if name in MOD_AFTER else 0):
                units.append((g, "M", "mod_w_2", mods, 0, ("mod", mods + 1)))
                mods += 1
            g += 1
    assert mods == 48
    return first, units


FIRST, UNITS = plan()
UNITS_OF = {}
MODS_OF = {}
for _n, _u in enumerate(UNITS):
    (MODS_OF if _u[1] == "M" else UNITS_OF).setdefault(_u[0], []).append(_n)
N_BEFORE = sum(1 for u in UNITS if u[0] < FIRST["pv"])


ROOTS = {0: 1, 1: 3, 2: 4, 3: 5, 4: 6, 5: 7}
ROW_NORMS = (0, 2, 3, 4, 5)


def mods_until(g):
    return sum(len(v) for k, v in MODS_OF.items() if k <= g)


def done(g, i):
    return 2 * g + i + 1


def program(nc, a, out, gate_dram):
    with ExitStack() as ctx:
        def sb(name, shape, dt=F32):
            return ctx.enter_context(nc.sbuf_tensor(name, shape, dt))

        def sem(name):
            return ctx.enter_context(nc.semaphore(name))

        ring = sb("ring", [P, SLOTS, UNIT])
        xres = sb("xres", [P, NB, D])
        nat = sb("nat", [P, NB, D])
        actT = sb("actT", [P, KC, T])
        big = sb("big", [P, 12288])
        wide = sb("wide", [P, D])
        stage = sb("stage", [P, 2, 512])
        work = sb("work", [P, 1792])
        ident = sb("ident", [P, P])
        later_ones = sb("later_ones", [P, P])
        prefix_ones = sb("prefix_ones", [P, P])
        ones = sb("ones", [P, P])
        sb_mask = sb("sb_mask", [P, 384])
        rows_a = sb("rows_a", [A_ROWS, P])
        rows_b = sb("rows_b", [B_ROWS, P])
        cols_a = sb("cols_a", [P, A_ROWS])
        cols_b = sb("cols_b", [P, B_ROWS])
        rows_c = sb("rows_c", [96, P])
        cols_c = sb("cols_c", [P, 96])
        cond = sb("cond", [P, KC])
        const = sb("const", [P, 4])
        iota_i = sb("iota_i", [P, 16], I32)
        iota_f = sb("iota_f", [P, 16])
        inv_freq = sb("inv_freq", [P, 16])
        pos_i = sb("pos_i", [P, NB], I32)
        pos_f = sb("pos_f", [P, NB])
        cosine = sb("cosine", [P, NB, 16])
        sine = sb("sine", [P, NB, 16])
        ang = sb("ang", [P, 4, NB, 16])
        ang_i = sb("ang_i", [P, NB, 16], I32)
        bc16 = sb("bc16", [P, 3, 16])
        ssq = sb("ssq", [P, 16])
        root = sb("root", [P, 16])
        rinv = sb("rinv", [P, 16])
        hstat = sb("hstat", [P, 3, 4])
        dts = sb("dts", [P, 6, NB, 16])
        ds_out = sb("ds_out", [P, 4, 16])
        expert_next = sb("expert_next", [P, 16], I32)
        gates = sb("gates", [P, 2, 16])
        gsum = sb("gsum", [P, 4])
        expert_now = sb("expert_now", [P, 2, 16], I32)
        dots = sb("dots", [P, 2, 16])
        gelu = sb("gelu", [P, 2, 16])
        weight = sb("weight", [P, 2, 16])
        mod_cols = sb("mod_cols", [P, 96])
        mod_gain = sb("mod_gain", [P, 2, KC])
        ki_wi = sb("ki_wi", [P, NB, 144])
        best8 = sb("best8", [P, 8])
        smax = sb("smax", [P, 2, 3])
        ssum = sb("ssum", [P, 2, 4])
        junk = sb("junk", [P, 4])
        PS = ctx.enter_context(nc.psum_tensor("PS", [P, 8, 512], F32))

        act_flat = actT[:, :, :].rearrange("p k t -> p (k t)")
        gather_buf = ring[:, :, :].rearrange("p s (h d) -> p (s h) d", h=2)
        qT_a = big[:, 0:2048].rearrange("p (h t) -> p h t", h=SBH)
        kT_a = big[:, 2048:4096].rearrange("p (h t) -> p h t", h=SBH)
        xbcT = big[:, 4096:7168].rearrange("p (c t) -> p c t", c=XC)
        scr = big[:, 7168:12288]
        xpad = scr[:, 0:XC * 259].rearrange("p (c t) -> p c t", c=XC)
        square = scr[:, 3200:3712]
        sb_l, sb_e, sb_sp = [scr[:, 1536 * i:1536 * (i + 1)].rearrange("p (h t) -> p h t", h=4) for i in range(3)]
        xs_nat = scr[:, 0:2048].rearrange("p (b n) -> p b n", b=NB)
        x_dt = scr[:, 2048:4096].rearrange("p (b n) -> p b n", b=NB)
        x_end = scr[:, 4096:5120]
        decay = big[:, 0:4096].rearrange("p (b h l) -> p b h l", b=NB, h=SSH)
        b_nat = act_flat[:, 0:256]
        cb_mask = act_flat[:, 256:768].rearrange("p (b g l) -> p b g l", b=NB, g=2)
        states = act_flat[:, 768:1792]
        y_tmp = act_flat[:, 1792:2816]
        y_skip = act_flat[:, 2816:3840]
        queryT = big[:, 0:4096].rearrange("p (s t) -> p s t", s=16)
        keys_nat = big[:, 4096:6144].rearrange("p (s k) -> p s k", s=16)
        keysT = big[:, 6144:8192].rearrange("p (s k) -> p s k", s=16)
        scores = big[:, 8192:12288].rearrange("p (s k) -> p s k", s=32)
        poolT = big[:, 0:4096].rearrange("p (c t) -> p c t", c=KC)
        pgateT = big[:, 4096:8192].rearrange("p (c t) -> p c t", c=KC)
        sums = [big[:, 8192 + 1024 * i:9216 + 1024 * i].rearrange("p (c t) -> p c t", c=4) for i in range(2)]
        counts = big[:, 10240:11264].rearrange("p (w t) -> p w t", w=4)
        qT_b = poolT
        kT_b = pgateT
        agateT = big[:, 8192:12288].rearrange("p (c t) -> p c t", c=NH)
        qiT = wide[:, :].rearrange("p (h t) -> p h t", h=8)
        w_dt = work[:, 0:256].rearrange("p (k n) -> p k n", k=KC)
        mod_acc = work[:, 256:1280].rearrange("p (i n) -> p i n", i=MOD_BUFS)
        sc_now = work[:, 0:256].rearrange("p (c k) -> p c k", c=2)
        cand = work[:, 256:512]
        top_s = work[:, 512:544].rearrange("p (c k) -> p c k", c=2)
        top_u = work[:, 544:576].bitcast(U32).rearrange("p (c k) -> p c k", c=2)
        top_f = work[:, 576:608].rearrange("p (c k) -> p c k", c=2)
        best = work[:, 608:624]
        pos_u = work[:, 624:640].bitcast(U32)
        pos_12 = work[:, 640:672].bitcast(U32).rearrange("p (c k) -> p c k", c=2)
        pos_12f = work[:, 672:704].rearrange("p (c k) -> p c k", c=2)
        half_id = work[:, 704:736].rearrange("p (c k) -> p c k", c=2)
        hot = work[:, 736:992].rearrange("p (k i) -> p k i", k=16)
        w_small = work[:, 0:1280].rearrange("p (k n) -> p k n", k=KC)
        rope_t = work[:, 1280:1792].rearrange("p (i n) -> p i n", i=4)
        diag = stage[:, 0, :].rearrange("p (i n) -> p i n", i=4)
        gate_rows = stage[0:16, 1, 0:P]
        kiT = sb_mask[:, 0:T]
        final_gain = big[:, 0:D]
        lm = act_flat[:, 0:768].rearrange("p (e s) -> p e s", e=2)
        pr = act_flat[:, 768:1536].rearrange("p (e s) -> p e s", e=2)
        prT = act_flat[:, 1536:2304].rearrange("p (e s) -> p e s", e=2)
        relu = act_flat[:, 2304:2816].rearrange("p (e s) -> p e s", e=2)
        iscore = act_flat[:, 2816:3328].rearrange("p (b s) -> p b s", b=NB)
        iwork = act_flat[:, 3328:3584]
        sel_bias = act_flat[:, 3584:3968]

        s_in = sem("x_loaded")
        s_rows = sem("rows_loaded")
        s_bc = sem("spread_rows_loaded")
        s_wdt = sem("w_dt_loaded")
        s_wsmall = sem("w_small_loaded")
        s_keys = sem("keys_loaded")
        s_wide = sem("wide_loaded")
        s_gateps = sem("gate_rows_psum")
        s_grow = sem("gate_rows_copied")
        s_gst = sem("gate_rows_stored")
        s_out = sem("out_stored")
        s_fin = sem("final_gain_loaded")
        s_issue = sem("gathers_issued")
        s_rstep = sem("routing_step")
        s_rcarry = sem("routing_waits_carried")
        s_gnorm = sem("gate_norm_step")
        s_now = sem("experts_of_head")
        s_cnt = sem("window_counts")
        s_causal = sem("selection_causal")
        s_xpad = sem("conv_padded")
        s_resu = sem("residual_with_experts")
        s_iuse = sem("index_relu_used")
        unit_in = [sem(f"unit_in_slot{i}") for i in range(SLOTS)]
        half_used = sem("half_used")
        bank_done = sem("gemm_bank_done")
        bank_free = [sem(f"gemm_bank_free{i}") for i in range(4)]
        s_const = sem("constants_ready")
        s_pool = sem("pool_step")
        s_dve = sem("dve_step")
        s_act = sem("act_step")
        s_colps = sem("columns_in_psum")
        s_cols = sem("columns_ready")
        s_ssq = sem("square_sums")
        s_root = sem("roots")
        s_nat = sem("normed_rows")
        s_tp = sem("transposes_done")
        s_xt = sem("activations_T")
        s_shift = sem("shifted_T")
        s_qkst = sem("qk_staged")
        s_qkrt = sem("qk_roots")
        s_qkss = sem("qk_square_sums")
        s_qkn = sem("qk_normed")
        s_qktp = sem("qk_transposed")
        s_qkT = sem("qk_T_ready")
        s_xraw = sem("conv_input")
        s_conv = sem("conv_done")
        s_silu = sem("conv_silu")
        s_dtps = sem("dt_in_psum")
        s_dtst = sem("dt_rows")
        s_dtl = sem("dt_log")
        s_dt = sem("dt_ready")
        s_L = sem("sb_logits")
        s_neg = sem("sb_neg_abs")
        s_ln = sem("sb_log1p")
        s_sp = sem("sb_softplus")
        s_S = sem("sb_later")
        s_w0 = sem("sb_exponent")
        s_w1 = sem("sb_exp")
        s_w = sem("sb_weights")
        s_O = sem("sb_out_psum")
        s_att = sem("sb_out")
        s_xsps = sem("xs_transposed")
        s_xs = sem("xs_natural")
        s_acsps = sem("cumulated_psum")
        s_acs = sem("cumulated")
        s_R = sem("cumulated_rows")
        s_seg = sem("segments")
        s_dec = sem("decay")
        s_edge = sem("edge_decays")
        s_edgein = sem("edge_decay_inputs")
        s_cbps = sem("cb_psum")
        s_cb = sem("cb_masked")
        s_sc = sem("ssd_scores")
        s_xf = sem("ssd_x")
        s_yd = sem("y_diag")
        s_stps = sem("states_psum")
        s_st = sem("states")
        s_yo = sem("y_off")
        s_y = sem("y_rows")
        s_res = sem("residual_ready")
        s_ktps = sem("keys_transposed")
        s_kt = sem("keys_T")
        s_scps = sem("peer_scores_psum")
        s_psc = sem("peer_scores")
        s_gin = sem("gate_exponents")
        s_gex = sem("gate_exps")
        s_route = sem("routing_ready")
        landed = [sem(f"gathered_buf{i}") for i in range(8)]
        s_down = sem("down_used")
        s_up = sem("up_used")
        s_gelu = sem("gelu_ready")
        s_wt = sem("expert_weights")
        s_diag = sem("diagonals")
        s_modw = sem("mod_unit_weighed")
        s_msum = sem("mod_unit_summed")
        s_mcol = sem("mod_cols_copied")
        s_cond = sem("condition_ready")
        s_modc = sem("mod_cols_ready")
        s_pool_T = sem("pooled_T")
        s_angle = sem("angles")
        s_trig = sem("sines")
        s_rst = sem("rope_staged")
        s_rope = sem("roped")
        s_rtp = sem("rope_transposed")
        s_rT = sem("qkT_ready")
        s_kips = sem("ki_psum")
        s_kist = sem("ki_staged")
        s_kirope = sem("ki_roped")
        s_kitp = sem("ki_transposed")
        s_kiT = sem("kiT_ready")
        s_ips = sem("index_psum")
        s_relu = sem("index_relu")
        s_iacc = sem("index_sum")
        s_iadm = sem("index_admissible")
        s_sel = sem("selection")
        s_lps = sem("logits_psum")
        s_lm = sem("logits_masked")
        s_pe = sem("probs_exp")
        s_pn = sem("probs_normed")
        s_ptps = sem("probs_transposed")
        s_pT = sem("probs_T")
        s_ops = sem("attn_out_psum")
        s_oT = sem("attn_out_T")

        def spread(src, n):
            return bass.AP(tensor=src.tensor, offset=src.offset, ap=[[0, P], [1, n]])

        def counted(eng, default):
            counts = {}

            def step(ins, s=default, by=1):
                counts[s.name] = counts.get(s.name, 0) + by
                ins.then_inc(s, by)
                eng.wait_ge(s, counts[s.name])

            def mark(ins, s, by=1):
                counts[s.name] = counts.get(s.name, 0) + by
                ins.then_inc(s, by)
            return step, mark

        def copied(eng, name, chunks=2):
            n = next(x[3] for x in STAGES if x[0] == name)
            for g in range(FIRST[name] + n - chunks, FIRST[name] + n):
                for i in range(2):
                    eng.wait_ge(bank_free[2 * (g % 2) + i], g // 2 + 1)

        block = ctx.enter_context(nc.Block())

        @block.sync
        def _(sp):
            weights = {k: a[k] for k in ("w_in", "w_out", "peer_query")}
            weights["pool_w_in"], weights["pool_w_out"] = a["pool_w_in_2"], a["pool_w_out_2"]
            weights["attn_w_in"], weights["attn_w_out"] = a["attn_w_in_2"], a["attn_w_out_2"]
            for b in range(NB):
                sp.dma_start(xres[:, b, :], a["x"][0, b * P:(b + 1) * P, :]).then_inc(s_in, 16)

            def load(n):
                _, kind, w, col, part, _ = UNITS[n]
                slot = ring[:, n % SLOTS, :]
                if kind == "N":
                    src = weights[w][0, part * 1024:(part + 1) * 1024, col:col + 512]
                    dst = slot.rearrange("p (k n) -> p k n", k=8)
                    src = src.rearrange("(k p) n -> p k n", p=P)
                elif kind == "M":
                    src = a[w][col // 24, :, 256 * (col % 24):256 * (col % 24) + 256].rearrange("(k p) n -> p k n", p=P)
                    dst = slot.rearrange("p (k n) -> p k n", k=KC)
                elif kind == "T":
                    src = weights[w][0, :, col:col + 256].rearrange("(k p) n -> p k n", p=P)
                    dst = slot.rearrange("p (k n) -> p k n", k=KC)
                else:
                    src = a["pool_w_grp_2"][0, part:part + 2].rearrange("g (k p) n -> p (g k) n", p=P)
                    dst = slot.rearrange("p (k n) -> p k n", k=8)
                sp.dma_start(dst, src).then_inc(unit_in[n % SLOTS], 16)

            used = {"half": half_used, "bank": bank_done, "mod": s_modw}

            for n in range(N_BEFORE):
                if n >= SLOTS:
                    what, value = UNITS[n - SLOTS][5]
                    sp.wait_ge(used[what], value)
                load(n)
            sp.wait_ge(s_up, UPS * NB)
            for n in range(N_BEFORE, len(UNITS)):
                if n >= N_BEFORE + SLOTS:
                    what, value = UNITS[n - SLOTS][5]
                    sp.wait_ge(used[what], value)
                load(n)
            for b in range(NB):
                sp.wait_ge(s_y, 4 + b)
                sp.dma_start(out[0, b * P:(b + 1) * P, :], nat[:, b, :]).then_inc(s_out, 16)
            sp.wait_ge(s_out, 16 * NB)

        @block.gpsimd
        def _(pool):
            step, mark = counted(pool, s_pool)
            g = nc.gpsimd
            step(g.memset(ident[:], 0.0))
            step(g.affine_select(out=ident[:], in_=ident[:], compare_op=ALU.not_equal, fill=1.0, base=0,
                                 pattern=[[-1, P]], channel_multiplier=1))
            step(g.memset(ones[:], 1.0))
            step(g.affine_select(out=later_ones[:], in_=ones[:], compare_op=ALU.is_gt, fill=0.0, base=0,
                                 pattern=[[-1, P]], channel_multiplier=1))
            step(g.affine_select(out=prefix_ones[:], in_=ones[:], compare_op=ALU.is_ge, fill=0.0, base=0,
                                 pattern=[[1, P]], channel_multiplier=-1))
            for i in (0, 2):
                step(g.affine_select(out=sb_mask[:, i * P:(i + 1) * P], in_=ones[:], compare_op=ALU.is_gt,
                                     fill=0.0, base=0, pattern=[[1, P]], channel_multiplier=-1))
            step(g.memset(sb_mask[:, P:2 * P], 1.0))
            for i, v in enumerate((EPS, 1.0, float(np.pi / 2), 0.0)):
                step(g.memset(const[:, i:i + 1], v))
            for i, v in enumerate(INV_FREQ):
                step(g.memset(inv_freq[:, i:i + 1], v))
            step(g.iota(iota_i[:], pattern=[[1, 16]], base=0, channel_multiplier=0))
            mark(g.tensor_copy(iota_f[:], iota_i[:]), s_const)

            tables = [a[k].rearrange("a e d -> (a e) d") for k in ("peer_down", "peer_up")]
            pool.wait_ge(bank_done, done(FIRST["pv"] - 1, 1))
            for b in range(NB):
                with pool.Fori(0, PH // 2) as j:
                    for e in range(2):
                        H = j * 2 + (PH * b + e)
                        pool.wait_ge(s_route, H + 1)
                        pool.sem_inc(s_issue, 1)
                        g.tensor_copy(expert_now[:, e, :], expert_next[:]).then_inc(s_now, 1)
                        pool.wait_ge(s_now, H + 1)
                        for s in range(32):
                            buf = s % 8
                            if s < 8:
                                pool.wait_ge(s_up, H * 16 + (8 * b + buf + 1))
                            elif s < 24:
                                pool.wait_ge(s_down, H * 16 + (s - 8 + 1))
                            else:
                                pool.wait_ge(s_up, H * 16 + (8 * (b + 1) + buf + 1))
                            pool.sem_inc(s_issue, 1)
                            k = s % 16
                            g.indirect_dma_start(out=gather_buf[:, buf, :], out_offset=None, in_=tables[s // 16],
                                                 in_offset=bass.IndirectOffsetOnAxis(ap=expert_now[:, e, k:k + 1], axis=0)
                                                 ).then_inc(landed[buf], 16)

            for w, width in enumerate(WINDOWS):
                g.iota(counts[:, w, :].bitcast(I32), pattern=[[1, T]], base=1, channel_multiplier=0).then_inc(s_cnt, 1)
            for b in range(NB):
                S = P * (b + 1)
                pool.wait_ge(s_iacc, 1 + b)
                g.affine_select(out=iscore[:, b, 0:S], in_=iscore[:, b, 0:S], compare_op=ALU.is_ge, fill=NEG,
                                base=P * b, pattern=[[-1, S]], channel_multiplier=1).then_inc(s_iadm, 1)
                pool.wait_ge(s_sel, 1 + b)
                o = sel_bias[:, 0:P] if b == 0 else sel_bias[:, P:]
                g.affine_select(out=o, in_=o, compare_op=ALU.is_ge, fill=MASKED,
                                base=P * b, pattern=[[-1, S]], channel_multiplier=1).then_inc(s_causal, 1)

        @block.tensor
        def _(pe):
            mm, tr = nc.tensor.matmul, nc.tensor.transpose

            def banks_free(g):
                if g >= 2:
                    for i in range(2):
                        pe.wait_ge(bank_free[2 * (g % 2) + i], g // 2)

            def arrived(n):
                pe.wait_ge(unit_in[n % SLOTS], 16 * (n // SLOTS + 1))

            summed = [0]

            def mod_sums(g, bank):
                for i in range(summed[0], mods_until(g)):
                    pe.wait_ge(s_modw, i + 1)
                    for h in range(2):
                        last = mm(PS[:, bank, 2 * (i % MOD_BUFS) + h:2 * (i % MOD_BUFS) + h + 1],
                                  mod_acc[:, i % MOD_BUFS, h * P:(h + 1) * P], ones[:, 0:1], start=True, stop=True)
                    last.then_inc(s_msum, 1)
                summed[0] = max(summed[0], mods_until(g))

            def gate_turn(layer, bank):
                pe.wait_ge(s_modc, layer + 1)
                tr(PS[0:16, bank, 0:P], mod_cols[:, 48 * layer + 32:48 * layer + 48], ident[:]).then_inc(s_gateps, 1)
                pe.wait_ge(s_grow, layer + 1)

            def gemm(name, lhs, before=None):
                n_chunks, kind = next((n, k) for m, _, _, n, k in STAGES if m == name)
                for g in range(FIRST[name], FIRST[name] + n_chunks):
                    if before is not None:
                        before(g - FIRST[name])
                    banks_free(g)
                    bank = 2 * (g % 2)
                    mod_sums(g - 2, bank + 1)
                    for part, n in enumerate(UNITS_OF[g]):
                        arrived(n)
                        slot = ring[:, n % SLOTS, :]
                        if kind == "N":
                            w = slot.rearrange("p (k n) -> p k n", k=8)
                            for b in range(NB):
                                if b == 1 and part == 0:
                                    pe.wait_ge(s_mcol, summed[0])
                                for k in range(8):
                                    last = mm(PS[:, bank + b, :], lhs[:, 8 * part + k, b * P:(b + 1) * P], w[:, k, :],
                                              start=(part == 0 and k == 0), stop=(part == 1 and k == 7))
                                if part == 1:
                                    last.then_inc(bank_done, 1)
                            if part == 0:
                                last.then_inc(half_used, 1)
                        else:
                            w = slot.rearrange("p (k n) -> p k n", k=KC)
                            if part == 1:
                                pe.wait_ge(s_mcol, summed[0])
                            for h in range(2):
                                for k in range(KC):
                                    last = mm(PS[:, bank + part, h * T:(h + 1) * T], w[:, k, h * P:(h + 1) * P],
                                              lhs[:, k, :], start=(k == 0), stop=(k == KC - 1))
                            last.then_inc(bank_done, 1)

            def turn(r):
                for t in range(8):
                    b, c = t // 4, t % 4
                    pe.wait_ge(s_nat, 2 * r + b + 1)
                    if t >= 4:
                        pe.wait_ge(s_xt, 8 * r + t - 3)
                    for i in range(4):
                        ch = 4 * c + i
                        last = tr(PS[:, 4 + t % 4, i * P:(i + 1) * P], nat[:, b, ch * P:(ch + 1) * P], ident[:])
                    last.then_inc(s_tp, 1)

            pe.wait_ge(s_const, 1)
            pe.wait_ge(s_rows, 16 * 11)
            tr(PS[:, 4, 0:A_ROWS], rows_a[:], ident[0:A_ROWS, 0:A_ROWS]).then_inc(s_colps, 1)
            tr(PS[:, 5, 0:B_ROWS], rows_b[:], ident[0:B_ROWS, 0:B_ROWS]).then_inc(s_colps, 1)
            tr(PS[:, 6, 0:96], rows_c[:], ident[0:96, 0:96]).then_inc(s_colps, 1)
            pe.wait_ge(s_cols, 3)
            turn(0)
            pe.wait_ge(s_xt, 8)

            def turn_qk(i):
                pe.wait_ge(s_qkn, i + 1)
                if i >= 2:
                    pe.wait_ge(s_qkT, i - 1)
                for h in range(4):
                    last = tr(PS[:, 4 + i % 2, h * P:(h + 1) * P], stage[:, i % 2, h * P:(h + 1) * P], ident[:])
                last.then_inc(s_qktp, 1)

            def turns(one, c):
                if c >= 2:
                    one(2 * c - 4)
                    one(2 * c - 3)

            gemm("q", actT)
            gemm("k", actT, lambda c: turns(turn_qk, c + 2))
            gemm("v", actT, lambda c: turns(turn_qk, c + 4))
            gemm("z", actT)
            gemm("xbc", actT)
            pe.wait_ge(s_wdt, 16)
            for b in range(NB):
                for k in range(KC):
                    last = mm(PS[:, 6, 16 * b:16 * b + 16], actT[:, k, b * P:(b + 1) * P], w_dt[:, k, :],
                              start=(k == 0), stop=(k == KC - 1))
            last.then_inc(s_dtps, 1)

            vnat = nat[:, :, 0:1024]
            for t in range(2):
                if t == 0:
                    pe.wait_ge(s_qkT, 8)
                    pe.wait_ge(s_dtst, 1)
                    copied(pe, "v")
                else:
                    pe.wait_ge(s_att, 1)
                for i in range(4):
                    h = 4 * t + i
                    mm(PS[:, 4 + i, 0:T], kT_a[:, h, 0:P], qT_a[:, h, :], start=True, stop=True)
                    last = mm(PS[:, 4 + i, T:384], kT_a[:, h, P:T], qT_a[:, h, P:T], start=True, stop=True)
                last.then_inc(s_L, 1)
                pe.wait_ge(s_sp, t + 1)
                for i in range(4):
                    mm(PS[:, 4 + i, 0:384], later_ones[:], sb_sp[:, i, :], start=True, stop=True)
                    last = mm(PS[:, 4 + i, P:T], ones[:], sb_sp[:, i, T:384], start=False, stop=True,
                              skip_group_check=True)
                last.then_inc(s_S, 1)
                pe.wait_ge(s_w, t + 1)
                for i in range(4):
                    h = 4 * t + i
                    hp = slice(i * P, (i + 1) * P)
                    v = slice(h * P, (h + 1) * P)
                    mm(PS[:, 4, hp], sb_l[:, i, 0:P], vnat[:, 0, v], start=True, stop=True)
                    mm(PS[:, 5, hp], sb_l[:, i, P:T], vnat[:, 0, v], start=True, stop=False)
                    last = mm(PS[:, 5, hp], sb_l[:, i, T:384], vnat[:, 1, v], start=False, stop=True)
                last.then_inc(s_O, 1)

            pe.wait_ge(s_att, 2)
            pe.wait_ge(s_silu, 1)
            for b in range(NB):
                for c in range(8):
                    last = tr(PS[:, 4 + 2 * b + c // 4, (c % 4) * P:(c % 4 + 1) * P],
                              xbcT[:, c, b * P:(b + 1) * P], ident[:])
            last.then_inc(s_xsps, 1)
            pe.wait_ge(s_xs, 1)
            for g in range(2):
                last = tr(PS[:, 4, g * P:(g + 1) * P], xbcT[:, 8 + g, 0:P], ident[:])
            last.then_inc(s_xsps, 1)
            pe.wait_ge(s_dt, 1)
            for b in range(NB):
                last = mm(PS[:, 5, 16 * b:16 * b + 16], prefix_ones[:], dts[:, 3, b, :], start=True, stop=True)
            last.then_inc(s_acsps, 1)
            for b in range(NB):
                for g in range(2):
                    last = mm(PS[:, 6, (2 * b + g) * P:(2 * b + g + 1) * P], xbcT[:, 8 + g, b * P:(b + 1) * P],
                              xbcT[:, 10 + g, b * P:(b + 1) * P], start=True, stop=True)
            last.then_inc(s_cbps, 1)
            pe.wait_ge(s_acs, 1)
            pe.wait_ge(s_cb, 1)
            pe.wait_ge(s_xs, 2)
            for b in range(NB):
                if b:
                    pe.wait_ge(s_edgein, 1)
                for h in range(SSH):
                    last = mm(PS[:, 4 + h // 4, (h % 4) * P:(h % 4 + 1) * P],
                              dts[:, 3, b, h:h + 1].to_broadcast([P, P]), prefix_ones[:], start=True, stop=True)
                last.then_inc(s_R, 1)
            pe.wait_ge(s_xf, 2)
            pe.wait_ge(s_edgein, 2)
            for g in range(2):
                last = mm(PS[:, 4 + g, :], b_nat[:, g * P:(g + 1) * P], x_end[:, g * 512:(g + 1) * 512],
                          start=True, stop=True)
            last.then_inc(s_stps, 1)
            for b in range(NB):
                pe.wait_ge(s_sc, b + 1)
                if b == 1:
                    banks_free(FIRST["mix"])
                    banks_free(FIRST["mix"] + 1)
                for h in range(SSH):
                    bank = (6 if b == 0 else 0) + h // 8
                    last = mm(PS[:, bank, (h % 8) * 64:(h % 8 + 1) * 64], decay[:, b, h, :],
                              x_dt[:, b, h * 64:(h + 1) * 64], start=True, stop=True)
                last.then_inc(s_yd, 1)
            pe.wait_ge(s_st, 1)
            for g in range(2):
                last = mm(PS[:, 2 + g, :], xbcT[:, 10 + g, P:T], states[:, g * 512:(g + 1) * 512],
                          start=True, stop=True)
            last.then_inc(s_yo, 1)

            turn(1)
            pe.wait_ge(s_xt, 16)
            gemm("mix", actT)

            pe.wait_ge(s_keys, 16)
            turn(2)
            pe.wait_ge(s_xt, 24)
            for t in range(4):
                for i in range(4):
                    last = tr(PS[:, 4 + t, i * P:(i + 1) * P], keys_nat[:, 4 * t + i, :], ident[:])
            last.then_inc(s_ktps, 1)
            gemm("query", actT)
            pe.wait_ge(s_kt, 1)
            copied(pe, "query")
            for b in range(NB):
                if b:
                    pe.wait_ge(s_psc, 1)
                for s in range(16):
                    last = mm(PS[:, 4 + s // 4, (s % 4) * P:(s % 4 + 1) * P], queryT[:, s, b * P:(b + 1) * P],
                              keysT[:, s, :], start=True, stop=True)
                last.then_inc(s_scps, 1)
            pe.wait_ge(s_psc, 2)

            banks_free(FIRST["pv"])
            banks_free(FIRST["pv"] + 1)
            mod_sums(FIRST["pv"] - 1, 3)
            gate_turn(0, 2)
            for b in range(NB):
                if b:
                    pe.wait_ge(s_resu, 1)
                for n in range(4):
                    mm(PS[:, 4 + n, :], ident[:], xres[:, b, n * 512:(n + 1) * 512], start=True,
                       stop=True).then_inc(s_up, 2)
                with pe.Fori(0, PH // 2) as j:
                    for e in range(2):
                        H = j * 2 + (PH * b + e)
                        for k in range(16):
                            pe.wait_ge(s_diag, H * 16 + (k + 1))
                            pe.wait_ge(landed[k % 8], H * 64 + 16 * (3 + k // 8))
                            for n in range(4):
                                last = mm(PS[:, 4 + n, :], diag[:, k % 4, :], gather_buf[:, k % 8, n * 512:(n + 1) * 512],
                                          start=False, stop=True, skip_group_check=True)
                            last.then_inc(s_up, 1)

            turn(3)
            pe.wait_ge(s_shift, 1)
            gemm("pv", actT)
            gemm("pg", actT)
            for i in range(4):
                g = FIRST["grp"] + i
                pe.wait_ge(s_pool_T, i + 1)
                banks_free(g)
                mod_sums(g - 2, 2 * (g % 2) + 1)
                n = UNITS_OF[FIRST["grp"] + (i // 2) * 2][0]
                arrived(n)
                w = ring[:, n % SLOTS, :].rearrange("p (g k n) -> p g k n", g=2, k=4)[:, i % 2]
                for o in range(4):
                    if o == 2:
                        pe.wait_ge(s_mcol, summed[0])
                    for k in range(4):
                        last = mm(PS[:, 2 * (g % 2) + o // 2, (o % 2) * T:(o % 2 + 1) * T], w[:, k, o * P:(o + 1) * P],
                                  poolT[:, 4 * i + k, :], start=(k == 0), stop=(k == 3))
                    if o % 2:
                        last.then_inc(bank_done, 1)
            copied(pe, "grp")
            gemm("po", pgateT)
            banks_free(FIRST["aq"])
            banks_free(FIRST["aq"] + 1)
            mod_sums(FIRST["aq"] - 1, 3)
            gate_turn(1, 2)
            turn(4)
            pe.wait_ge(s_shift, 2)

            def turn_rope(i):
                pe.wait_ge(s_rope, i + 1)
                if i >= 2:
                    pe.wait_ge(s_rT, i - 1)
                for h in range(4):
                    last = tr(PS[:, 4 + i % 2, h * P:(h + 1) * P], stage[:, i % 2, h * P:(h + 1) * P], ident[:])
                last.then_inc(s_rtp, 1)

            gemm("aq", actT, lambda c: turns(turn_rope, c))
            gemm("ak", actT, lambda c: turns(turn_rope, c + 4))
            gemm("av", actT, lambda c: turns(turn_rope, c + 8) if c < 2 else None)
            gemm("ag", actT)
            gemm("ai", actT)
            pe.wait_ge(s_wsmall, 16)
            for b in range(NB):
                for k in range(KC):
                    last = mm(PS[:, 6, 80 * b:80 * b + 80], actT[:, k, b * P:(b + 1) * P], w_small[:, k, :],
                              start=(k == 0), stop=(k == KC - 1))
            last.then_inc(s_kips, 1)
            for i in range(16, 20):
                turn_rope(i)
            pe.wait_ge(s_kirope, 1)
            for b in range(NB):
                last = tr(PS[:, 7, b * P:(b + 1) * P], ki_wi[:, b, 0:P], ident[:])
            last.then_inc(s_kitp, 1)
            pe.wait_ge(s_kiT, 1)
            pe.wait_ge(s_rT, 20)
            for b in range(NB):
                for h in range(IH):
                    i = IH * b + h
                    if i >= 4:
                        pe.wait_ge(s_relu, i - 3)
                    part = slice(64 * (h % 2), 64 * (h % 2) + 64)
                    mm(PS[:, 4 + i % 4, 0:P * (b + 1)], qiT[part, h // 2, b * P:(b + 1) * P],
                       kiT[part, 0:P * (b + 1)], start=True, stop=True).then_inc(s_ips, 1)
            pe.wait_ge(s_relu, 2 * IH)
            copied(pe, "av")

            def logits(h):
                if h >= 2:
                    pe.wait_ge(s_lm, 2 * (h - 1))
                mm(PS[:, 4 + h % 2, 0:P], qT_b[:, h, 0:P], kT_b[:, h, 0:P], start=True, stop=True)
                mm(PS[:, 4 + h % 2, P:384], qT_b[:, h, P:T], kT_b[:, h, :], start=True, stop=True).then_inc(s_lps, 1)

            def values(h):
                pe.wait_ge(s_pn, h + 1)
                if h >= 1:
                    pe.wait_ge(s_pT, h)
                for i in range(3):
                    last = tr(PS[:, 6, i * P:(i + 1) * P], pr[:, h % 2, i * P:(i + 1) * P], ident[:])
                last.then_inc(s_ptps, 1)

            def outputs(h):
                pe.wait_ge(s_pT, h + 1)
                if h >= 1:
                    pe.wait_ge(s_oT, h)
                mm(PS[:, 7, 0:T], nat[:, 0, h * P:(h + 1) * P], prT[:, h % 2, 0:T], start=True, stop=True)
                mm(PS[:, 7, P:T], nat[:, 1, h * P:(h + 1) * P], prT[:, h % 2, T:384], start=False, stop=True,
                   skip_group_check=True).then_inc(s_ops, 1)

            for h in range(NH + 2):
                if h < NH:
                    logits(h)
                if 1 <= h <= NH:
                    values(h - 1)
                if h >= 2:
                    outputs(h - 2)
            pe.wait_ge(s_oT, NH)
            gemm("ao", agateT)

        @block.scalar
        def _(act):
            step, mark = counted(act, s_act)
            A = nc.scalar.activation
            for dst, src, n in (
                (rows_a[A_NORM:A_NORM + 16], a["attn_norm"], 16),
                (rows_a[A_MIX:A_MIX + 8], a["sb_out_norm"], 8),
                (rows_a[A_MIX + 8:A_MIX + 16], a["ssd_out_norm"], 8),
                (rows_a[A_Q:A_Q + 1], a["sb_q_norm"], 1),
                (rows_a[A_K:A_K + 1], a["sb_k_norm"], 1),
                (rows_a[A_CB:A_CB + 12], a["conv_b"], 12),
            ):
                act.dma_start(dst, src.rearrange("a (c p) -> (a c) p", p=P)).then_inc(s_rows, 16)
            act.dma_start(rows_a[A_CW:A_CW + 48], a["conv_w"].rearrange("a w i (c p) -> (a w i c) p", p=P)).then_inc(s_rows, 16)
            act.dma_start(rows_b[B_NORM:B_NORM + 32], a["norm_g_2"].rearrange("l (c p) -> (l c) p", p=P)).then_inc(s_rows, 16)
            act.dma_start(rows_b[B_SCALE:B_SCALE + 16], a["pool_scale_2"].rearrange("l (c p) -> (l c) p", p=P)).then_inc(s_rows, 16)
            act.dma_start(rows_b[B_COND:B_COND + 16], a["c_2"].rearrange("l (c p) -> (l c) p", p=P)).then_inc(s_rows, 16)
            act.dma_start(rows_c[:], a["mod_b_2"].rearrange("l (c p) -> (l c) p", p=P)).then_inc(s_rows, 16)
            for i, k in enumerate(("dt_bias", "a_log", "d_skip")):
                act.dma_start(bc16[:, i, :], spread(a[k], 16)).then_inc(s_bc, 16)
            act.dma_start(pos_i[:], a["positions_2"].rearrange("a (b p) -> p (a b)", p=P),
                          allow_slow_non_contiguous=True).then_inc(s_bc, 16)
            act.dma_start(w_dt, a["w_in"][0, :, 5632:5648].rearrange("(k p) n -> p k n", p=P)).then_inc(s_wdt, 16)
            act.dma_start(wide[:], spread(a["ffn_norm"], D)).then_inc(s_wide, 16)

            copied_mods = [0]

            def mod_columns(g, bank):
                if mods_until(g) > copied_mods[0]:
                    act.wait_ge(s_msum, mods_until(g))
                for i in range(copied_mods[0], mods_until(g)):
                    mark(A(mod_cols[:, 2 * i:2 * i + 2], PS[:, bank, 2 * (i % MOD_BUFS):2 * (i % MOD_BUFS) + 2], ACT.Copy), s_mcol)
                copied_mods[0] = max(copied_mods[0], mods_until(g))

            def mods(g):
                mod_columns(g - 2, 2 * (g % 2) + 1)

            def gate_row(layer):
                act.wait_ge(s_gateps, layer + 1)
                step(A(gate_rows, PS[0:16, 2, 0:P], ACT.Copy), s_grow)
                act.dma_start(gate_dram[layer:layer + 1, :].rearrange("l (c p) -> (l c) p", p=P), gate_rows).then_inc(s_gst, 16)

            def norm_stats(r):
                for b in range(NB):
                    if r == 0:
                        act.wait_ge(s_in, 16 * NB)
                    mark(A(act_flat[:, b * D:(b + 1) * D], xres[:, b, :], ACT.Square, accum_out=ssq[:, b:b + 1]), s_ssq)
                act.wait_ge(s_ssq, 2 * ROW_NORMS.index(r) + 2)
                mark(A(root[:, 0:2], ssq[:, 0:2], ACT.Sqrt, bias=const[:, 0:1], scale=1.0 / D), s_root)

            def copy_banks(name, dst):
                n = next(x[3] for x in STAGES if x[0] == name)
                for c in range(n):
                    g = FIRST[name] + c
                    mods(g)
                    for b in range(NB):
                        act.wait_ge(bank_done, done(g, b))
                        A(dst(c, b), PS[:, 2 * (g % 2) + b, :], ACT.Copy).then_inc(bank_free[2 * (g % 2) + b], 1)

            act.wait_ge(s_const, 1)
            norm_stats(0)
            act.wait_ge(s_cols, 2)
            mark(A(cond[:], cols_b[:, B_COND:B_COND + 16], ACT.Silu), s_cond)

            def qk_stage(i):
                g = FIRST["q"] + i // 2
                mods(g)
                act.wait_ge(bank_done, done(g, i % 2))
                if i >= 2:
                    act.wait_ge(s_qktp, i - 1)
                A(stage[:, i % 2, :], PS[:, 2 * (g % 2) + i % 2, :], ACT.Copy).then_inc(bank_free[2 * (g % 2) + i % 2], 1)
                act.wait_ge(bank_free[2 * (g % 2) + i % 2], g // 2 + 1)
                mark(A(square, stage[:, i % 2, :], ACT.Square), s_qkst)

            for i in range(8):
                if i >= 1:
                    act.wait_ge(s_qkss, i)
                qk_stage(i)
                act.wait_ge(s_qkss, i + 1)
                mark(A(hstat[:, 1, :], hstat[:, 0, :], ACT.Sqrt, bias=const[:, 0:1], scale=1.0 / P), s_qkrt)
            copy_banks("v", lambda c, b: nat[:, b, c * 512:(c + 1) * 512])
            for c in range(2):
                g = FIRST["z"] + c
                mods(g)
                for b in range(NB):
                    act.wait_ge(bank_done, done(g, b))
                    A(nat[:, b, 1024 + c * 512:1536 + c * 512], PS[:, 2 * (g % 2) + b, :], ACT.Silu
                      ).then_inc(bank_free[2 * (g % 2) + b], 1)
            act.wait_ge(s_xpad, 1)
            for c in range(3):
                g = FIRST["xbc"] + c
                mods(g)
                for u in range(2):
                    act.wait_ge(bank_done, done(g, u))
                    ch = 4 * c + 2 * u
                    A(xpad[:, ch:ch + 2, 3:], PS[:, 2 * (g % 2) + u, :].rearrange("p (h t) -> p h t", h=2), ACT.Copy
                      ).then_inc(bank_free[2 * (g % 2) + u], 1)
            act.wait_ge(s_conv, 1)
            mark(A(xbcT, xbcT, ACT.Silu), s_silu)
            act.wait_ge(s_dtst, 2)
            step(A(dts[:, 1], dts[:, 1], ACT.Exp))
            step(A(bc16[:, 1, :], bc16[:, 1, :], ACT.Exp))
            mark(A(dts[:, 2], dts[:, 1], ACT.Ln, bias=const[:, 1:2]), s_dtl)
            for t in range(2):
                act.wait_ge(s_neg, t + 1)
                step(A(sb_e, sb_e, ACT.Exp))
                mark(A(sb_e, sb_e, ACT.Ln, bias=const[:, 1:2]), s_ln)
                act.wait_ge(s_w0, t + 1)
                mark(A(sb_l, sb_l, ACT.Exp), s_w1)
                act.wait_ge(s_O, t + 1)
                mark(A(nat[:, :, 512 * t:512 * t + 512], PS[:, 4:6, :], ACT.Copy), s_att)
            act.wait_ge(s_xsps, 1)
            mark(A(xs_nat, PS[:, 4:8, :].rearrange("p (b c) n -> p b (c n)", b=2), ACT.Copy), s_xs)
            act.wait_ge(s_xsps, 2)
            mark(A(b_nat, PS[:, 4, 0:256], ACT.Copy), s_xs)
            for b in range(NB):
                act.wait_ge(s_seg, b + 1)
                mark(A(decay[:, b], decay[:, b], ACT.Exp), s_dec)
                act.wait_ge(s_edgein, b + 1)
                mark(A(ds_out[:, 2 + b, :], ds_out[:, b, :], ACT.Exp), s_edge)
            act.wait_ge(s_stps, 1)
            mark(A(states, PS[:, 4:6, :].rearrange("p c n -> p (c n)"), ACT.Copy), s_st)
            act.wait_ge(s_y, 3)
            mark(A(root[:, 4:6], ssq[:, 10:12], ACT.Sqrt, bias=const[:, 0:1], scale=1.0 / 1024), s_root)
            mark(A(root[:, 6:10], ssq[:, 6:10], ACT.Sqrt, bias=const[:, 0:1], scale=1.0 / 512), s_root)
            act.wait_ge(s_y, 2)
            act.dma_start(keys_nat, a["peer_sub_keys"][0].rearrange("h c k d -> k (h c) d")).then_inc(s_keys, 16)
            for c in range(4):
                mods(FIRST["mix"] + c)
            act.wait_ge(s_res, 1)
            norm_stats(2)
            act.wait_ge(s_ktps, 1)
            mark(A(keysT, PS[:, 4:8, :].rearrange("p c (s k) -> p (c s) k", k=P), ACT.Copy), s_kt)
            for c in range(4):
                g = FIRST["query"] + c
                mods(g)
                for u in range(2):
                    act.wait_ge(bank_done, done(g, u))
                    s = 4 * c + 2 * u
                    A(queryT[:, s:s + 2, :], PS[:, 2 * (g % 2) + u, :].rearrange("p (h t) -> p h t", h=2), ACT.Copy
                      ).then_inc(bank_free[2 * (g % 2) + u], 1)
            for b in range(NB):
                act.wait_ge(s_scps, b + 1)
                mark(A(scores[:, 16 * b:16 * b + 16, :], PS[:, 4:8, :].rearrange("p c (s k) -> p (c s) k", k=P), ACT.Copy), s_psc)
            mod_columns(FIRST["pv"] - 1, 3)
            gate_row(0)
            act.wait_ge(s_angle, 1)
            mark(A(sine[:], ang[:, 2], ACT.Sin), s_trig)
            mark(A(cosine[:], ang[:, 3], ACT.Sin, scale=-1.0, bias=const[:, 2:3]), s_trig)
            for b in range(NB):
                with act.Fori(0, PH // 2) as j:
                    for e in range(2):
                        H = j * 2 + (PH * b + e)
                        act.wait_ge(s_gin, H + 1)
                        A(gates[:, e, :], gates[:, e, :], ACT.Exp).then_inc(s_gex, 1)
                        act.wait_ge(s_down, H * 16 + 16)
                        A(gelu[:, e, :], dots[:, e, :], ACT.Gelu).then_inc(s_gelu, 1)
                        act.wait_ge(s_wt, H + 1)
                        for k in range(16):
                            act.wait_ge(s_up, H * 16 + (8 * (b + 1) + k - 3))
                            A(diag[:, k % 4, :], ident[:], ACT.Copy, scale=weight[:, e, k:k + 1]).then_inc(s_diag, 1)
                act.wait_ge(s_up, UPS * (b + 1))
                mark(A(xres[:, b, :], PS[:, 4:8, :].rearrange("p c n -> p (c n)"), ACT.Copy), s_resu)
            act.wait_ge(s_gst, 16)
            act.dma_start(wide[:], spread(gate_dram[0:1, :], D)).then_inc(s_wide, 16)
            act.wait_ge(s_resu, 2)
            norm_stats(3)
            for c in range(4):
                g = FIRST["pv"] + c
                mods(g)
                for u in range(2):
                    act.wait_ge(bank_done, done(g, u))
                    s = 4 * c + 2 * u
                    A(poolT[:, s:s + 2, :], PS[:, 2 * (g % 2) + u, :].rearrange("p (h t) -> p h t", h=2), ACT.Copy
                      ).then_inc(bank_free[2 * (g % 2) + u], 1)
            for c in range(4):
                g = FIRST["pg"] + c
                mods(g)
                for u in range(2):
                    act.wait_ge(bank_done, done(g, u))
                    s = 4 * c + 2 * u
                    A(pgateT[:, s:s + 2, :], PS[:, 2 * (g % 2) + u, :].rearrange("p (h t) -> p h t", h=2), ACT.Silu
                      ).then_inc(bank_free[2 * (g % 2) + u], 1)
            for name in ("grp", "po"):
                for c in range(4):
                    mods(FIRST[name] + c)
            mod_columns(FIRST["aq"] - 1, 3)
            gate_row(1)
            act.wait_ge(s_res, 9)
            norm_stats(4)
            act.dma_start(w_small, a["attn_w_in_2"][0, :, 9216:9296].rearrange("(k p) n -> p k n", p=P)).then_inc(s_wsmall, 16)
            def rope_stage(i, g):
                act.wait_ge(bank_done, done(g, i % 2))
                if i >= 2:
                    act.wait_ge(s_rtp, i - 1)
                A(stage[:, i % 2, :], PS[:, 2 * (g % 2) + i % 2, :], ACT.Copy).then_inc(bank_free[2 * (g % 2) + i % 2], 1)

            def rope_T(i):
                act.wait_ge(s_rtp, i + 1)
                b, c = i % 2, i // 2
                dst = (qT_b if c < 4 else kT_b)[:, 4 * (c % 4):4 * (c % 4) + 4, b * P:(b + 1) * P] if i < 16 else \
                    qiT[:, 4 * (c - 8):4 * (c - 8) + 4, b * P:(b + 1) * P]
                mark(A(dst, PS[:, 4 + i % 2, :].rearrange("p (h t) -> p h t", h=4), ACT.Copy), s_rT)

            act.wait_ge(s_gst, 32)
            for i in range(16):
                rope_stage(i, FIRST["aq"] + i // 2)
                if i >= 1:
                    rope_T(i - 1)
            copy_banks("av", lambda c, b: nat[:, b, c * 512:(c + 1) * 512])
            rope_T(15)
            for c in range(4):
                g = FIRST["ag"] + c
                mods(g)
                for u in range(2):
                    act.wait_ge(bank_done, done(g, u))
                    s = 4 * c + 2 * u
                    A(agateT[:, s:s + 2, :], PS[:, 2 * (g % 2) + u, :].rearrange("p (h t) -> p h t", h=2), ACT.Silu
                      ).then_inc(bank_free[2 * (g % 2) + u], 1)
            for i in range(16, 20):
                rope_stage(i, FIRST["ai"] + (i - 16) // 2)
                if i > 16:
                    rope_T(i - 1)
            act.wait_ge(s_kips, 1)
            mark(A(ki_wi[:, :, 0:64], PS[:, 6, 0:160].rearrange("p (b n) -> p b n", b=2)[:, :, 0:64], ACT.Copy), s_kist)
            mark(A(ki_wi[:, :, 128:144], PS[:, 6, 0:160].rearrange("p (b n) -> p b n", b=2)[:, :, 64:80], ACT.Copy,
                   scale=float(IH ** -0.5 * 64 ** -0.5)), s_kist)
            rope_T(19)
            act.wait_ge(s_kitp, 1)
            mark(A(kiT, PS[:, 7, 0:T], ACT.Copy), s_kiT)
            for i in range(2 * IH):
                S = P * (i // IH + 1)
                act.wait_ge(s_ips, i + 1)
                if i >= 2:
                    act.wait_ge(s_iuse, i - 1)
                mark(A(relu[:, i % 2, 0:S], PS[:, 4 + i % 4, 0:S], ACT.Relu), s_relu)
            act.wait_ge(s_relu, 2 * IH)
            act.dma_start(wide[:], spread(gate_dram[1:2, :], D)).then_inc(s_wide, 16)

            def exps(h):
                e = h % 2
                for b in range(NB):
                    act.wait_ge(s_lm, 2 * h + b + 1)
                    if h >= 2 and b == 0:
                        act.wait_ge(s_ptps, h - 1)
                    s = slice(0, P) if b == 0 else slice(P, 384)
                    mark(A(pr[:, e, s], lm[:, e, s], ACT.Exp, bias=smax[:, e, b:b + 1], accum_out=ssum[:, e, b:b + 1]), s_pe)

            def probs_T(h):
                act.wait_ge(s_ptps, h + 1)
                if h >= 2:
                    act.wait_ge(s_ops, h - 1)
                mark(A(prT[:, h % 2, :], PS[:, 6, 0:384], ACT.Copy), s_pT)

            for h in range(NH + 1):
                if h < NH:
                    exps(h)
                if h >= 1:
                    probs_T(h - 1)
            act.wait_ge(s_lps, NH)
            act.dma_start(final_gain, spread(a["final_g_2"], D)).then_inc(s_fin, 16)
            act.wait_ge(s_res, 17)
            norm_stats(5)

        @block.vector
        def _(dve):
            step, mark = counted(dve, s_dve)
            v = nc.vector
            TT, TS, STT = v.tensor_tensor, v.tensor_scalar, v.scalar_tensor_tensor

            dve.wait_ge(s_colps, 1)
            mark(v.tensor_copy(cols_a[:], PS[:, 4, 0:A_ROWS]), s_cols)
            dve.wait_ge(s_colps, 3)
            mark(v.tensor_copy(cols_b[:], PS[:, 5, 0:B_ROWS]), s_cols)
            mark(v.tensor_copy(cols_c[:], PS[:, 6, 0:96]), s_cols)
            dve.wait_ge(s_cols, 3)

            def weigh(g):
                for n in MODS_OF.get(g, []):
                    i = UNITS[n][3]
                    dve.wait_ge(s_cond, 1)
                    dve.wait_ge(unit_in[n % SLOTS], 16 * (n // SLOTS + 1))
                    if i >= MOD_BUFS:
                        dve.wait_ge(s_msum, i - MOD_BUFS + 1)
                    w, acc = ring[:, n % SLOTS, :].rearrange("p (k n) -> p k n", k=KC), mod_acc[:, i % MOD_BUFS, :]
                    step(TS(acc, w[:, 0, :], cond[:, 0:1], None, ALU.mult))
                    for k in range(1, KC):
                        ins = STT(out=acc, in0=w[:, k, :], scalar=cond[:, k:k + 1], in1=acc, op0=ALU.mult, op1=ALU.add)
                        if k < KC - 1:
                            step(ins)
                        else:
                            mark(ins, s_modw)

            def mod_ready(layer):
                dve.wait_ge(s_mcol, 24 * (layer + 1))
                cols = slice(48 * layer, 48 * layer + 48)
                step(TT(mod_cols[:, cols], mod_cols[:, cols], cols_c[:, cols], ALU.add))
                step(STT(out=mod_gain[:, layer, :], in0=mod_cols[:, 48 * layer + 16:48 * layer + 32], scalar=1.0,
                         in1=cols_b[:, B_NORM + 16 * layer:B_NORM + 16 * layer + 16], op0=ALU.add, op1=ALU.mult), s_modc)

            def norm_rows(r):
                dve.wait_ge(s_root, ROOTS[r])
                step(v.reciprocal(rinv[:, 0:2], root[:, 0:2]))
                for b in range(NB):
                    if r == 2:
                        dve.wait_ge(s_wide, 16)
                        mark(STT(out=nat[:, b, :], in0=xres[:, b, :], scalar=rinv[:, b:b + 1], in1=wide[:],
                                 op0=ALU.mult, op1=ALU.mult), s_nat)
                    else:
                        mark(TS(nat[:, b, :], xres[:, b, :], rinv[:, b:b + 1], None, ALU.mult), s_nat)

            def take_T(r, gain):
                for t in range(8):
                    b, c = t // 4, t % 4
                    dve.wait_ge(s_tp, 8 * r + t + 1)
                    dst = actT[:, 4 * c:4 * c + 4, b * P:(b + 1) * P]
                    src = PS[:, 4 + t % 4, :].rearrange("p (c t) -> p c t", c=4)
                    if gain is None:
                        mark(v.tensor_copy(dst, src), s_xt)
                    else:
                        mark(TT(dst, src, gain[:, 4 * c:4 * c + 4].unsqueeze(2).to_broadcast([P, 4, P]), ALU.mult), s_xt)

            norm_rows(0)
            take_T(0, cols_a[:, A_NORM:A_NORM + 16])

            def qk_T(i):
                g, b = i // 2, i % 2
                dve.wait_ge(s_qktp, i + 1)
                dst = (qT_a if g < 2 else kT_a)[:, 4 * (g % 2):4 * (g % 2) + 4, b * P:(b + 1) * P]
                col = A_Q if g < 2 else A_K
                mark(TS(dst, PS[:, 4 + i % 2, :].rearrange("p (h t) -> p h t", h=4), cols_a[:, col:col + 1], None,
                        ALU.mult), s_qkT)

            for i in range(8):
                dve.wait_ge(s_qkst, i + 1)
                mark(v.tensor_reduce(hstat[:, 0, :], square.rearrange("p (h n) -> p h n", h=4), AX, ALU.add), s_qkss)
                dve.wait_ge(s_qkrt, i + 1)
                step(v.reciprocal(hstat[:, 2, :], hstat[:, 1, :]))
                st = stage[:, i % 2, :].rearrange("p (h n) -> p h n", h=4)
                mark(TT(st, st, hstat[:, 2, :].unsqueeze(2).to_broadcast([P, 4, P]), ALU.mult), s_qkn)
                if i >= 1:
                    qk_T(i - 1)
                if i % 2:
                    weigh(FIRST["q"] + i // 2)
            qk_T(7)
            for name in ("v", "z"):
                for c in range(2):
                    weigh(FIRST[name] + c)
            mark(v.memset(xpad[:, :, 0:3], 0.0), s_xpad)
            dve.wait_ge(s_xpad, 1)
            for c in range(XC):
                g = FIRST["xbc"] + c // 4
                if c % 2 == 0:
                    dve.wait_ge(bank_free[2 * (g % 2) + (c // 2) % 2], g // 2 + 1)

                def w(i):
                    return cols_a[:, A_CW + XC * i + c:A_CW + XC * i + c + 1]
                step(TS(xbcT[:, c, :], xpad[:, c, 3:], w(3), cols_a[:, A_CB + c:A_CB + c + 1], ALU.mult, ALU.add))
                for i in (2, 1, 0):
                    ins = STT(out=xbcT[:, c, :], in0=xpad[:, c, i:i + T], scalar=w(i), in1=xbcT[:, c, :],
                              op0=ALU.mult, op1=ALU.add)
                    if i == 0 and c == XC - 1:
                        mark(ins, s_conv)
                    else:
                        step(ins)
                if c % 4 == 3:
                    weigh(g)
            dve.wait_ge(s_dtps, 1)
            dve.wait_ge(s_bc, 64)
            mark(TT(dts[:, 0], PS[:, 6, 0:32].rearrange("p (b h) -> p b h", b=2),
                    bc16[:, 0, :].unsqueeze(1).to_broadcast([P, 2, 16]), ALU.add), s_dtst)
            dve.wait_ge(s_dtst, 1)
            mark(STT(out=dts[:, 1], in0=dts[:, 0], scalar=-1.0, in1=dts[:, 0], op0=ALU.mult, op1=ALU.min), s_dtst)
            dve.wait_ge(s_dtl, 1)
            step(STT(out=dts[:, 2], in0=dts[:, 0], scalar=0.0, in1=dts[:, 2], op0=ALU.max, op1=ALU.add))
            mark(STT(out=dts[:, 3], in0=dts[:, 2], scalar=-1.0, in1=bc16[:, 1, :].unsqueeze(1).to_broadcast([P, 2, 16]),
                     op0=ALU.mult, op1=ALU.mult), s_dt)
            mask4 = sb_mask[:].unsqueeze(1).to_broadcast([P, 4, 384])
            for t in range(2):
                dve.wait_ge(s_L, t + 1)
                L = PS[:, 4:8, 0:384]
                step(TS(sb_l, L, float(P ** -0.5), None, ALU.mult))
                mark(STT(out=sb_e, in0=sb_l, scalar=-1.0, in1=sb_l, op0=ALU.mult, op1=ALU.min), s_neg)
                dve.wait_ge(s_ln, t + 1)
                step(STT(out=sb_sp, in0=sb_l, scalar=0.0, in1=sb_e, op0=ALU.max, op1=ALU.add))
                mark(TT(sb_sp, sb_sp, mask4, ALU.mult), s_sp)
                step(STT(out=sb_l, in0=sb_l, scalar=0.0, in1=sb_e, op0=ALU.min, op1=ALU.subtract))
                dve.wait_ge(s_S, t + 1)
                mark(TT(sb_l, sb_l, L, ALU.subtract), s_w0)
                dve.wait_ge(s_w1, t + 1)
                mark(TT(sb_l, sb_l, mask4, ALU.mult), s_w)
            dve.wait_ge(s_acsps, 1)
            mark(v.tensor_copy(dts[:, 4], PS[:, 5, 0:32].rearrange("p (b h) -> p b h", b=2)), s_acs)
            dve.wait_ge(s_cbps, 1)
            mark(TT(cb_mask.rearrange("p b g l -> p (b g) l"), PS[:, 6, :].rearrange("p (c l) -> p c l", c=4),
                    prefix_ones[:].unsqueeze(1).to_broadcast([P, 4, P]), ALU.mult), s_cb)
            dve.wait_ge(s_acs, 1)
            dve.wait_ge(s_xs, 1)
            mark(TT(x_dt.rearrange("p b (h n) -> p (b h) n", n=64), xs_nat.rearrange("p b (h n) -> p (b h) n", n=64),
                    dts[:, 2].rearrange("p b h -> p (b h)").unsqueeze(2).to_broadcast([P, 32, 64]), ALU.mult), s_xf)
            for b in range(NB):
                dve.wait_ge(s_R, b + 1)
                R = PS[:, 4:8, :].rearrange("p c (h l) -> p (c h) l", l=P)
                step(TT(decay[:, b], R, dts[:, 4, b, :].unsqueeze(2).to_broadcast([P, 16, P]), ALU.subtract))
                mark(TS(decay[:, b], decay[:, b], 0.0, None, ALU.min), s_seg)
                if b == 0:
                    mark(TT(ds_out[:, 0, :], R[:, :, P - 1:P].rearrange("p h o -> p (h o)"), dts[:, 4, 0, :], ALU.subtract), s_edgein)
                else:
                    mark(v.tensor_copy(ds_out[:, 1, :], dts[:, 4, 1, :]), s_edgein)
                if b == 0:
                    dve.wait_ge(s_edge, 1)
                    dve.wait_ge(s_xf, 1)
                    mark(TT(x_end.rearrange("p (h n) -> p h n", n=64), x_dt[:, 0, :].rearrange("p (h n) -> p h n", n=64),
                            ds_out[:, 2, :].unsqueeze(2).to_broadcast([P, 16, 64]), ALU.mult), s_xf)
                dve.wait_ge(s_dec, b + 1)
                dve.wait_ge(s_cb, 1)
                d4 = decay[:, b].rearrange("p (g h) l -> p g h l", g=2)
                mark(TT(d4, d4, cb_mask[:, b].unsqueeze(2).to_broadcast([P, 2, 8, P]), ALU.mult), s_sc)
            copied(dve, "z")
            skip = bc16[:, 2, :].unsqueeze(2).to_broadcast([P, 16, 64])
            for b in range(NB):
                z = nat[:, b, 1024:2048]
                step(TT(y_skip.rearrange("p (h n) -> p h n", n=64), xs_nat[:, b, :].rearrange("p (h n) -> p h n", n=64),
                        skip, ALU.mult))
                dve.wait_ge(s_yd, b + 1)
                bank = 6 if b == 0 else 0
                step(TT(y_skip, y_skip, PS[:, bank:bank + 2, :].rearrange("p c n -> p (c n)"), ALU.add))
                if b == 1:
                    dve.wait_ge(s_yo, 1)
                    dve.wait_ge(s_edge, 2)
                    step(TT(y_tmp.rearrange("p (h n) -> p h n", n=64), PS[:, 2:4, :].rearrange("p c (h n) -> p (c h) n", n=64),
                            ds_out[:, 3, :].unsqueeze(2).to_broadcast([P, 16, 64]), ALU.mult))
                    step(TT(y_skip, y_skip, y_tmp, ALU.add))
                step(TT(z, z, y_skip, ALU.mult), s_y)
            dve.wait_ge(s_att, 2)
            rows4 = nat[:, :, :].rearrange("p b (g n) -> p (b g) n", g=4)
            sq = big[:, 0:4096].rearrange("p (b n) -> p b n", b=8)
            step(TT(sq, rows4, rows4, ALU.mult))
            step(v.tensor_reduce(ds_out[:, 0, 0:8], sq, AX, ALU.add))
            ss = ds_out[:, 0, 0:8].rearrange("p (b g) -> p b g", b=2)
            step(v.tensor_copy(ssq[:, 6:10].rearrange("p (b g) -> p b g", b=2), ss[:, :, 2:4]))
            step(TT(ssq[:, 10:12], ss[:, :, 0], ss[:, :, 1], ALU.add), s_y)
            dve.wait_ge(s_root, ROOTS[1])
            step(v.reciprocal(rinv[:, 4:10], root[:, 4:10]))
            for b in range(NB):
                step(TS(nat[:, b, 0:1024], nat[:, b, 0:1024], rinv[:, 4 + b:5 + b], None, ALU.mult))
                mark(TT(nat[:, b, 1024:2048].rearrange("p (g n) -> p g n", g=2), nat[:, b, 1024:2048].rearrange("p (g n) -> p g n", g=2),
                        rinv[:, 6 + 2 * b:8 + 2 * b].unsqueeze(2).to_broadcast([P, 2, 512]), ALU.mult), s_nat)
            take_T(1, cols_a[:, A_MIX:A_MIX + 16])

            def add_plain(name, s):
                for c in range(4):
                    g = FIRST[name] + c
                    for b in range(NB):
                        dve.wait_ge(bank_done, done(g, b))
                        x = xres[:, b, c * 512:(c + 1) * 512]
                        TT(x, x, PS[:, 2 * (g % 2) + b, :], ALU.add).then_inc(bank_free[2 * (g % 2) + b], 1)
                    weigh(g)
                copied(dve, name)
                mark(v.memset(junk[:, 1:2], 0.0), s)

            add_plain("mix", s_res)
            norm_rows(2)
            take_T(2, None)

            for c in range(4):
                weigh(FIRST["query"] + c)
            mod_ready(0)
            dve.wait_ge(s_psc, 2)

            def route(H, e):
                ds2 = bass.ds(H * 2, 2)
                route_step(v.tensor_copy(sc_now, scores[:, ds2, :]))
                for c in range(2):
                    sc = sc_now[:, c, :]
                    route_step(v.max(top_s[:, c, 0:8], sc))
                    route_step(v.max_index(top_u[:, c, 0:8], top_s[:, c, 0:8], sc))
                    route_step(v.match_replace(sc, top_s[:, c, 0:8], sc, TAKEN))
                    route_step(v.max(top_s[:, c, 8:16], sc))
                    route_step(v.max_index(top_u[:, c, 8:16], top_s[:, c, 8:16], sc))
                route_step(v.tensor_copy(top_f, top_u))
                route_step(TT(cand.rearrange("p (i j) -> p i j", i=16), top_s[:, 0, :].unsqueeze(2).to_broadcast([P, 16, 16]),
                              top_s[:, 1, :].unsqueeze(1).to_broadcast([P, 16, 16]), ALU.add))
                route_step(v.max(best[:, 0:8], cand))
                route_step(v.max_index(pos_u[:, 0:8], best[:, 0:8], cand))
                route_step(v.match_replace(cand, best[:, 0:8], cand, TAKEN))
                route_step(v.max(best[:, 8:16], cand))
                route_step(v.max_index(pos_u[:, 8:16], best[:, 8:16], cand))
                route_step(TS(pos_12[:, 0], pos_u, 4, None, ALU.logical_shift_right))
                route_step(TS(pos_12[:, 1], pos_u, 15, None, ALU.bitwise_and))
                route_step(v.tensor_copy(pos_12f, pos_12))
                for c in range(2):
                    route_step(TT(hot, pos_12f[:, c].unsqueeze(2).to_broadcast([P, 16, 16]),
                                  iota_f[:].unsqueeze(1).to_broadcast([P, 16, 16]), ALU.is_equal))
                    route_step(TT(hot, hot, top_f[:, c, :].unsqueeze(1).to_broadcast([P, 16, 16]), ALU.mult))
                    route_step(v.tensor_reduce(half_id[:, c], hot, AX, ALU.add))
                if not isinstance(H, int) or H > 0:
                    dve.wait_ge(s_now, H)
                STT(out=expert_next[:], in0=half_id[:, 0], scalar=float(NK), in1=half_id[:, 1],
                    op0=ALU.mult, op1=ALU.add).then_inc(s_route, 1)
                TS(gates[:, e, :], best, best[:, 0:1], None, ALU.subtract).then_inc(s_gin, 1)

            step(v.tensor_copy(pos_f[:], pos_i[:]))
            step(TT(ang[:, 0], pos_f[:].unsqueeze(2).to_broadcast([P, 2, 16]),
                    inv_freq[:].unsqueeze(1).to_broadcast([P, 2, 16]), ALU.mult))
            step(TS(ang[:, 1], ang[:, 0], float(1 / (2 * np.pi)), None, ALU.mult))
            step(v.tensor_copy(ang_i[:], ang[:, 1]))
            step(v.tensor_copy(ang[:, 1], ang_i[:]))
            step(STT(out=ang[:, 0], in0=ang[:, 1], scalar=-TWO_PI_HI, in1=ang[:, 0], op0=ALU.mult, op1=ALU.add))
            step(STT(out=ang[:, 0], in0=ang[:, 1], scalar=-TWO_PI_LO, in1=ang[:, 0], op0=ALU.mult, op1=ALU.add))
            for bound, op, turn_by in ((PI, ALU.is_gt, -2 * np.pi), (-PI, ALU.is_lt, 2 * np.pi)):
                step(TS(ang[:, 1], ang[:, 0], bound, float(turn_by), op, ALU.mult))
                step(TT(ang[:, 0], ang[:, 0], ang[:, 1], ALU.add))
            step(TS(ang[:, 2], ang[:, 0], PI, -PI, ALU.min, ALU.max))
            step(STT(out=ang[:, 3], in0=ang[:, 2], scalar=-1.0, in1=ang[:, 2], op0=ALU.mult, op1=ALU.max), s_angle)

            in_route = [0, None]

            def route_step(ins):
                in_route[0] += 1
                ins.then_inc(s_rstep, 1)
                dve.wait_ge(s_rstep, in_route[1] * ROUTE_STEPS + in_route[0])
                if in_route[0] in BEFORE_MAX:
                    dve.sem_inc(s_rcarry, 1)

            def route_head(H, e):
                in_route[:] = [0, H]
                route(H, e)
                assert in_route[0] == ROUTE_STEPS

            in_route[:] = [0, 0]
            route_head(0, 0)

            def head(H, b, e, more):
                for k in range(16):
                    dve.wait_ge(landed[k % 8], H * 64 + 16 * (1 + k // 8))
                    row = gather_buf[:, k % 8, :]
                    v.tensor_tensor_reduce(out=row, in0=row, in1=nat[:, b, :], scale=1.0, scalar=0.0,
                                           op0=ALU.mult, op1=ALU.add, accum_out=dots[:, e, k:k + 1]
                                           ).then_inc(s_down, 1)
                dve.wait_ge(s_gex, H + 1)
                v.tensor_reduce(gsum[:, 0:1], gates[:, e, :], AX, ALU.add).then_inc(s_gnorm, 1)
                dve.wait_ge(s_gnorm, H * 3 + 1)
                v.reciprocal(gsum[:, 1:2], gsum[:, 0:1]).then_inc(s_gnorm, 1)
                dve.wait_ge(s_gnorm, H * 3 + 2)
                TS(gates[:, e, :], gates[:, e, :], gsum[:, 1:2], None, ALU.mult).then_inc(s_gnorm, 1)
                dve.wait_ge(s_gnorm, H * 3 + 3)
                dve.wait_ge(s_gelu, H + 1)
                TT(weight[:, e, :], gelu[:, e, :], gates[:, e, :], ALU.mult).then_inc(s_wt, 1)
                if more:
                    route_head(H + 1, 1 - e)

            for b in range(NB):
                with dve.Fori(0, PH // 2 - b) as j:
                    for e in range(2):
                        head(j * 2 + (PH * b + e), b, e, True)
            for e in range(2):
                head(NB * PH - 2 + e, 1, e, e == 0)
            mc = mod_cols[:].rearrange("p (l c) -> p l c", l=2)

            def shift(layer):
                dve.wait_ge(s_xt, 8 * (4 + layer))
                mark(TT(actT[:], actT[:], mc[:, layer, 0:16].unsqueeze(2).to_broadcast([P, KC, T]), ALU.add), s_shift)

            norm_rows(3)
            take_T(3, mod_gain[:, 0, :])
            shift(0)
            dve.wait_ge(s_cnt, 4)
            step(v.tensor_copy(counts, counts.bitcast(I32)))
            for w, width in enumerate(WINDOWS):
                step(TS(counts[:, w, :], counts[:, w, :], float(width), None, ALU.min))
            step(v.reciprocal(counts, counts))
            for gi, width in enumerate(WINDOWS):
                g = FIRST["pv"] + gi
                for u in range(2):
                    dve.wait_ge(bank_free[2 * (g % 2) + u], g // 2 + 1)
                weigh(g)
                cur = poolT[:, 4 * gi:4 * gi + 4, :]
                own, by, i = cur, 1, 0
                while by < width:
                    nxt = sums[i % 2]
                    step(v.tensor_copy(nxt[:, :, 0:by], cur[:, :, 0:by]))
                    step(TT(nxt[:, :, by:], cur[:, :, by:], cur[:, :, 0:T - by], ALU.add))
                    cur, by, i = nxt, 2 * by, i + 1
                step(TT(cur, cur, counts[:, gi, :].unsqueeze(1).to_broadcast([P, 4, T]), ALU.mult))
                step(TT(own, cur, own, ALU.subtract), s_pool_T)
            for c in range(4):
                weigh(FIRST["pg"] + c)
            for i in range(4):
                g = FIRST["grp"] + i
                for u in range(2):
                    dve.wait_ge(bank_done, done(g, u))
                    if i == 0 and u == 0:
                        copied(dve, "pg")
                    for o in range(2):
                        c = 4 * i + 2 * u + o
                        ins = STT(out=pgateT[:, c, :], in0=PS[:, 2 * (g % 2) + u, o * T:(o + 1) * T],
                                  scalar=cols_b[:, B_SCALE + c:B_SCALE + c + 1], in1=pgateT[:, c, :],
                                  op0=ALU.mult, op1=ALU.mult)
                        if o:
                            ins.then_inc(bank_free[2 * (g % 2) + u], 1)
                        else:
                            mark(ins, s_dve)

            def add_gated(name, layer):
                dve.wait_ge(s_wide, 32 + 16 * layer)
                for c in range(4):
                    g = FIRST[name] + c
                    for b in range(NB):
                        dve.wait_ge(bank_done, done(g, b))
                        bank = PS[:, 2 * (g % 2) + b, :]
                        cs = slice(c * 512, (c + 1) * 512)
                        TT(stage[:, b, :], bank, wide[:, cs], ALU.mult).then_inc(bank_free[2 * (g % 2) + b], 1)
                        dve.wait_ge(bank_free[2 * (g % 2) + b], g // 2 + 1)
                        step(TT(xres[:, b, cs], xres[:, b, cs], stage[:, b, :], ALU.add), s_res)
                    weigh(g)

            add_gated("po", 0)
            mod_ready(1)
            norm_rows(4)
            take_T(4, mod_gain[:, 1, :])
            shift(1)

            def rotate(x, heads, half, cs, sn, last_sem):
                x1, x2 = x[:, :, 0:half], x[:, :, half:2 * half]
                cs, sn = [t.unsqueeze(1).to_broadcast([P, heads, half]) for t in (cs, sn)]
                t = [rope_t[:, i, 0:heads * half].rearrange("p (h n) -> p h n", h=heads) for i in range(4)]
                mark(TT(t[0], x1, cs, ALU.mult), s_dve)
                mark(TT(t[1], x2, sn, ALU.mult), s_dve)
                mark(TT(t[2], x2, cs, ALU.mult), s_dve)
                step(TT(t[3], x1, sn, ALU.mult))
                step(TT(x1, t[0], t[1], ALU.subtract))
                step(TT(x2, t[2], t[3], ALU.add), last_sem)

            dve.wait_ge(s_trig, 2)
            for i in range(20):
                g = FIRST["aq"] + i // 2 if i < 16 else FIRST["ai"] + (i - 16) // 2
                b = i % 2
                dve.wait_ge(bank_free[2 * (g % 2) + b], g // 2 + 1)
                if i < 16:
                    rotate(stage[:, b, :].rearrange("p (h n) -> p h n", h=4), 4, 16, cosine[:, b, :], sine[:, b, :], s_rope)
                else:
                    rotate(stage[:, b, :].rearrange("p (h n) -> p h n", h=8), 8, 8,
                           cosine[:, b, 0:16:2], sine[:, b, 0:16:2], s_rope)
            dve.wait_ge(s_kist, 2)
            for b in range(NB):
                rotate(ki_wi[:, b:b + 1, 0:64], 1, 8, cosine[:, b, 0:16:2], sine[:, b, 0:16:2], s_dve)
            step(v.tensor_copy(ki_wi[:, :, 64:128], ki_wi[:, :, 0:64]), s_kirope)
            for i in range(2 * IH):
                b, h = i // IH, i % IH
                S = P * (b + 1)
                dve.wait_ge(s_relu, i + 1)
                w = ki_wi[:, b, 128 + h:129 + h]
                if h == 0:
                    ins = TS(iscore[:, b, 0:S], relu[:, i % 2, 0:S], w, None, ALU.mult)
                else:
                    ins = STT(out=iscore[:, b, 0:S], in0=relu[:, i % 2, 0:S], scalar=w, in1=iscore[:, b, 0:S],
                              op0=ALU.mult, op1=ALU.add)
                step(ins, s_iuse)
                if h == IH - 1:
                    mark(v.memset(junk[:, 3:4], 0.0), s_iacc)
            for b in range(NB):
                S = P * (b + 1)
                dve.wait_ge(s_iadm, b + 1)
                src = iscore[:, b, 0:S]
                for r in range(SELECT // 8):
                    step(v.max(best8[:], src))
                    step(v.match_replace(iwork[:, 0:S], best8[:], src, TAKEN))
                    src = iwork[:, 0:S]
                o = sel_bias[:, 0:P] if b == 0 else sel_bias[:, P:]
                step(TT(o, iwork[:, 0:S], iscore[:, b, 0:S], ALU.is_equal))
                mark(TS(o, o, MASKED, None, ALU.mult), s_sel)
            dve.wait_ge(s_causal, 2)

            def masked(h):
                e = h % 2
                dve.wait_ge(s_lps, h + 1)
                if h >= 2:
                    dve.wait_ge(s_pe, 2 * (h - 1))
                for b in range(NB):
                    s = slice(0, P) if b == 0 else slice(P, 384)
                    step(v.tensor_tensor_reduce(out=lm[:, e, s], in0=PS[:, 4 + e, s], in1=sel_bias[:, s],
                                                scale=float(P ** -0.5), scalar=-3.0e38, op0=ALU.add, op1=ALU.max,
                                                accum_out=smax[:, e, b:b + 1]))
                    mark(TS(smax[:, e, b:b + 1], smax[:, e, b:b + 1], -1.0, None, ALU.mult), s_lm)

            def normed(h):
                e = h % 2
                dve.wait_ge(s_pe, 2 * h + 2)
                step(v.reciprocal(ssum[:, e, 2:4], ssum[:, e, 0:2]))
                step(TS(pr[:, e, 0:P], pr[:, e, 0:P], ssum[:, e, 2:3], None, ALU.mult))
                mark(TS(pr[:, e, P:384], pr[:, e, P:384], ssum[:, e, 3:4], None, ALU.mult), s_pn)

            def gated(h):
                dve.wait_ge(s_ops, h + 1)
                mark(TT(agateT[:, h, :], PS[:, 7, 0:T], agateT[:, h, :], ALU.mult), s_oT)

            copied(dve, "ag")
            for h in range(NH + 2):
                if h < NH:
                    masked(h)
                if 1 <= h <= NH:
                    normed(h - 1)
                if h >= 2:
                    gated(h - 2)
            add_gated("ao", 1)
            dve.wait_ge(s_fin, 16)
            dve.wait_ge(s_root, ROOTS[5])
            step(v.reciprocal(rinv[:, 0:2], root[:, 0:2]))
            for b in range(NB):
                step(STT(out=nat[:, b, :], in0=xres[:, b, :], scalar=rinv[:, b:b + 1], in1=final_gain,
                         op0=ALU.mult, op1=ALU.mult), s_y)


_OUT = ("out_0_dram", (1, T, D))


def kernel(**inputs):
    import numpy as _np
    import concourse.bacc as _bacc
    from concourse import mybir as _mybir
    from concourse.bass_utils import run_bass_kernel_spmd as _run

    nc = _bacc.Bacc("TRN2", target_bir_lowering=False, num_devices=1)
    arrays, args = {}, {}
    for name, value in inputs.items():
        value = _np.ascontiguousarray(value)
        if value.ndim == 1:
            value = value.reshape(1, -1)
        arrays[f"in_{name}_dram"] = value
        args[name] = nc.dram_tensor(f"in_{name}_dram", value.shape, _mybir.dt.from_np(value.dtype),
                                    kind="ExternalInput").ap()
    out = nc.dram_tensor(_OUT[0], _OUT[1], _mybir.dt.float32, kind="ExternalOutput").ap()
    gate_dram = nc.dram_tensor("gate_rows", (2, D), _mybir.dt.float32, kind="Internal").ap()
    program(nc, args, out, gate_dram)
    r = _run(nc, [arrays], core_ids=[0])
    return r.results[0][_OUT[0]]
```

```python
from contextlib import ExitStack

import concourse.bass as bass
from concourse import mybir
import numpy as np

F32 = mybir.dt.float32
I32 = mybir.dt.int32
U32 = mybir.dt.uint32
ALU = mybir.AluOpType
ACT = mybir.ActivationFunctionType
AX = mybir.AxisListType.X

P = 128
D = 2048
NB = 2
T = NB * P
KC = D // P
EPS = 1e-6
SLOTS = 5
UNIT = 4096
SBH, SSH = 8, 16
XC = 12
PH, NK, TOPK = 8, 128, 16
UPS = PH * TOPK
NH, IH = 16, 16
ROUTE_STEPS = 27
BEFORE_MAX = (1, 2, 3, 4, 5, 6, 7, 8, 9, 10, 13, 14, 15, 16, 17)
SELECT = 64
WINDOWS = (2, 4, 8, 16)
NEG = -3.0e38
TAKEN = -3.3e38
MASKED = -1.0e30
TWO_PI_HI = 6.28125
TWO_PI_LO = float(np.float32(2 * np.pi - 6.28125))
PI = 3.1415925
INV_FREQ = [float(v) for v in (np.float32(500000.0) ** (-np.arange(16, dtype=np.float32) * np.float32(2.0) / np.float32(32)))]

A_NORM, A_MIX, A_Q, A_K, A_CB, A_CW, A_ROWS = 0, 16, 32, 33, 34, 46, 94
B_NORM, B_SCALE, B_COND, B_ROWS = 0, 32, 48, 64

STAGES = [
    ("q", "w_in", 0, 2, "N"), ("k", "w_in", 1024, 2, "N"), ("v", "w_in", 2048, 2, "N"),
    ("z", "w_in", 3072, 2, "N"), ("xbc", "w_in", 4096, 3, "T"), ("mix", "w_out", 0, 4, "N"),
    ("query", "peer_query", 0, 4, "T"),
    ("pv", "pool_w_in", 0, 4, "T"), ("pg", "pool_w_in", 2048, 4, "T"), ("grp", "pool_w_grp", 0, 4, "G"),
    ("po", "pool_w_out", 0, 4, "N"),
    ("aq", "attn_w_in", 0, 4, "N"), ("ak", "attn_w_in", 2048, 4, "N"), ("ai", "attn_w_in", 8192, 2, "N"),
    ("ag", "attn_w_in", 6144, 4, "T"), ("av", "attn_w_in", 4096, 4, "N"), ("ao", "attn_w_out", 0, 4, "N"),
]


MOD_AFTER = {"q": (1, 1), "k": (1, 2), "v": (2, 2), "z": (2, 2), "xbc": (2, 1, 0), "mix": (2, 2, 2, 2),
             "pv": (2, 2, 2, 2), "pg": (2, 2, 2, 2), "po": (2, 2, 2, 2)}
MOD_BUFS = 4
PADS = 3


def plan():
    first, units, halves, g, mods = {}, [], 0, 0, 0
    for name, weight, col, n, kind in STAGES:
        first[name] = g
        for c in range(n):
            if kind == "N":
                halves += 1
                units.append((g, kind, weight, col + 512 * c, 0, ("half", halves)))
                units.append((g, kind, weight, col + 512 * c, 1, ("bank", 2 * g + 2)))
            elif kind == "T":
                for u in range(2):
                    units.append((g, kind, weight, col + 512 * c + 256 * u, u, ("bank", 2 * g + u + 1)))
            elif c % 2 == 0:
                units.append((g, kind, weight, 0, c, ("bank", 2 * (g + 1) + 2)))
            for _ in range(MOD_AFTER[name][c] if name in MOD_AFTER else 0):
                units.append((g, "M", "mod_w_2", mods, 0, ("mod", mods + 1)))
                mods += 1
            g += 1
    assert mods == 48
    return first, units


FIRST, UNITS = plan()
UNITS_OF = {}
MODS_OF = {}
for _n, _u in enumerate(UNITS):
    (MODS_OF if _u[1] == "M" else UNITS_OF).setdefault(_u[0], []).append(_n)
N_BEFORE = sum(1 for u in UNITS if u[0] < FIRST["pv"])
GATHER_AT = [2 * ((N_BEFORE + i) % SLOTS) + h for i in range(4) for h in range(2)]


ROOTS = {0: 1, 1: 3, 2: 4, 3: 6, 4: 7, 5: 8}
SQUARES = {0: 2, 2: 10, 3: 12, 4: 20, 5: 28}


def mods_until(g):
    return sum(len(v) for k, v in MODS_OF.items() if k <= g)


def done(g, i):
    return 2 * g + i + 1


def program(nc, a, out, gate_dram):
    with ExitStack() as ctx:
        def sb(name, shape, dt=F32):
            return ctx.enter_context(nc.sbuf_tensor(name, shape, dt))

        def sem(name):
            return ctx.enter_context(nc.semaphore(name))

        ring = sb("ring", [P, SLOTS, UNIT])
        xres = sb("xres", [P, NB, D])
        nat = sb("nat", [P, NB, D])
        actT = sb("actT", [P, KC, T])
        big = sb("big", [P, 12288])
        wide = sb("wide", [P, D])
        stage = sb("stage", [P, 2, 512])
        work = sb("work", [P, 1792])
        ident = sb("ident", [P, P])
        later_ones = sb("later_ones", [P, P])
        prefix_ones = sb("prefix_ones", [P, P])
        ones = sb("ones", [P, P])
        sb_mask = sb("sb_mask", [P, 384])
        rows_a = sb("rows_a", [A_ROWS, P])
        rows_b = sb("rows_b", [B_ROWS, P])
        cols_a = sb("cols_a", [P, A_ROWS])
        cols_b = sb("cols_b", [P, B_ROWS])
        rows_c = sb("rows_c", [96, P])
        cols_c = sb("cols_c", [P, 96])
        cond = sb("cond", [P, KC])
        const = sb("const", [P, 4])
        iota_i = sb("iota_i", [P, 16], I32)
        iota_f = sb("iota_f", [P, 16])
        inv_freq = sb("inv_freq", [P, 16])
        pos_i = sb("pos_i", [P, NB], I32)
        pos_f = sb("pos_f", [P, NB])
        cosine = sb("cosine", [P, NB, 16])
        sine = sb("sine", [P, NB, 16])
        ang = sb("ang", [P, 4, NB, 16])
        ang_i = sb("ang_i", [P, NB, 16], I32)
        bc16 = sb("bc16", [P, 3, 16])
        ssq = sb("ssq", [P, 16])
        ssq_part = sb("ssq_part", [P, NB, 4])
        root = sb("root", [P, 16])
        rinv = sb("rinv", [P, 16])
        hstat = sb("hstat", [P, 3, 4])
        dts = sb("dts", [P, 6, NB, 16])
        ds_out = sb("ds_out", [P, 4, 16])
        expert_next = sb("expert_next", [P, 16], I32)
        gates = sb("gates", [P, 2, 16])
        gsum = sb("gsum", [P, 4])
        expert_now = sb("expert_now", [P, 2, 16], I32)
        dots = sb("dots", [P, 2, 16])
        gelu = sb("gelu", [P, 2, 16])
        weight = sb("weight", [P, 2, 16])
        mod_cols = sb("mod_cols", [P, 96])
        mod_gain = sb("mod_gain", [P, 2, KC])
        ki_wi = sb("ki_wi", [P, NB, 144])
        best8 = sb("best8", [P, 8])
        smax = sb("smax", [P, 2, 3])
        ssum = sb("ssum", [P, 2, 4])
        junk = sb("junk", [P, 4])
        PS = ctx.enter_context(nc.psum_tensor("PS", [P, 8, 512], F32))

        act_flat = actT[:, :, :].rearrange("p k t -> p (k t)")
        ring_rows = ring[:, :, :].rearrange("p s (h d) -> p (s h) d", h=2)
        gather_buf = [ring_rows[:, i, :] for i in GATHER_AT]
        qT_a = big[:, 0:2048].rearrange("p (h t) -> p h t", h=SBH)
        kT_a = big[:, 2048:4096].rearrange("p (h t) -> p h t", h=SBH)
        xbcT = big[:, 4096:7168].rearrange("p (c t) -> p c t", c=XC)
        scr = big[:, 7168:12288]
        xpad = wide[:, 0:PADS * 2 * 259].rearrange("p (i c t) -> p i c t", i=PADS, c=2)
        square = scr[:, 3200:3712]
        sb_l, sb_e, sb_sp = [scr[:, 1536 * i:1536 * (i + 1)].rearrange("p (h t) -> p h t", h=4) for i in range(3)]
        xs_nat = scr[:, 0:2048].rearrange("p (b n) -> p b n", b=NB)
        x_dt = scr[:, 2048:4096].rearrange("p (b n) -> p b n", b=NB)
        x_end = scr[:, 4096:5120]
        decay = big[:, 0:4096].rearrange("p (b h l) -> p b h l", b=NB, h=SSH)
        b_nat = act_flat[:, 0:256]
        cb_mask = act_flat[:, 256:768].rearrange("p (b g l) -> p b g l", b=NB, g=2)
        states = act_flat[:, 768:1792]
        y_tmp = act_flat[:, 1792:2816]
        y_skip = act_flat[:, 2816:3840]
        queryT = big[:, 0:4096].rearrange("p (s t) -> p s t", s=16)
        keys_nat = big[:, 4096:6144].rearrange("p (s k) -> p s k", s=16)
        keysT = big[:, 6144:8192].rearrange("p (s k) -> p s k", s=16)
        scores = big[:, 8192:12288].rearrange("p (s k) -> p s k", s=32)
        poolT = big[:, 0:4096].rearrange("p (c t) -> p c t", c=KC)
        pgateT = big[:, 4096:8192].rearrange("p (c t) -> p c t", c=KC)
        sums = [big[:, 8192 + 1024 * i:9216 + 1024 * i].rearrange("p (c t) -> p c t", c=4) for i in range(2)]
        counts = big[:, 10240:11264].rearrange("p (w t) -> p w t", w=4)
        qT_b = poolT
        kT_b = pgateT
        agateT = big[:, 8192:12288].rearrange("p (c t) -> p c t", c=NH)
        qiT = wide[:, :].rearrange("p (h t) -> p h t", h=8)
        w_dt = work[:, 0:256].rearrange("p (k n) -> p k n", k=KC)
        mod_acc = work[:, 256:1280].rearrange("p (i n) -> p i n", i=MOD_BUFS)
        sc_now = work[:, 0:256].rearrange("p (c k) -> p c k", c=2)
        cand = work[:, 256:512]
        top_s = work[:, 512:544].rearrange("p (c k) -> p c k", c=2)
        top_u = work[:, 544:576].bitcast(U32).rearrange("p (c k) -> p c k", c=2)
        top_f = work[:, 576:608].rearrange("p (c k) -> p c k", c=2)
        best = work[:, 608:624]
        pos_u = work[:, 624:640].bitcast(U32)
        pos_12 = work[:, 640:672].bitcast(U32).rearrange("p (c k) -> p c k", c=2)
        pos_12f = work[:, 672:704].rearrange("p (c k) -> p c k", c=2)
        half_id = work[:, 704:736].rearrange("p (c k) -> p c k", c=2)
        hot = work[:, 736:992].rearrange("p (k i) -> p k i", k=16)
        w_small = work[:, 0:1280].rearrange("p (k n) -> p k n", k=KC)
        rope_t = work[:, 1280:1792].rearrange("p (i n) -> p i n", i=4)
        diag = stage[:, 0, :].rearrange("p (i n) -> p i n", i=4)
        row_scale = stage[:, 1, 0:NB * P].rearrange("p (b n) -> p b n", b=NB)
        mix_scale = stage[:, :, :].rearrange("p i n -> p (i n)")[:, 0:6 * P].rearrange("p (b g n) -> p b g n", b=NB, g=3)
        spare = stage[:, :, :].rearrange("p i n -> p (i n)")
        gate_rows = rows_c[0:16, :]
        kiT = sb_mask[:, 0:T]
        final_gain = big[:, 0:D]
        lm = act_flat[:, 0:768].rearrange("p (e s) -> p e s", e=2)
        pr = act_flat[:, 768:1536].rearrange("p (e s) -> p e s", e=2)
        prT = act_flat[:, 1536:2304].rearrange("p (e s) -> p e s", e=2)
        relu = work[:, 0:512].rearrange("p (e s) -> p e s", e=2)
        iscore = work[:, 512:1024].rearrange("p (b s) -> p b s", b=NB)
        iwork = work[:, 1024:1280]
        sel_bias = work[:, 1280:1664]

        s_in = sem("x_loaded")
        s_rows = sem("rows_loaded")
        s_bc = sem("spread_rows_loaded")
        s_wdt = sem("w_dt_loaded")
        s_wsmall = sem("w_small_loaded")
        s_keys = sem("keys_loaded")
        s_wide = sem("wide_loaded")
        s_gateps = sem("gate_rows_psum")
        s_grow = sem("gate_rows_copied")
        s_gst = sem("gate_rows_stored")
        s_out = sem("out_stored")
        s_fin = sem("final_gain_loaded")
        s_issue = sem("gathers_issued")
        s_rstep = sem("routing_step")
        s_rcarry = sem("routing_waits_carried")
        s_gnorm = sem("gate_norm_step")
        s_now = sem("experts_of_head")
        s_cnt = sem("window_counts")
        s_causal = sem("selection_causal")
        s_xpad = sem("conv_padded")
        s_resu = sem("residual_with_experts")
        s_iuse = sem("index_relu_used")
        unit_in = [sem(f"unit_in_slot{i}") for i in range(SLOTS)]
        half_used = sem("half_used")
        bank_done = sem("gemm_bank_done")
        bank_free = [sem(f"gemm_bank_free{i}") for i in range(4)]
        s_const = sem("constants_ready")
        s_pool = sem("pool_step")
        s_dve = sem("dve_step")
        s_act = sem("act_step")
        s_colps = sem("columns_in_psum")
        s_cols = sem("columns_ready")
        s_ssq = sem("square_sums")
        s_ssum = sem("square_sums_of_quarters")
        s_root = sem("roots")
        s_nat = sem("normed_rows")
        s_tp = sem("transposes_done")
        s_xt = sem("activations_T")
        s_qkst = sem("qk_staged")
        s_qkrt = sem("qk_roots")
        s_qkss = sem("qk_square_sums")
        s_qkn = sem("qk_normed")
        s_qktp = sem("qk_transposed")
        s_qkT = sem("qk_T_ready")
        s_conv = sem("conv_done")
        s_silu = sem("conv_silu")
        s_dtps = sem("dt_in_psum")
        s_dtst = sem("dt_rows")
        s_dtl = sem("dt_log")
        s_dt = sem("dt_ready")
        s_L = sem("sb_logits")
        s_neg = sem("sb_neg_abs")
        s_ln = sem("sb_log1p")
        s_sp = sem("sb_softplus")
        s_S = sem("sb_later")
        s_w0 = sem("sb_exponent")
        s_w1 = sem("sb_exp")
        s_w = sem("sb_weights")
        s_O = sem("sb_out_psum")
        s_att = sem("sb_out")
        s_xsps = sem("xs_transposed")
        s_xs = sem("xs_natural")
        s_acsps = sem("cumulated_psum")
        s_acs = sem("cumulated")
        s_R = sem("cumulated_rows")
        s_seg = sem("segments")
        s_dec = sem("decay")
        s_edge = sem("edge_decays")
        s_edgein = sem("edge_decay_inputs")
        s_cbps = sem("cb_psum")
        s_cb = sem("cb_masked")
        s_sc = sem("ssd_scores")
        s_xf = sem("ssd_x")
        s_yd = sem("y_diag")
        s_stps = sem("states_psum")
        s_st = sem("states")
        s_yo = sem("y_off")
        s_y = sem("y_rows")
        s_res = sem("residual_ready")
        s_ktps = sem("keys_transposed")
        s_kt = sem("keys_T")
        s_scps = sem("peer_scores_psum")
        s_psc = sem("peer_scores")
        s_gin = sem("gate_exponents")
        s_gex = sem("gate_exps")
        s_route = sem("routing_ready")
        landed = [sem(f"gathered_buf{i}") for i in range(8)]
        s_down = sem("down_used")
        s_up = sem("up_used")
        s_tail = sem("tail_rows_used")
        s_tailed = sem("tail_added")
        s_gelu = sem("gelu_ready")
        s_wt = sem("expert_weights")
        s_diag = sem("diagonals")
        s_modw = sem("mod_unit_weighed")
        s_msum = sem("mod_unit_summed")
        s_mcol = sem("mod_cols_copied")
        s_cond = sem("condition_ready")
        s_modc = sem("mod_cols_ready")
        s_pool_T = sem("pooled_T")
        s_angle = sem("angles")
        s_trig = sem("sines")
        s_rope = sem("roped")
        s_rtp = sem("rope_transposed")
        s_rT = sem("qkT_ready")
        s_kips = sem("ki_psum")
        s_kist = sem("ki_staged")
        s_kirope = sem("ki_roped")
        s_kitp = sem("ki_transposed")
        s_kiT = sem("kiT_ready")
        s_ips = sem("index_psum")
        s_relu = sem("index_relu")
        s_iacc = sem("index_sum")
        s_iadm = sem("index_admissible")
        s_sel = sem("selection")
        s_lps = sem("logits_psum")
        s_lm = sem("logits_masked")
        s_pe = sem("probs_exp")
        s_pn = sem("probs_normed")
        s_ptps = sem("probs_transposed")
        s_pT = sem("probs_T")
        s_ops = sem("attn_out_psum")
        s_oT = sem("attn_out_T")

        def spread(src, n):
            return bass.AP(tensor=src.tensor, offset=src.offset, ap=[[0, P], [1, n]])

        def counted(eng, default):
            counts = {}

            def step(ins, s=default, by=1):
                counts[s.name] = counts.get(s.name, 0) + by
                ins.then_inc(s, by)
                eng.wait_ge(s, counts[s.name])

            def mark(ins, s, by=1):
                counts[s.name] = counts.get(s.name, 0) + by
                ins.then_inc(s, by)
            return step, mark

        def bank_of(r, t):
            return t if r == 3 and t < 4 else 4 + t % 4

        def copied(eng, name, chunks=2):
            n = next(x[3] for x in STAGES if x[0] == name)
            for g in range(FIRST[name] + n - chunks, FIRST[name] + n):
                for i in range(2):
                    eng.wait_ge(bank_free[2 * (g % 2) + i], g // 2 + 1)

        block = ctx.enter_context(nc.Block())

        @block.sync
        def _(sp):
            weights = {k: a[k] for k in ("w_in", "w_out", "peer_query")}
            weights["pool_w_in"], weights["pool_w_out"] = a["pool_w_in_2"], a["pool_w_out_2"]
            weights["attn_w_in"], weights["attn_w_out"] = a["attn_w_in_2"], a["attn_w_out_2"]
            for b in range(NB):
                sp.dma_start(xres[:, b, :], a["x"][0, b * P:(b + 1) * P, :]).then_inc(s_in, 16)

            def load(n):
                _, kind, w, col, part, _ = UNITS[n]
                slot = ring[:, n % SLOTS, :]
                if kind == "N":
                    src = weights[w][0, part * 1024:(part + 1) * 1024, col:col + 512]
                    dst = slot.rearrange("p (k n) -> p k n", k=8)
                    src = src.rearrange("(k p) n -> p k n", p=P)
                elif kind == "M":
                    src = a[w][col // 24, :, 256 * (col % 24):256 * (col % 24) + 256].rearrange("(k p) n -> p k n", p=P)
                    dst = slot.rearrange("p (k n) -> p k n", k=KC)
                elif kind == "T":
                    src = weights[w][0, :, col:col + 256].rearrange("(k p) n -> p k n", p=P)
                    dst = slot.rearrange("p (k n) -> p k n", k=KC)
                else:
                    src = a["pool_w_grp_2"][0, part:part + 2].rearrange("g (k p) n -> p (g k) n", p=P)
                    dst = slot.rearrange("p (k n) -> p k n", k=8)
                sp.dma_start(dst, src).then_inc(unit_in[n % SLOTS], 16)

            sp.wait_ge(s_rows, 16 * 11)
            used = {"half": half_used, "bank": bank_done, "mod": s_modw}

            for n in range(N_BEFORE):
                if n >= SLOTS:
                    what, value = UNITS[n - SLOTS][5]
                    sp.wait_ge(used[what], value)
                load(n)
            for n in range(N_BEFORE, len(UNITS)):
                if n < N_BEFORE + SLOTS - 1:
                    last_use = 2 * (n - N_BEFORE + 1)
                    sp.wait_ge(s_up, UPS * NB + last_use)
                    sp.wait_ge(s_tail, last_use)
                elif n >= N_BEFORE + SLOTS:
                    what, value = UNITS[n - SLOTS][5]
                    sp.wait_ge(used[what], value)
                load(n)
            for b in range(NB):
                sp.wait_ge(s_y, 3 + b)
                sp.dma_start(out[0, b * P:(b + 1) * P, :], nat[:, b, :]).then_inc(s_out, 16)
            sp.wait_ge(s_out, 16 * NB)

        @block.gpsimd
        def _(pool):
            step, mark = counted(pool, s_pool)
            g = nc.gpsimd
            step(g.memset(ident[:], 0.0))
            step(g.affine_select(out=ident[:], in_=ident[:], compare_op=ALU.not_equal, fill=1.0, base=0,
                                 pattern=[[-1, P]], channel_multiplier=1))
            step(g.memset(ones[:], 1.0))
            step(g.affine_select(out=later_ones[:], in_=ones[:], compare_op=ALU.is_gt, fill=0.0, base=0,
                                 pattern=[[-1, P]], channel_multiplier=1))
            step(g.affine_select(out=prefix_ones[:], in_=ones[:], compare_op=ALU.is_ge, fill=0.0, base=0,
                                 pattern=[[1, P]], channel_multiplier=-1))
            for i in (0, 2):
                step(g.affine_select(out=sb_mask[:, i * P:(i + 1) * P], in_=ones[:], compare_op=ALU.is_gt,
                                     fill=0.0, base=0, pattern=[[1, P]], channel_multiplier=-1))
            step(g.memset(sb_mask[:, P:2 * P], 1.0))
            for i, v in enumerate((EPS, 1.0, float(np.pi / 2), 0.0)):
                step(g.memset(const[:, i:i + 1], v))
            for i, v in enumerate(INV_FREQ):
                step(g.memset(inv_freq[:, i:i + 1], v))
            step(g.iota(iota_i[:], pattern=[[1, 16]], base=0, channel_multiplier=0))
            mark(g.tensor_copy(iota_f[:], iota_i[:]), s_const)

            tables = [a[k].rearrange("a e d -> (a e) d") for k in ("peer_down", "peer_up")]
            for b in range(NB):
                with pool.Fori(0, PH // 2) as j:
                    for e in range(2):
                        H = j * 2 + (PH * b + e)
                        pool.wait_ge(s_route, H + 1)
                        pool.sem_inc(s_issue, 1)
                        g.tensor_copy(expert_now[:, e, :], expert_next[:]).then_inc(s_now, 1)
                        pool.wait_ge(s_now, H + 1)
                        for s in range(32):
                            buf = s % 8
                            if s < 8:
                                pool.wait_ge(s_up, H * 16 + (buf + 1))
                            elif s < 24:
                                pool.wait_ge(s_down, H * 16 + (s - 8 + 1))
                            else:
                                pool.wait_ge(s_up, H * 16 + (8 + buf + 1))
                            pool.sem_inc(s_issue, 1)
                            k = s % 16
                            g.indirect_dma_start(out=gather_buf[buf], out_offset=None, in_=tables[s // 16],
                                                 in_offset=bass.IndirectOffsetOnAxis(ap=expert_now[:, e, k:k + 1], axis=0)
                                                 ).then_inc(landed[buf], 16)

            for w, width in enumerate(WINDOWS):
                g.iota(counts[:, w, :].bitcast(I32), pattern=[[1, T]], base=1, channel_multiplier=0).then_inc(s_cnt, 1)
            for b in range(NB):
                S = P * (b + 1)
                pool.wait_ge(s_iacc, 1 + b)
                g.affine_select(out=iscore[:, b, 0:S], in_=iscore[:, b, 0:S], compare_op=ALU.is_ge, fill=NEG,
                                base=P * b, pattern=[[-1, S]], channel_multiplier=1).then_inc(s_iadm, 1)
                pool.wait_ge(s_sel, 1 + b)
                o = sel_bias[:, 0:P] if b == 0 else sel_bias[:, P:]
                g.affine_select(out=o, in_=o, compare_op=ALU.is_ge, fill=MASKED,
                                base=P * b, pattern=[[-1, S]], channel_multiplier=1).then_inc(s_causal, 1)

        @block.tensor
        def _(pe):
            mm, tr = nc.tensor.matmul, nc.tensor.transpose

            def banks_free(g):
                if g >= 2:
                    for i in range(2):
                        pe.wait_ge(bank_free[2 * (g % 2) + i], g // 2)

            def arrived(n):
                pe.wait_ge(unit_in[n % SLOTS], 16 * (n // SLOTS + 1))

            summed = [0]

            def mod_sums(g, bank):
                for i in range(summed[0], mods_until(g)):
                    pe.wait_ge(s_modw, i + 1)
                    for h in range(2):
                        last = mm(PS[:, bank, 2 * (i % MOD_BUFS) + h:2 * (i % MOD_BUFS) + h + 1],
                                  mod_acc[:, i % MOD_BUFS, h * P:(h + 1) * P], ones[:, 0:1], start=True, stop=True)
                    last.then_inc(s_msum, 1)
                summed[0] = max(summed[0], mods_until(g))

            def gate_turn(layer, bank):
                pe.wait_ge(s_modc, layer + 1)
                tr(PS[0:16, bank, 0:P], mod_cols[:, 48 * layer + 32:48 * layer + 48], ident[:]).then_inc(s_gateps, 1)

            def gemm(name, lhs, before=None, half_way=None):
                n_chunks, kind = next((n, k) for m, _, _, n, k in STAGES if m == name)
                for g in range(FIRST[name], FIRST[name] + n_chunks):
                    if before is not None:
                        before(g - FIRST[name])
                    banks_free(g)
                    bank = 2 * (g % 2)
                    mod_sums(g - 2, bank + 1)
                    for part, n in enumerate(UNITS_OF[g]):
                        arrived(n)
                        slot = ring[:, n % SLOTS, :]
                        if kind == "N":
                            w = slot.rearrange("p (k n) -> p k n", k=8)
                            for b in range(NB):
                                if b == 1 and part == 0:
                                    pe.wait_ge(s_mcol, summed[0])
                                for k in range(8):
                                    last = mm(PS[:, bank + b, :], lhs[:, 8 * part + k, b * P:(b + 1) * P], w[:, k, :],
                                              start=(part == 0 and k == 0), stop=(part == 1 and k == 7))
                                if part == 1:
                                    last.then_inc(bank_done, 1)
                            if part == 0:
                                last.then_inc(half_used, 1)
                        else:
                            w = slot.rearrange("p (k n) -> p k n", k=KC)
                            if part == 1:
                                pe.wait_ge(s_mcol, summed[0])
                            for h in range(2):
                                for k in range(KC):
                                    last = mm(PS[:, bank + part, h * T:(h + 1) * T], w[:, k, h * P:(h + 1) * P],
                                              lhs[:, k, :], start=(k == 0), stop=(k == KC - 1))
                                    if half_way and (part, h, k) == (1, 0, 0) and g - FIRST[name] in half_way:
                                        last.then_inc(*half_way[g - FIRST[name]])
                            last.then_inc(bank_done, 1)

            def turn(r, blocks=range(NB)):
                for t in range(4 * blocks[0], 4 * blocks[-1] + 4):
                    b, c = t // 4, t % 4
                    pe.wait_ge(s_nat, 2 * r + b + 1)
                    if t >= 4:
                        pe.wait_ge(s_xt, 8 * r + t - 3)
                    for i in range(4):
                        ch = 4 * c + i
                        dst = PS[:, bank_of(r, t), i * P:(i + 1) * P]
                        if r == 2:
                            last = tr(dst, nat[:, b, ch * P:(ch + 1) * P], ident[:])
                        else:
                            rows = nat if r == 1 else xres
                            scale = mix_scale[:, b, max(0, c - 1), :] if r == 1 else row_scale[:, b, :]
                            last = mm(dst, rows[:, b, ch * P:(ch + 1) * P], scale, start=True, stop=True)
                    last.then_inc(s_tp, 1)

            pe.wait_ge(s_const, 1)
            pe.wait_ge(s_rows, 16 * 11)
            tr(PS[:, 4, 0:A_ROWS], rows_a[:], ident[0:A_ROWS, 0:A_ROWS]).then_inc(s_colps, 1)
            tr(PS[:, 5, 0:B_ROWS], rows_b[:], ident[0:B_ROWS, 0:B_ROWS]).then_inc(s_colps, 1)
            tr(PS[:, 6, 0:96], rows_c[:], ident[0:96, 0:96]).then_inc(s_colps, 1)
            pe.wait_ge(s_cols, 3)
            turn(0)
            pe.wait_ge(s_xt, 8)

            def turn_qk(i):
                pe.wait_ge(s_qkn, i + 1)
                if i >= 2:
                    pe.wait_ge(s_qkT, i - 1)
                for h in range(4):
                    last = tr(PS[:, 4 + i % 2, h * P:(h + 1) * P], stage[:, i % 2, h * P:(h + 1) * P], ident[:])
                last.then_inc(s_qktp, 1)

            def turns(one, c):
                if c >= 2:
                    one(2 * c - 4)
                    one(2 * c - 3)

            gemm("q", actT)
            gemm("k", actT, lambda c: turns(turn_qk, c + 2))

            def v_step(c):
                turns(turn_qk, c + 4)
                if c == 0:
                    pe.wait_ge(s_wdt, 16)
                    for b in range(NB):
                        for k in range(KC):
                            last = mm(PS[:, 6, 16 * b:16 * b + 16], actT[:, k, b * P:(b + 1) * P], w_dt[:, k, :],
                                      start=(k == 0), stop=(k == KC - 1))
                    last.then_inc(s_dtps, 1)
                else:
                    pe.wait_ge(s_dt, 1)
                    for b in range(NB):
                        last = mm(PS[:, 6, 16 * b:16 * b + 16], prefix_ones[:], dts[:, 3, b, :], start=True, stop=True)
                    last.then_inc(s_acsps, 1)

            gemm("v", actT, v_step)

            vnat = nat[:, :, 0:1024]

            def sb_logits(t):
                if t == 0:
                    pe.wait_ge(s_qkT, 8)
                    pe.wait_ge(s_acs, 1)
                else:
                    pe.wait_ge(s_att, 1)
                for i in range(4):
                    h = 4 * t + i
                    mm(PS[:, 4 + i, 0:T], kT_a[:, h, 0:P], qT_a[:, h, :], start=True, stop=True)
                    last = mm(PS[:, 4 + i, T:384], kT_a[:, h, P:T], qT_a[:, h, P:T], start=True, stop=True)
                last.then_inc(s_L, 1)

            def sb_later_sums(t):
                pe.wait_ge(s_sp, t + 1)
                for i in range(4):
                    mm(PS[:, 4 + i, 0:384], later_ones[:], sb_sp[:, i, :], start=True, stop=True)
                    last = mm(PS[:, 4 + i, P:T], ones[:], sb_sp[:, i, T:384], start=False, stop=True,
                              skip_group_check=True)
                last.then_inc(s_S, 1)

            def sb_output(t):
                if t == 0:
                    copied(pe, "v")
                pe.wait_ge(s_w, t + 1)
                for i in range(4):
                    h = 4 * t + i
                    hp = slice(i * P, (i + 1) * P)
                    v = slice(h * P, (h + 1) * P)
                    mm(PS[:, 4, hp], sb_l[:, i, 0:P], vnat[:, 0, v], start=True, stop=True)
                    mm(PS[:, 5, hp], sb_l[:, i, P:T], vnat[:, 0, v], start=True, stop=False)
                    last = mm(PS[:, 5, hp], sb_l[:, i, T:384], vnat[:, 1, v], start=False, stop=True)
                last.then_inc(s_O, 1)

            gemm("z", actT, lambda c: (sb_logits, sb_later_sums)[c](0))
            gemm("xbc", actT, lambda c: sb_output(0) if c == 0 else (sb_logits, sb_later_sums)[c - 1](1))
            sb_output(1)

            def head_rows(b):
                for h in range(SSH):
                    last = mm(PS[:, 4 + h // 4, (h % 4) * P:(h % 4 + 1) * P],
                              dts[:, 3, b, h:h + 1].to_broadcast([P, P]), prefix_ones[:], start=True, stop=True)
                last.then_inc(s_R, 1)

            copied(pe, "xbc")
            pe.wait_ge(s_silu, 2)
            for b in range(NB):
                for c in range(8):
                    last = tr(PS[:, 2 - 2 * b + c // 4, (c % 4) * P:(c % 4 + 1) * P],
                              xbcT[:, c, b * P:(b + 1) * P], ident[:])
                last.then_inc(s_xsps, 1)
            pe.wait_ge(s_att, 2)
            head_rows(0)
            pe.wait_ge(s_silu, 3)
            pe.wait_ge(s_xs, 2)
            for g in range(2):
                last = tr(PS[:, 0, g * P:(g + 1) * P], xbcT[:, 8 + g, 0:P], ident[:])
            last.then_inc(s_xsps, 1)
            for b in range(NB):
                for g in range(2):
                    last = mm(PS[:, 2, (2 * b + g) * P:(2 * b + g + 1) * P], xbcT[:, 8 + g, b * P:(b + 1) * P],
                              xbcT[:, 10 + g, b * P:(b + 1) * P], start=True, stop=True)
            last.then_inc(s_cbps, 1)
            pe.wait_ge(s_edgein, 1)
            head_rows(1)
            pe.wait_ge(s_xs, 3)
            pe.wait_ge(s_xf, 2)
            pe.wait_ge(s_edgein, 2)
            for g in range(2):
                last = mm(PS[:, 4 + g, :], b_nat[:, g * P:(g + 1) * P], x_end[:, g * 512:(g + 1) * 512],
                          start=True, stop=True)
            last.then_inc(s_stps, 1)
            for b in range(NB):
                pe.wait_ge(s_sc, b + 1)
                if b == 1:
                    banks_free(FIRST["mix"])
                    banks_free(FIRST["mix"] + 1)
                for h in range(SSH):
                    bank = (6 if b == 0 else 0) + h // 8
                    last = mm(PS[:, bank, (h % 8) * 64:(h % 8 + 1) * 64], decay[:, b, h, :],
                              x_dt[:, b, h * 64:(h + 1) * 64], start=True, stop=True)
                last.then_inc(s_yd, 1)
            pe.wait_ge(s_cb, 1)
            pe.wait_ge(s_st, 1)
            for g in range(2):
                last = mm(PS[:, 2 + g, :], xbcT[:, 10 + g, P:T], states[:, g * 512:(g + 1) * 512],
                          start=True, stop=True)
            last.then_inc(s_yo, 1)

            turn(1)
            pe.wait_ge(s_xt, 16)

            def keys_turn(c):
                if c != 2:
                    return
                pe.wait_ge(s_keys, 16)
                for t in range(4):
                    for i in range(4):
                        last = tr(PS[:, 4 + t, i * P:(i + 1) * P], keys_nat[:, 4 * t + i, :], ident[:])
                last.then_inc(s_ktps, 1)

            gemm("mix", actT, keys_turn)

            pe.wait_ge(s_kt, 1)
            turn(2)
            pe.wait_ge(s_xt, 24)

            def peer_scores(b, slots, freed):
                for n, s in enumerate(slots):
                    last = mm(PS[:, 4 + s // 4, (s % 4) * P:(s % 4 + 1) * P], queryT[:, s, b * P:(b + 1) * P],
                              keysT[:, s, :], start=True, stop=True)
                    if n == 0 and freed:
                        last.then_inc(s_up, freed)
                last.then_inc(s_scps, 1)

            def first_scores(c):
                if c >= 1:
                    g = FIRST["query"] + c - 1
                    for i in range(2):
                        pe.wait_ge(bank_free[2 * (g % 2) + i], g // 2 + 1)
                    peer_scores(0, range(4 * c - 4, 4 * c), 2 if c == 3 else 0)

            gemm("query", actT, first_scores, {2: (s_up, 4), 3: (s_up, 2)})
            copied(pe, "query")
            peer_scores(0, range(12, 16), 0)
            pe.wait_ge(s_psc, 4)
            peer_scores(1, range(16), 0)
            pe.wait_ge(s_psc, 5)

            banks_free(FIRST["pv"])
            banks_free(FIRST["pv"] + 1)
            mod_sums(FIRST["pv"] - 1, 3)
            gate_turn(0, 2)
            pe.wait_ge(s_grow, 1)
            def up_rows(H, whole=TOPK):
                for k in range(TOPK):
                    pe.wait_ge(s_diag, H * 16 + (k + 1))
                    pe.wait_ge(landed[k % 8], H * 64 + 16 * (3 + k // 8))
                    for n in range(4 if k < whole else 3):
                        last = mm(PS[:, 4 + n, :], diag[:, k % 4, :], gather_buf[k % 8][:, n * 512:(n + 1) * 512],
                                  start=False, stop=True, skip_group_check=True)
                    last.then_inc(s_up, 1)

            for b in range(NB):
                if b:
                    pe.wait_ge(s_resu, 1)
                for n in range(4):
                    mm(PS[:, 4 + n, :], ident[:], xres[:, b, n * 512:(n + 1) * 512], start=True, stop=True)
                with pe.Fori(0, PH // 2 - b) as j:
                    for e in range(2):
                        up_rows(j * 2 + (PH * b + e))
            turn(3, [0])
            up_rows(NB * PH - 2)
            up_rows(NB * PH - 1, 8)

            turn(3, [1])
            pe.wait_ge(s_xt, 32)
            gemm("pv", actT)
            gemm("pg", actT)
            for i in range(4):
                g = FIRST["grp"] + i
                pe.wait_ge(s_pool_T, i + 1)
                banks_free(g)
                mod_sums(g - 2, 2 * (g % 2) + 1)
                n = UNITS_OF[FIRST["grp"] + (i // 2) * 2][0]
                arrived(n)
                w = ring[:, n % SLOTS, :].rearrange("p (g k n) -> p g k n", g=2, k=4)[:, i % 2]
                for o in range(4):
                    if o == 2:
                        pe.wait_ge(s_mcol, summed[0])
                    for k in range(4):
                        last = mm(PS[:, 2 * (g % 2) + o // 2, (o % 2) * T:(o % 2 + 1) * T], w[:, k, o * P:(o + 1) * P],
                                  poolT[:, 4 * i + k, :], start=(k == 0), stop=(k == 3))
                    if o % 2:
                        last.then_inc(bank_done, 1)
            copied(pe, "grp")
            gemm("po", pgateT)
            banks_free(FIRST["aq"])
            banks_free(FIRST["aq"] + 1)
            mod_sums(FIRST["aq"] - 1, 3)
            turn(4)
            pe.wait_ge(s_xt, 40)

            def turn_rope(i):
                pe.wait_ge(s_rope, i + 1)
                if i >= 2:
                    pe.wait_ge(s_rT, i - 1)
                for h in range(4):
                    last = tr(PS[:, 4 + i % 2, h * P:(h + 1) * P], stage[:, i % 2, h * P:(h + 1) * P], ident[:])
                last.then_inc(s_rtp, 1)

            def query_step(c):
                turns(turn_rope, c)
                if c == 1:
                    gate_turn(1, 6)

            def index_keys():
                pe.wait_ge(s_wsmall, 16)
                pe.wait_ge(s_grow, 2)
                for b in range(NB):
                    for k in range(KC):
                        last = mm(PS[:, 6, 80 * b:80 * b + 80], actT[:, k, b * P:(b + 1) * P], w_small[:, k, :],
                                  start=(k == 0), stop=(k == KC - 1))
                last.then_inc(s_kips, 1)

            def index_keys_turn():
                pe.wait_ge(s_kirope, 1)
                for b in range(NB):
                    last = tr(PS[:, 7, b * P:(b + 1) * P], ki_wi[:, b, 0:P], ident[:])
                last.then_inc(s_kitp, 1)

            def index_scores(part_of):
                pe.wait_ge(s_kiT, 1)
                pe.wait_ge(s_rT, 20)
                for i in range(8 * part_of, 8 * part_of + 8):
                    b, h = i // IH, i % IH
                    if i >= 4:
                        pe.wait_ge(s_relu, i - 3)
                    part = slice(64 * (h % 2), 64 * (h % 2) + 64)
                    mm(PS[:, 4 + i % 4, 0:P * (b + 1)], qiT[part, h // 2, b * P:(b + 1) * P],
                       kiT[part, 0:P * (b + 1)], start=True, stop=True).then_inc(s_ips, 1)

            def gate_step(c):
                if c == 0:
                    index_keys()
                if c < 2:
                    turns(turn_rope, c + 10)
                if c == 1:
                    index_keys_turn()
                if c >= 2:
                    index_scores(c - 2)

            gemm("aq", actT, query_step)
            gemm("ak", actT, lambda c: turns(turn_rope, c + 4))
            gemm("ai", actT, lambda c: turns(turn_rope, c + 8))
            gemm("ag", actT, gate_step)
            gemm("av", actT, lambda c: index_scores(c + 2) if c < 2 else None)
            pe.wait_ge(s_relu, 2 * IH)
            copied(pe, "av")

            def logits(h):
                if h >= 2:
                    pe.wait_ge(s_lm, 2 * (h - 1))
                mm(PS[:, 4 + h % 2, 0:P], qT_b[:, h, 0:P], kT_b[:, h, 0:P], start=True, stop=True)
                mm(PS[:, 4 + h % 2, P:384], qT_b[:, h, P:T], kT_b[:, h, :], start=True, stop=True).then_inc(s_lps, 1)

            def values(h):
                pe.wait_ge(s_pn, h + 1)
                if h >= 2:
                    pe.wait_ge(s_pT, h - 1)
                for i in range(3):
                    last = tr(PS[:, 6 + h % 2, i * P:(i + 1) * P], pr[:, h % 2, i * P:(i + 1) * P], ident[:])
                last.then_inc(s_ptps, 1)

            def outputs(h):
                bank = h % 2
                pe.wait_ge(s_pT, h + 1)
                if h >= 2:
                    pe.wait_ge(s_oT, h - 1)
                mm(PS[:, bank, 0:T], nat[:, 0, h * P:(h + 1) * P], prT[:, h % 2, 0:T], start=True, stop=True)
                mm(PS[:, bank, P:T], nat[:, 1, h * P:(h + 1) * P], prT[:, h % 2, T:384], start=False, stop=True,
                   skip_group_check=True).then_inc(s_ops, 1)

            logits(0)
            for h in range(NH + 2):
                if h + 1 < NH:
                    logits(h + 1)
                if 1 <= h <= NH:
                    values(h - 1)
                if h >= 2:
                    outputs(h - 2)
            pe.wait_ge(s_oT, NH)
            gemm("ao", agateT)

        @block.scalar
        def _(act):
            step, mark = counted(act, s_act)
            A = nc.scalar.activation
            for dst, src, n in (
                (rows_a[A_NORM:A_NORM + 16], a["attn_norm"], 16),
                (rows_a[A_MIX:A_MIX + 8], a["sb_out_norm"], 8),
                (rows_a[A_MIX + 8:A_MIX + 16], a["ssd_out_norm"], 8),
                (rows_a[A_Q:A_Q + 1], a["sb_q_norm"], 1),
                (rows_a[A_K:A_K + 1], a["sb_k_norm"], 1),
                (rows_a[A_CB:A_CB + 12], a["conv_b"], 12),
            ):
                act.dma_start(dst, src.rearrange("a (c p) -> (a c) p", p=P)).then_inc(s_rows, 16)
            act.dma_start(rows_a[A_CW:A_CW + 48], a["conv_w"].rearrange("a w i (c p) -> (a w i c) p", p=P)).then_inc(s_rows, 16)
            act.dma_start(rows_b[B_NORM:B_NORM + 32], a["norm_g_2"].rearrange("l (c p) -> (l c) p", p=P)).then_inc(s_rows, 16)
            act.dma_start(rows_b[B_SCALE:B_SCALE + 16], a["pool_scale_2"].rearrange("l (c p) -> (l c) p", p=P)).then_inc(s_rows, 16)
            act.dma_start(rows_b[B_COND:B_COND + 16], a["c_2"].rearrange("l (c p) -> (l c) p", p=P)).then_inc(s_rows, 16)
            act.dma_start(rows_c[:], a["mod_b_2"].rearrange("l (c p) -> (l c) p", p=P)).then_inc(s_rows, 16)
            copied_mods = [0]

            def mod_columns(g, bank):
                if mods_until(g) > copied_mods[0]:
                    act.wait_ge(s_msum, mods_until(g))
                for i in range(copied_mods[0], mods_until(g)):
                    mark(A(mod_cols[:, 2 * i:2 * i + 2], PS[:, bank, 2 * (i % MOD_BUFS):2 * (i % MOD_BUFS) + 2], ACT.Copy), s_mcol)
                copied_mods[0] = max(copied_mods[0], mods_until(g))

            def mods(g):
                mod_columns(g - 2, 2 * (g % 2) + 1)

            def gate_row(layer, bank):
                act.wait_ge(s_gateps, layer + 1)
                if layer:
                    act.wait_ge(s_gst, 16)
                step(A(gate_rows, PS[0:16, bank, 0:P], ACT.Copy), s_grow)
                act.dma_start(gate_dram[layer:layer + 1, :].rearrange("l (c p) -> (l c) p", p=P), gate_rows).then_inc(s_gst, 16)

            def squares(b):
                mark(A(act_flat[:, b * D:(b + 1) * D], xres[:, b, :], ACT.Square, accum_out=ssq[:, b:b + 1]), s_ssq)

            def squares_of_quarter(c, trash, ready):
                for b in range(NB):
                    ready(b)
                    step(A(trash, xres[:, b, c * 512:(c + 1) * 512], ACT.Square, accum_out=ssq_part[:, b, c:c + 1]), s_ssq)

            def row_roots(r):
                if r == 0:
                    act.wait_ge(s_ssq, SQUARES[r])
                else:
                    act.wait_ge(s_ssum, (2, 4, 5).index(r) + 1)
                mark(A(root[:, 0:2], ssq[:, 0:2], ACT.Sqrt, bias=const[:, 0:1], scale=1.0 / D), s_root)

            def copy_banks(name, dst, before=None):
                n = next(x[3] for x in STAGES if x[0] == name)
                for c in range(n):
                    g = FIRST[name] + c
                    mods(g)
                    if before is not None:
                        before(c)
                    for b in range(NB):
                        act.wait_ge(bank_done, done(g, b))
                        A(dst(c, b), PS[:, 2 * (g % 2) + b, :], ACT.Copy).then_inc(bank_free[2 * (g % 2) + b], 1)

            act.wait_ge(s_const, 1)
            act.wait_ge(s_in, 16 * NB)
            for b in range(NB):
                squares(b)
            row_roots(0)
            for i, k in enumerate(("dt_bias", "a_log", "d_skip")):
                act.dma_start(bc16[:, i, :], spread(a[k], 16)).then_inc(s_bc, 16)
            act.dma_start(pos_i[:], a["positions_2"].rearrange("a (b p) -> p (a b)", p=P),
                          allow_slow_non_contiguous=True).then_inc(s_bc, 16)
            act.dma_start(w_dt, a["w_in"][0, :, 5632:5648].rearrange("(k p) n -> p k n", p=P)).then_inc(s_wdt, 16)
            act.wait_ge(s_cols, 2)
            mark(A(cond[:], cols_b[:, B_COND:B_COND + 16], ACT.Silu), s_cond)

            def qk_stage(i):
                g = FIRST["q"] + i // 2
                if i % 2 == 0:
                    mods(g + 1)
                act.wait_ge(bank_done, done(g, i % 2))
                if i >= 2:
                    act.wait_ge(s_qktp, i - 1)
                A(stage[:, i % 2, :], PS[:, 2 * (g % 2) + i % 2, :], ACT.Copy).then_inc(bank_free[2 * (g % 2) + i % 2], 1)
                act.wait_ge(bank_free[2 * (g % 2) + i % 2], g // 2 + 1)
                mark(A(square, stage[:, i % 2, :], ACT.Square), s_qkst)
                act.wait_ge(s_qkss, i + 1)
                mark(A(hstat[:, 1, :], hstat[:, 0, :], ACT.Sqrt, bias=const[:, 0:1], scale=1.0 / P), s_qkrt)

            for i in range(8):
                qk_stage(i)
            act.wait_ge(s_dtst, 2)
            step(A(dts[:, 1], dts[:, 1], ACT.Exp))
            step(A(bc16[:, 1, :], bc16[:, 1, :], ACT.Exp))
            mark(A(dts[:, 2], dts[:, 1], ACT.Ln, bias=const[:, 1:2]), s_dtl)
            copy_banks("v", lambda c, b: nat[:, b, c * 512:(c + 1) * 512])

            def silu_z(c):
                g = FIRST["z"] + c
                mods(g)
                for b in range(NB):
                    act.wait_ge(bank_done, done(g, b))
                    A(nat[:, b, 1024 + c * 512:1536 + c * 512], PS[:, 2 * (g % 2) + b, :], ACT.Silu
                      ).then_inc(bank_free[2 * (g % 2) + b], 1)

            def pad_xbc(c):
                g = FIRST["xbc"] + c
                mods(g)
                for u in range(2):
                    i = 2 * c + u
                    act.wait_ge(bank_done, done(g, u))
                    if i >= PADS:
                        act.wait_ge(s_conv, i - PADS + 1)
                    A(xpad[:, i % PADS, :, 3:], PS[:, 2 * (g % 2) + u, :].rearrange("p (h t) -> p h t", h=2), ACT.Copy
                      ).then_inc(bank_free[2 * (g % 2) + u], 1)

            def silu_xbc(c):
                act.wait_ge(s_conv, 2 * c + 2)
                mark(A(xbcT[:, 4 * c:4 * c + 4, :], xbcT[:, 4 * c:4 * c + 4, :], ACT.Silu), s_silu)

            def sb_log1p(t):
                act.wait_ge(s_neg, t + 1)
                step(A(sb_e, sb_e, ACT.Exp))
                mark(A(sb_e, sb_e, ACT.Ln, bias=const[:, 1:2]), s_ln)

            def sb_weights(t):
                act.wait_ge(s_w0, t + 1)
                mark(A(sb_l, sb_l, ACT.Exp), s_w1)

            def sb_out(t):
                act.wait_ge(s_O, t + 1)
                mark(A(nat[:, :, 512 * t:512 * t + 512], PS[:, 4:6, :], ACT.Copy), s_att)

            sb_log1p(0)
            silu_z(0)
            sb_weights(0)
            silu_z(1)
            sb_out(0)
            act.wait_ge(s_xpad, 1)
            pad_xbc(0)
            sb_log1p(1)
            pad_xbc(1)
            silu_xbc(0)
            sb_weights(1)
            silu_xbc(1)
            pad_xbc(2)
            sb_out(1)
            for b in range(NB):
                act.wait_ge(s_xsps, b + 1)
                mark(A(xs_nat[:, b, :], PS[:, 2 - 2 * b:4 - 2 * b, :].rearrange("p c n -> p (c n)"), ACT.Copy), s_xs)
            act.wait_ge(s_att, 2)
            for b in range(NB):
                step(A(spare, nat[:, b, 0:1024], ACT.Square, accum_out=ssq[:, 6 + 3 * b:7 + 3 * b]))
            silu_xbc(2)
            act.dma_start(wide[:], spread(a["ffn_norm"], D)).then_inc(s_wide, 16)
            act.wait_ge(s_xsps, 3)
            mark(A(b_nat, PS[:, 0, 0:256], ACT.Copy), s_xs)
            for b in range(NB):
                act.wait_ge(s_seg, b + 1)
                mark(A(decay[:, b], decay[:, b], ACT.Exp), s_dec)
                act.wait_ge(s_edgein, b + 1)
                mark(A(ds_out[:, 2 + b, :], ds_out[:, b, :], ACT.Exp), s_edge)
            act.wait_ge(s_stps, 1)
            mark(A(states, PS[:, 4:6, :].rearrange("p c n -> p (c n)"), ACT.Copy), s_st)
            for b in range(NB):
                act.wait_ge(s_y, b + 1)
                for i in range(2):
                    step(A(spare[:, 0:512], nat[:, b, 1024 + 512 * i:1536 + 512 * i], ACT.Square,
                           accum_out=ssq[:, 7 + 3 * b + i:8 + 3 * b + i]))
            sums6, roots6 = [x[:, 6:12].rearrange("p (b g) -> p b g", b=NB) for x in (ssq, root)]
            mark(A(roots6[:, :, 0], sums6[:, :, 0], ACT.Sqrt, bias=const[:, 0:1], scale=1.0 / 1024), s_root)
            mark(A(roots6[:, :, 1:3], sums6[:, :, 1:3], ACT.Sqrt, bias=const[:, 0:1], scale=1.0 / 512), s_root)
            act.wait_ge(s_y, 2)
            act.dma_start(keys_nat, a["peer_sub_keys"][0].rearrange("h c k d -> k (h c) d")).then_inc(s_keys, 16)
            for c in range(4):
                mods(FIRST["mix"] + c)
                if c == 1:
                    act.wait_ge(s_ktps, 1)
                    mark(A(keysT, PS[:, 4:8, :].rearrange("p c (s k) -> p (c s) k", k=P), ACT.Copy), s_kt)
                g = FIRST["mix"] + c
                squares_of_quarter(c, big[:, 0:512], lambda b: act.wait_ge(bank_free[2 * (g % 2) + b], g // 2 + 1))
            row_roots(2)
            for c in range(4):
                g = FIRST["query"] + c
                mods(g)
                for u in range(2):
                    act.wait_ge(bank_done, done(g, u))
                    s = 4 * c + 2 * u
                    A(queryT[:, s:s + 2, :], PS[:, 2 * (g % 2) + u, :].rearrange("p (h t) -> p h t", h=2), ACT.Copy
                      ).then_inc(bank_free[2 * (g % 2) + u], 1)
                act.wait_ge(s_scps, c + 1)
                mark(A(scores[:, 4 * c:4 * c + 4, :], PS[:, 4 + c, :].rearrange("p (s k) -> p s k", k=P), ACT.Copy), s_psc)
            act.wait_ge(s_scps, 5)
            mark(A(scores[:, 16:32, :], PS[:, 4:8, :].rearrange("p c (s k) -> p (c s) k", k=P), ACT.Copy), s_psc)
            mod_columns(FIRST["pv"] - 1, 3)
            gate_row(0, 2)
            act.wait_ge(s_angle, 1)
            mark(A(sine[:], ang[:, 2], ACT.Sin), s_trig)
            mark(A(cosine[:], ang[:, 3], ACT.Sin, scale=-1.0, bias=const[:, 2:3]), s_trig)
            for b in range(NB):
                with act.Fori(0, PH // 2) as j:
                    for e in range(2):
                        H = j * 2 + (PH * b + e)
                        act.wait_ge(s_gin, H + 1)
                        A(gates[:, e, :], gates[:, e, :], ACT.Exp).then_inc(s_gex, 1)
                        act.wait_ge(s_down, H * 16 + 16)
                        A(gelu[:, e, :], dots[:, e, :], ACT.Gelu).then_inc(s_gelu, 1)
                        act.wait_ge(s_wt, H + 1)
                        for k in range(16):
                            act.wait_ge(s_up, H * 16 + (8 + k - 3))
                            A(diag[:, k % 4, :], ident[:], ACT.Copy, scale=weight[:, e, k:k + 1]).then_inc(s_diag, 1)
                act.wait_ge(s_up, 8 + UPS * (b + 1))
                n = 4 - b
                mark(A(xres[:, b, 0:n * 512], PS[:, 4:4 + n, :].rearrange("p c n -> p (c n)"), ACT.Copy), s_resu)
                act.wait_ge(s_resu, b + 1)
                if b:
                    act.wait_ge(s_tailed, 1)
                step(A(big[:, b * D:(b + 1) * D], xres[:, b, :], ACT.Square, accum_out=ssq[:, b:b + 1]), s_ssq)
                mark(A(root[:, b:b + 1], ssq[:, b:b + 1], ACT.Sqrt, bias=const[:, 0:1], scale=1.0 / D), s_root)
            act.wait_ge(s_gst, 16)
            act.dma_start(wide[:], spread(gate_dram[0:1, :], D)).then_inc(s_wide, 16)
            for c in range(4):
                g = FIRST["pv"] + c
                mods(g)
                for u in range(2):
                    act.wait_ge(bank_done, done(g, u))
                    s = 4 * c + 2 * u
                    A(poolT[:, s:s + 2, :], PS[:, 2 * (g % 2) + u, :].rearrange("p (h t) -> p h t", h=2), ACT.Copy
                      ).then_inc(bank_free[2 * (g % 2) + u], 1)
            for c in range(4):
                g = FIRST["pg"] + c
                mods(g)
                for u in range(2):
                    act.wait_ge(bank_done, done(g, u))
                    s = 4 * c + 2 * u
                    A(pgateT[:, s:s + 2, :], PS[:, 2 * (g % 2) + u, :].rearrange("p (h t) -> p h t", h=2), ACT.Silu
                      ).then_inc(bank_free[2 * (g % 2) + u], 1)
            for name in ("grp", "po"):
                for c in range(4):
                    mods(FIRST[name] + c)
                    if name == "po":
                        squares_of_quarter(c, big[:, 0:512], lambda b: act.wait_ge(s_res, 2 + 2 * c + b))
            mod_columns(FIRST["aq"] - 1, 3)
            row_roots(4)
            act.dma_start(w_small, a["attn_w_in_2"][0, :, 9216:9296].rearrange("(k p) n -> p k n", p=P)).then_inc(s_wsmall, 16)
            def rope_stage(i, g):
                act.wait_ge(bank_done, done(g, i % 2))
                if i >= 2:
                    act.wait_ge(s_rtp, i - 1)
                A(stage[:, i % 2, :], PS[:, 2 * (g % 2) + i % 2, :], ACT.Copy).then_inc(bank_free[2 * (g % 2) + i % 2], 1)

            def rope_T(i):
                act.wait_ge(s_rtp, i + 1)
                b, c = i % 2, i // 2
                dst = (qT_b if c < 4 else kT_b)[:, 4 * (c % 4):4 * (c % 4) + 4, b * P:(b + 1) * P] if i < 16 else \
                    qiT[:, 4 * (c - 8):4 * (c - 8) + 4, b * P:(b + 1) * P]
                mark(A(dst, PS[:, 4 + i % 2, :].rearrange("p (h t) -> p h t", h=4), ACT.Copy), s_rT)

            def relus(part_of):
                for i in range(8 * part_of, 8 * part_of + 8):
                    S = P * (i // IH + 1)
                    act.wait_ge(s_ips, i + 1)
                    if i >= 2:
                        act.wait_ge(s_iuse, i - 1)
                    mark(A(relu[:, i % 2, 0:S], PS[:, 4 + i % 4, 0:S], ACT.Relu), s_relu)

            for i in range(20):
                if i == 2:
                    gate_row(1, 6)
                rope_stage(i, FIRST["aq"] + i // 2)
                if i == 19:
                    act.wait_ge(s_kips, 1)
                    mark(A(ki_wi[:, :, 0:64], PS[:, 6, 0:160].rearrange("p (b n) -> p b n", b=2)[:, :, 0:64], ACT.Copy), s_kist)
                    mark(A(ki_wi[:, :, 128:144], PS[:, 6, 0:160].rearrange("p (b n) -> p b n", b=2)[:, :, 64:80], ACT.Copy,
                           scale=float(IH ** -0.5 * 64 ** -0.5)), s_kist)
                if i >= 1:
                    rope_T(i - 1)
            rope_T(19)
            act.wait_ge(s_kitp, 1)
            mark(A(kiT, PS[:, 7, 0:T], ACT.Copy), s_kiT)
            for c in range(4):
                g = FIRST["ag"] + c
                if c >= 2:
                    relus(c - 2)
                for u in range(2):
                    act.wait_ge(bank_done, done(g, u))
                    s = 4 * c + 2 * u
                    A(agateT[:, s:s + 2, :], PS[:, 2 * (g % 2) + u, :].rearrange("p (h t) -> p h t", h=2), ACT.Silu
                      ).then_inc(bank_free[2 * (g % 2) + u], 1)
            copy_banks("av", lambda c, b: nat[:, b, c * 512:(c + 1) * 512], lambda c: relus(c + 2) if c < 2 else None)
            act.wait_ge(s_relu, 2 * IH)
            act.wait_ge(s_gst, 32)
            act.dma_start(wide[:], spread(gate_dram[1:2, :], D)).then_inc(s_wide, 16)

            def exps(h):
                e = h % 2
                for b in range(NB):
                    act.wait_ge(s_lm, 2 * h + b + 1)
                    if h >= 2 and b == 0:
                        act.wait_ge(s_ptps, h - 1)
                    s = slice(0, P) if b == 0 else slice(P, 384)
                    mark(A(pr[:, e, s], lm[:, e, s], ACT.Exp, bias=smax[:, e, b:b + 1], accum_out=ssum[:, e, b:b + 1]), s_pe)

            def probs_T(h):
                act.wait_ge(s_ptps, h + 1)
                if h >= 2:
                    act.wait_ge(s_ops, h - 1)
                mark(A(prT[:, h % 2, :], PS[:, 6 + h % 2, 0:384], ACT.Copy), s_pT)

            for h in range(NH + 1):
                if h < NH:
                    exps(h)
                if h >= 1:
                    probs_T(h - 1)
            act.wait_ge(s_lps, NH)
            act.dma_start(final_gain, spread(a["final_g_2"], D)).then_inc(s_fin, 16)
            for c in range(4):
                squares_of_quarter(c, big[:, 4096:4608], lambda b: act.wait_ge(s_res, 10 + 2 * c + b))
            row_roots(5)

        @block.vector
        def _(dve):
            step, mark = counted(dve, s_dve)
            v = nc.vector
            TT, TS, STT = v.tensor_tensor, v.tensor_scalar, v.scalar_tensor_tensor

            dve.wait_ge(s_colps, 1)
            mark(v.tensor_copy(cols_a[:], PS[:, 4, 0:A_ROWS]), s_cols)
            dve.wait_ge(s_colps, 3)
            mark(v.tensor_copy(cols_b[:], PS[:, 5, 0:B_ROWS]), s_cols)
            mark(v.tensor_copy(cols_c[:], PS[:, 6, 0:96]), s_cols)
            dve.wait_ge(s_cols, 3)

            def weigh(g):
                for n in MODS_OF.get(g, []):
                    i = UNITS[n][3]
                    dve.wait_ge(s_cond, 1)
                    dve.wait_ge(unit_in[n % SLOTS], 16 * (n // SLOTS + 1))
                    if i >= MOD_BUFS:
                        dve.wait_ge(s_msum, i - MOD_BUFS + 1)
                    w, acc = ring[:, n % SLOTS, :].rearrange("p (k n) -> p k n", k=KC), mod_acc[:, i % MOD_BUFS, :]
                    step(TS(acc, w[:, 0, :], cond[:, 0:1], None, ALU.mult))
                    for k in range(1, KC):
                        ins = STT(out=acc, in0=w[:, k, :], scalar=cond[:, k:k + 1], in1=acc, op0=ALU.mult, op1=ALU.add)
                        if k < KC - 1:
                            step(ins)
                        else:
                            mark(ins, s_modw)

            def mod_ready(layer):
                dve.wait_ge(s_mcol, 24 * (layer + 1))
                cols = slice(48 * layer, 48 * layer + 48)
                step(TT(mod_cols[:, cols], mod_cols[:, cols], cols_c[:, cols], ALU.add))
                step(STT(out=mod_gain[:, layer, :], in0=mod_cols[:, 48 * layer + 16:48 * layer + 32], scalar=1.0,
                         in1=cols_b[:, B_NORM + 16 * layer:B_NORM + 16 * layer + 16], op0=ALU.add, op1=ALU.mult), s_modc)

            def sum_quarters(r):
                dve.wait_ge(s_ssq, SQUARES[r])
                mark(v.tensor_reduce(ssq[:, 0:2], ssq_part[:], AX, ALU.add), s_ssum)

            def norm_rows(r):
                dve.wait_ge(s_root, ROOTS[r])
                step(v.reciprocal(rinv[:, 0:2], root[:, 0:2]))
                for b in range(NB):
                    if r == 2:
                        dve.wait_ge(s_wide, 16)
                        mark(STT(out=nat[:, b, :], in0=xres[:, b, :], scalar=rinv[:, b:b + 1], in1=wide[:],
                                 op0=ALU.mult, op1=ALU.mult), s_nat)
                    else:
                        mark(TS(row_scale[:, b, :], ident[:], rinv[:, b:b + 1], None, ALU.mult), s_nat)

            def take_T(r, gain, shift=None, blocks=range(NB)):
                for t in range(4 * blocks[0], 4 * blocks[-1] + 4):
                    b, c = t // 4, t % 4
                    dve.wait_ge(s_tp, 8 * r + t + 1)
                    dst = actT[:, 4 * c:4 * c + 4, b * P:(b + 1) * P]
                    src = PS[:, bank_of(r, t), :].rearrange("p (c t) -> p c t", c=4)
                    if gain is None:
                        mark(v.tensor_copy(dst, src), s_xt)
                        continue
                    per_channel = [x[:, 4 * c:4 * c + 4].unsqueeze(2).to_broadcast([P, 4, P]) for x in (gain, shift) if x is not None]
                    if shift is None:
                        mark(TT(dst, src, per_channel[0], ALU.mult), s_xt)
                    else:
                        step(TT(dst, src, per_channel[0], ALU.mult))
                        mark(TT(dst, dst, per_channel[1], ALU.add), s_xt)

            norm_rows(0)
            take_T(0, cols_a[:, A_NORM:A_NORM + 16])

            def qk_T(i):
                g, b = i // 2, i % 2
                dve.wait_ge(s_qktp, i + 1)
                dst = (qT_a if g < 2 else kT_a)[:, 4 * (g % 2):4 * (g % 2) + 4, b * P:(b + 1) * P]
                col = A_Q if g < 2 else A_K
                mark(TS(dst, PS[:, 4 + i % 2, :].rearrange("p (h t) -> p h t", h=4), cols_a[:, col:col + 1], None,
                        ALU.mult), s_qkT)

            def dt_steps():
                dve.wait_ge(s_dtps, 1)
                dve.wait_ge(s_bc, 64)
                mark(TT(dts[:, 0], PS[:, 6, 0:32].rearrange("p (b h) -> p b h", b=2),
                        bc16[:, 0, :].unsqueeze(1).to_broadcast([P, 2, 16]), ALU.add), s_dtst)
                dve.wait_ge(s_dtst, 1)
                mark(STT(out=dts[:, 1], in0=dts[:, 0], scalar=-1.0, in1=dts[:, 0], op0=ALU.mult, op1=ALU.min), s_dtst)
                dve.wait_ge(s_dtl, 1)
                step(STT(out=dts[:, 2], in0=dts[:, 0], scalar=0.0, in1=dts[:, 2], op0=ALU.max, op1=ALU.add))
                mark(STT(out=dts[:, 3], in0=dts[:, 2], scalar=-1.0, in1=bc16[:, 1, :].unsqueeze(1).to_broadcast([P, 2, 16]),
                         op0=ALU.mult, op1=ALU.mult), s_dt)

            weigh(FIRST["q"])
            for i in range(8):
                dve.wait_ge(s_qkst, i + 1)
                mark(v.tensor_reduce(hstat[:, 0, :], square.rearrange("p (h n) -> p h n", h=4), AX, ALU.add), s_qkss)
                dve.wait_ge(s_qkrt, i + 1)
                step(v.reciprocal(hstat[:, 2, :], hstat[:, 1, :]))
                st = stage[:, i % 2, :].rearrange("p (h n) -> p h n", h=4)
                mark(TT(st, st, hstat[:, 2, :].unsqueeze(2).to_broadcast([P, 4, P]), ALU.mult), s_qkn)
                if i == 7:
                    dt_steps()
                if i % 2:
                    if i >= 3:
                        qk_T(i - 3)
                        qk_T(i - 2)
                    if i < 7:
                        weigh(FIRST["q"] + (i + 1) // 2)
            weigh(FIRST["v"])
            qk_T(6)
            qk_T(7)
            dve.wait_ge(s_acsps, 1)
            step(v.tensor_copy(dts[:, 4], PS[:, 6, 0:32].rearrange("p (b h) -> p b h", b=2)), s_acs)
            mask4 = sb_mask[:].unsqueeze(1).to_broadcast([P, 4, 384])
            L = PS[:, 4:8, 0:384]

            def sb_softplus(t):
                dve.wait_ge(s_L, t + 1)
                step(TS(sb_l, L, float(P ** -0.5), None, ALU.mult))
                mark(STT(out=sb_e, in0=sb_l, scalar=-1.0, in1=sb_l, op0=ALU.mult, op1=ALU.min), s_neg)
                dve.wait_ge(s_ln, t + 1)
                step(STT(out=sb_sp, in0=sb_l, scalar=0.0, in1=sb_e, op0=ALU.max, op1=ALU.add))
                mark(TT(sb_sp, sb_sp, mask4, ALU.mult), s_sp)
                step(STT(out=sb_l, in0=sb_l, scalar=0.0, in1=sb_e, op0=ALU.min, op1=ALU.subtract))

            def sb_exponents(t):
                dve.wait_ge(s_S, t + 1)
                mark(TT(sb_l, sb_l, L, ALU.subtract), s_w0)
                dve.wait_ge(s_w1, t + 1)
                mark(TT(sb_l, sb_l, mask4, ALU.mult), s_w)

            def convolve(chunk):
                g = FIRST["xbc"] + chunk
                for u in range(2):
                    i = 2 * chunk + u
                    dve.wait_ge(bank_free[2 * (g % 2) + u], g // 2 + 1)
                    for h in range(2):
                        c = 2 * i + h

                        def w(tap):
                            return cols_a[:, A_CW + XC * tap + c:A_CW + XC * tap + c + 1]
                        pad = xpad[:, i % PADS, h, :]
                        step(TS(xbcT[:, c, :], pad[:, 3:], w(3), cols_a[:, A_CB + c:A_CB + c + 1], ALU.mult, ALU.add))
                        for tap in (2, 1, 0):
                            ins = STT(out=xbcT[:, c, :], in0=pad[:, tap:tap + T], scalar=w(tap), in1=xbcT[:, c, :],
                                      op0=ALU.mult, op1=ALU.add)
                            if tap == 0 and h == 1:
                                mark(ins, s_conv)
                            else:
                                step(ins)

            mark(v.memset(xpad[:, :, :, 0:3], 0.0), s_xpad)
            weigh(FIRST["v"] + 1)
            sb_softplus(0)
            weigh(FIRST["z"])
            sb_exponents(0)
            weigh(FIRST["z"] + 1)
            weigh(FIRST["xbc"])
            sb_softplus(1)
            dve.wait_ge(s_xpad, 1)
            convolve(0)
            weigh(FIRST["xbc"] + 1)
            sb_exponents(1)
            convolve(1)
            convolve(2)
            dve.wait_ge(s_xs, 2)
            mark(TT(x_dt.rearrange("p b (h n) -> p (b h) n", n=64), xs_nat.rearrange("p b (h n) -> p (b h) n", n=64),
                    dts[:, 2].rearrange("p b h -> p (b h)").unsqueeze(2).to_broadcast([P, 32, 64]), ALU.mult), s_xf)
            for b in range(NB):
                dve.wait_ge(s_R, b + 1)
                R = PS[:, 4:8, :].rearrange("p c (h l) -> p (c h) l", l=P)
                step(TT(decay[:, b], R, dts[:, 4, b, :].unsqueeze(2).to_broadcast([P, 16, P]), ALU.subtract))
                mark(TS(decay[:, b], decay[:, b], 0.0, None, ALU.min), s_seg)
                if b == 0:
                    mark(TT(ds_out[:, 0, :], R[:, :, P - 1:P].rearrange("p h o -> p (h o)"), dts[:, 4, 0, :], ALU.subtract), s_edgein)
                else:
                    mark(v.tensor_copy(ds_out[:, 1, :], dts[:, 4, 1, :]), s_edgein)
                if b == 0:
                    dve.wait_ge(s_edge, 1)
                    dve.wait_ge(s_xf, 1)
                    mark(TT(x_end.rearrange("p (h n) -> p h n", n=64), x_dt[:, 0, :].rearrange("p (h n) -> p h n", n=64),
                            ds_out[:, 2, :].unsqueeze(2).to_broadcast([P, 16, 64]), ALU.mult), s_xf)
                    dve.wait_ge(s_cbps, 1)
                    mark(TT(cb_mask.rearrange("p b g l -> p (b g) l"), PS[:, 2, :].rearrange("p (c l) -> p c l", c=4),
                            prefix_ones[:].unsqueeze(1).to_broadcast([P, 4, P]), ALU.mult), s_cb)
                dve.wait_ge(s_dec, b + 1)
                dve.wait_ge(s_cb, 1)
                d4 = decay[:, b].rearrange("p (g h) l -> p g h l", g=2)
                mark(TT(d4, d4, cb_mask[:, b].unsqueeze(2).to_broadcast([P, 2, 8, P]), ALU.mult), s_sc)
            copied(dve, "z")
            skip = bc16[:, 2, :].unsqueeze(2).to_broadcast([P, 16, 64])
            for b in range(NB):
                z = nat[:, b, 1024:2048]
                step(TT(y_skip.rearrange("p (h n) -> p h n", n=64), xs_nat[:, b, :].rearrange("p (h n) -> p h n", n=64),
                        skip, ALU.mult))
                dve.wait_ge(s_yd, b + 1)
                bank = 6 if b == 0 else 0
                step(TT(y_skip, y_skip, PS[:, bank:bank + 2, :].rearrange("p c n -> p (c n)"), ALU.add))
                if b == 1:
                    dve.wait_ge(s_yo, 1)
                    dve.wait_ge(s_edge, 2)
                    step(TT(y_tmp.rearrange("p (h n) -> p h n", n=64), PS[:, 2:4, :].rearrange("p c (h n) -> p (c h) n", n=64),
                            ds_out[:, 3, :].unsqueeze(2).to_broadcast([P, 16, 64]), ALU.mult))
                    step(TT(y_skip, y_skip, y_tmp, ALU.add))
                step(TT(z, z, y_skip, ALU.mult), s_y)
            dve.wait_ge(s_root, ROOTS[1])
            step(v.reciprocal(rinv[:, 6:12], root[:, 6:12]))
            for b in range(NB):
                mark(TT(mix_scale[:, b], ident[:].unsqueeze(1).to_broadcast([P, 3, P]),
                        rinv[:, 6 + 3 * b:9 + 3 * b].unsqueeze(2).to_broadcast([P, 3, P]), ALU.mult), s_nat)
            take_T(1, cols_a[:, A_MIX:A_MIX + 16])

            def add_plain(name, s):
                for c in range(4):
                    g = FIRST[name] + c
                    weigh(g)
                    for b in range(NB):
                        dve.wait_ge(bank_done, done(g, b))
                        x = xres[:, b, c * 512:(c + 1) * 512]
                        TT(x, x, PS[:, 2 * (g % 2) + b, :], ALU.add).then_inc(bank_free[2 * (g % 2) + b], 1)
                copied(dve, name)
                mark(v.memset(junk[:, 1:2], 0.0), s)

            add_plain("mix", s_res)
            sum_quarters(2)
            norm_rows(2)
            take_T(2, None)

            mod_ready(0)

            def route(H, e):
                ds2 = bass.ds(H * 2, 2)
                route_step(v.tensor_copy(sc_now, scores[:, ds2, :]))
                for c in range(2):
                    sc = sc_now[:, c, :]
                    route_step(v.max(top_s[:, c, 0:8], sc))
                    route_step(v.max_index(top_u[:, c, 0:8], top_s[:, c, 0:8], sc))
                    route_step(v.match_replace(sc, top_s[:, c, 0:8], sc, TAKEN))
                    route_step(v.max(top_s[:, c, 8:16], sc))
                    route_step(v.max_index(top_u[:, c, 8:16], top_s[:, c, 8:16], sc))
                route_step(v.tensor_copy(top_f, top_u))
                route_step(TT(cand.rearrange("p (i j) -> p i j", i=16), top_s[:, 0, :].unsqueeze(2).to_broadcast([P, 16, 16]),
                              top_s[:, 1, :].unsqueeze(1).to_broadcast([P, 16, 16]), ALU.add))
                route_step(v.max(best[:, 0:8], cand))
                route_step(v.max_index(pos_u[:, 0:8], best[:, 0:8], cand))
                route_step(v.match_replace(cand, best[:, 0:8], cand, TAKEN))
                route_step(v.max(best[:, 8:16], cand))
                route_step(v.max_index(pos_u[:, 8:16], best[:, 8:16], cand))
                route_step(TS(pos_12[:, 0], pos_u, 4, None, ALU.logical_shift_right))
                route_step(TS(pos_12[:, 1], pos_u, 15, None, ALU.bitwise_and))
                route_step(v.tensor_copy(pos_12f, pos_12))
                for c in range(2):
                    route_step(TT(hot, pos_12f[:, c].unsqueeze(2).to_broadcast([P, 16, 16]),
                                  iota_f[:].unsqueeze(1).to_broadcast([P, 16, 16]), ALU.is_equal))
                    route_step(TT(hot, hot, top_f[:, c, :].unsqueeze(1).to_broadcast([P, 16, 16]), ALU.mult))
                    route_step(v.tensor_reduce(half_id[:, c], hot, AX, ALU.add))
                if not isinstance(H, int) or H > 0:
                    dve.wait_ge(s_now, H)
                STT(out=expert_next[:], in0=half_id[:, 0], scalar=float(NK), in1=half_id[:, 1],
                    op0=ALU.mult, op1=ALU.add).then_inc(s_route, 1)
                TS(gates[:, e, :], best, best[:, 0:1], None, ALU.subtract).then_inc(s_gin, 1)

            step(v.tensor_copy(pos_f[:], pos_i[:]))
            step(TT(ang[:, 0], pos_f[:].unsqueeze(2).to_broadcast([P, 2, 16]),
                    inv_freq[:].unsqueeze(1).to_broadcast([P, 2, 16]), ALU.mult))
            step(TS(ang[:, 1], ang[:, 0], float(1 / (2 * np.pi)), None, ALU.mult))
            step(v.tensor_copy(ang_i[:], ang[:, 1]))
            step(v.tensor_copy(ang[:, 1], ang_i[:]))
            step(STT(out=ang[:, 0], in0=ang[:, 1], scalar=-TWO_PI_HI, in1=ang[:, 0], op0=ALU.mult, op1=ALU.add))
            step(STT(out=ang[:, 0], in0=ang[:, 1], scalar=-TWO_PI_LO, in1=ang[:, 0], op0=ALU.mult, op1=ALU.add))
            for bound, op, turn_by in ((PI, ALU.is_gt, -2 * np.pi), (-PI, ALU.is_lt, 2 * np.pi)):
                step(TS(ang[:, 1], ang[:, 0], bound, float(turn_by), op, ALU.mult))
                step(TT(ang[:, 0], ang[:, 0], ang[:, 1], ALU.add))
            step(TS(ang[:, 2], ang[:, 0], PI, -PI, ALU.min, ALU.max))
            step(STT(out=ang[:, 3], in0=ang[:, 2], scalar=-1.0, in1=ang[:, 2], op0=ALU.mult, op1=ALU.max), s_angle)

            in_route = [0, None]

            def route_step(ins):
                in_route[0] += 1
                ins.then_inc(s_rstep, 1)
                dve.wait_ge(s_rstep, in_route[1] * ROUTE_STEPS + in_route[0])
                if in_route[0] in BEFORE_MAX:
                    dve.sem_inc(s_rcarry, 1)

            def route_head(H, e):
                in_route[:] = [0, H]
                if not isinstance(H, int):
                    dve.wait_ge(s_psc, 5)
                route(H, e)
                assert in_route[0] == ROUTE_STEPS

            dve.wait_ge(s_psc, 1)
            route_head(0, 0)

            def head(H, b, e, more):
                for k in range(16):
                    dve.wait_ge(landed[k % 8], H * 64 + 16 * (1 + k // 8))
                    row = gather_buf[k % 8]
                    v.tensor_tensor_reduce(out=row, in0=row, in1=nat[:, b, :], scale=1.0, scalar=0.0,
                                           op0=ALU.mult, op1=ALU.add, accum_out=dots[:, e, k:k + 1]
                                           ).then_inc(s_down, 1)
                dve.wait_ge(s_gex, H + 1)
                v.tensor_reduce(gsum[:, 0:1], gates[:, e, :], AX, ALU.add).then_inc(s_gnorm, 1)
                dve.wait_ge(s_gnorm, H * 3 + 1)
                v.reciprocal(gsum[:, 1:2], gsum[:, 0:1]).then_inc(s_gnorm, 1)
                dve.wait_ge(s_gnorm, H * 3 + 2)
                TS(gates[:, e, :], gates[:, e, :], gsum[:, 1:2], None, ALU.mult).then_inc(s_gnorm, 1)
                dve.wait_ge(s_gnorm, H * 3 + 3)
                dve.wait_ge(s_gelu, H + 1)
                TT(weight[:, e, :], gelu[:, e, :], gates[:, e, :], ALU.mult).then_inc(s_wt, 1)
                if more:
                    route_head(H + 1, 1 - e)

            mc = mod_cols[:].rearrange("p (l c) -> p l c", l=2)

            def pool_scale(b):
                dve.wait_ge(s_root, ROOTS[3] - 1 + b)
                step(v.reciprocal(rinv[:, b:b + 1], root[:, b:b + 1]))
                mark(TS(row_scale[:, b, :], ident[:], rinv[:, b:b + 1], None, ALU.mult), s_nat)

            for b in range(NB):
                with dve.Fori(0, PH // 2 - b) as j:
                    for e in range(2):
                        head(j * 2 + (PH * b + e), b, e, True)
            pool_scale(0)
            head(NB * PH - 2, 1, 0, True)
            take_T(3, mod_gain[:, 0, :], mc[:, 0, 0:16], [0])
            head(NB * PH - 1, 1, 1, False)
            H, tail = NB * PH - 1, big[:, 4096:4608]
            dve.wait_ge(s_wt, H + 1)
            for k in range(8, TOPK):
                dve.wait_ge(landed[k % 8], H * 64 + 16 * (3 + k // 8))
                row, w = gather_buf[k % 8][:, 1536:2048], weight[:, 1, k:k + 1]
                if k == 8:
                    step(TS(tail, row, w, None, ALU.mult), s_tail)
                else:
                    step(STT(out=tail, in0=row, scalar=w, in1=tail, op0=ALU.mult, op1=ALU.add), s_tail)
            dve.wait_ge(s_up, 8 + UPS * NB)
            mark(TT(xres[:, 1, 1536:2048], PS[:, 7, :], tail, ALU.add), s_tailed)
            pool_scale(1)
            take_T(3, mod_gain[:, 0, :], mc[:, 0, 0:16], [1])
            dve.wait_ge(s_cnt, 4)
            step(v.tensor_copy(counts, counts.bitcast(I32)))
            for w, width in enumerate(WINDOWS):
                step(TS(counts[:, w, :], counts[:, w, :], float(width), None, ALU.min))
            step(v.reciprocal(counts, counts))
            for gi, width in enumerate(WINDOWS):
                g = FIRST["pv"] + gi
                weigh(g)
                for u in range(2):
                    dve.wait_ge(bank_free[2 * (g % 2) + u], g // 2 + 1)
                cur = poolT[:, 4 * gi:4 * gi + 4, :]
                own, by, i = cur, 1, 0
                while by < width:
                    nxt = sums[i % 2]
                    step(v.tensor_copy(nxt[:, :, 0:by], cur[:, :, 0:by]))
                    step(TT(nxt[:, :, by:], cur[:, :, by:], cur[:, :, 0:T - by], ALU.add))
                    cur, by, i = nxt, 2 * by, i + 1
                step(TT(cur, cur, counts[:, gi, :].unsqueeze(1).to_broadcast([P, 4, T]), ALU.mult))
                step(TT(own, cur, own, ALU.subtract), s_pool_T)
            for c in range(4):
                weigh(FIRST["pg"] + c)
            for i in range(4):
                g = FIRST["grp"] + i
                for u in range(2):
                    dve.wait_ge(bank_done, done(g, u))
                    if i == 0 and u == 0:
                        copied(dve, "pg")
                    for o in range(2):
                        c = 4 * i + 2 * u + o
                        ins = STT(out=pgateT[:, c, :], in0=PS[:, 2 * (g % 2) + u, o * T:(o + 1) * T],
                                  scalar=cols_b[:, B_SCALE + c:B_SCALE + c + 1], in1=pgateT[:, c, :],
                                  op0=ALU.mult, op1=ALU.mult)
                        if o:
                            ins.then_inc(bank_free[2 * (g % 2) + u], 1)
                        else:
                            mark(ins, s_dve)

            def add_gated(name, layer):
                for c in range(4):
                    g = FIRST[name] + c
                    weigh(g)
                    if c == 0:
                        dve.wait_ge(s_wide, 32 + 16 * layer)
                    for b in range(NB):
                        dve.wait_ge(bank_done, done(g, b))
                        bank = PS[:, 2 * (g % 2) + b, :]
                        cs = slice(c * 512, (c + 1) * 512)
                        TT(stage[:, b, :], bank, wide[:, cs], ALU.mult).then_inc(bank_free[2 * (g % 2) + b], 1)
                        dve.wait_ge(bank_free[2 * (g % 2) + b], g // 2 + 1)
                        step(TT(xres[:, b, cs], xres[:, b, cs], stage[:, b, :], ALU.add), s_res)

            add_gated("po", 0)
            sum_quarters(4)
            mod_ready(1)
            norm_rows(4)
            take_T(4, mod_gain[:, 1, :], mc[:, 1, 0:16])

            def rotate(x, heads, half, cs, sn, last_sem):
                x1, x2 = x[:, :, 0:half], x[:, :, half:2 * half]
                cs, sn = [t.unsqueeze(1).to_broadcast([P, heads, half]) for t in (cs, sn)]
                t = [rope_t[:, i, 0:heads * half].rearrange("p (h n) -> p h n", h=heads) for i in range(4)]
                mark(TT(t[0], x1, cs, ALU.mult), s_dve)
                mark(TT(t[1], x2, sn, ALU.mult), s_dve)
                mark(TT(t[2], x2, cs, ALU.mult), s_dve)
                step(TT(t[3], x1, sn, ALU.mult))
                step(TT(x1, t[0], t[1], ALU.subtract))
                step(TT(x2, t[2], t[3], ALU.add), last_sem)

            dve.wait_ge(s_trig, 2)
            for i in range(20):
                g = FIRST["aq"] + i // 2
                b = i % 2
                dve.wait_ge(bank_free[2 * (g % 2) + b], g // 2 + 1)
                if i < 16:
                    rotate(stage[:, b, :].rearrange("p (h n) -> p h n", h=4), 4, 16, cosine[:, b, :], sine[:, b, :], s_rope)
                else:
                    rotate(stage[:, b, :].rearrange("p (h n) -> p h n", h=8), 8, 8,
                           cosine[:, b, 0:16:2], sine[:, b, 0:16:2], s_rope)
            dve.wait_ge(s_kist, 2)
            for b in range(NB):
                rotate(ki_wi[:, b:b + 1, 0:64], 1, 8, cosine[:, b, 0:16:2], sine[:, b, 0:16:2], s_dve)
            step(v.tensor_copy(ki_wi[:, :, 64:128], ki_wi[:, :, 0:64]), s_kirope)
            for i in range(2 * IH):
                b, h = i // IH, i % IH
                S = P * (b + 1)
                dve.wait_ge(s_relu, i + 1)
                w = ki_wi[:, b, 128 + h:129 + h]
                if h == 0:
                    ins = TS(iscore[:, b, 0:S], relu[:, i % 2, 0:S], w, None, ALU.mult)
                else:
                    ins = STT(out=iscore[:, b, 0:S], in0=relu[:, i % 2, 0:S], scalar=w, in1=iscore[:, b, 0:S],
                              op0=ALU.mult, op1=ALU.add)
                step(ins, s_iuse)
                if h == IH - 1:
                    mark(v.memset(junk[:, 3:4], 0.0), s_iacc)
            for b in range(NB):
                S = P * (b + 1)
                dve.wait_ge(s_iadm, b + 1)
                src = iscore[:, b, 0:S]
                for r in range(SELECT // 8):
                    step(v.max(best8[:], src))
                    step(v.match_replace(iwork[:, 0:S], best8[:], src, TAKEN))
                    src = iwork[:, 0:S]
                o = sel_bias[:, 0:P] if b == 0 else sel_bias[:, P:]
                step(TT(o, iwork[:, 0:S], iscore[:, b, 0:S], ALU.is_equal))
                mark(TS(o, o, MASKED, None, ALU.mult), s_sel)
            dve.wait_ge(s_causal, 2)

            def masked(h):
                e = h % 2
                dve.wait_ge(s_lps, h + 1)
                if h >= 2:
                    dve.wait_ge(s_pe, 2 * (h - 1))
                for b in range(NB):
                    s = slice(0, P) if b == 0 else slice(P, 384)
                    step(v.tensor_tensor_reduce(out=lm[:, e, s], in0=PS[:, 4 + e, s], in1=sel_bias[:, s],
                                                scale=float(P ** -0.5), scalar=-3.0e38, op0=ALU.add, op1=ALU.max,
                                                accum_out=smax[:, e, b:b + 1]))
                    mark(TS(smax[:, e, b:b + 1], smax[:, e, b:b + 1], -1.0, None, ALU.mult), s_lm)

            def normed(h):
                e = h % 2
                dve.wait_ge(s_pe, 2 * h + 2)
                step(v.reciprocal(ssum[:, e, 2:4], ssum[:, e, 0:2]))
                step(TS(pr[:, e, 0:P], pr[:, e, 0:P], ssum[:, e, 2:3], None, ALU.mult))
                mark(TS(pr[:, e, P:384], pr[:, e, P:384], ssum[:, e, 3:4], None, ALU.mult), s_pn)

            def gated(h):
                dve.wait_ge(s_ops, h + 1)
                mark(TT(agateT[:, h, :], PS[:, h % 2, 0:T], agateT[:, h, :], ALU.mult), s_oT)

            copied(dve, "ag")
            for h in range(NH + 3):
                if h < NH:
                    masked(h)
                if 1 <= h <= NH:
                    normed(h - 1)
                if h >= 3:
                    gated(h - 3)
            add_gated("ao", 1)
            sum_quarters(5)
            dve.wait_ge(s_fin, 16)
            dve.wait_ge(s_root, ROOTS[5])
            step(v.reciprocal(rinv[:, 0:2], root[:, 0:2]))
            for b in range(NB):
                step(STT(out=nat[:, b, :], in0=xres[:, b, :], scalar=rinv[:, b:b + 1], in1=final_gain,
                         op0=ALU.mult, op1=ALU.mult), s_y)


_OUT = ("out_0_dram", (1, T, D))


def kernel(**inputs):
    import numpy as _np
    import concourse.bacc as _bacc
    from concourse import mybir as _mybir
    from concourse.bass_utils import run_bass_kernel_spmd as _run

    nc = _bacc.Bacc("TRN2", target_bir_lowering=False, num_devices=1)
    arrays, args = {}, {}
    for name, value in inputs.items():
        value = _np.ascontiguousarray(value)
        if value.ndim == 1:
            value = value.reshape(1, -1)
        arrays[f"in_{name}_dram"] = value
        args[name] = nc.dram_tensor(f"in_{name}_dram", value.shape, _mybir.dt.from_np(value.dtype),
                                    kind="ExternalInput").ap()
    out = nc.dram_tensor(_OUT[0], _OUT[1], _mybir.dt.float32, kind="ExternalOutput").ap()
    gate_dram = nc.dram_tensor("gate_rows", (2, D), _mybir.dt.float32, kind="Internal").ap()
    program(nc, args, out, gate_dram)
    r = _run(nc, [arrays], core_ids=[0])
    return r.results[0][_OUT[0]]
```
